# Optimizing a Trainium2 kernel written in Bass

```python
import math
import jax, jax.numpy as jnp
from jax import lax
import numpy as np

D_MODEL = 1024
BATCH = 1
SEQ = 2048
DEPTH = 1

CHUNK = 64
Q_BLOCK = 128
HEAD_DIM = 64
DIFF_HEADS = 4
DIFF_V_DIM = 2 * HEAD_DIM
DIFF_WIDTH = DIFF_HEADS * DIFF_V_DIM
FOX_HEADS = 8
FOX_WIDTH = FOX_HEADS * HEAD_DIM
MIX_WIDTH = DIFF_WIDTH + FOX_WIDTH
DIFF_QK_WIDTH = DIFF_HEADS * 2 * HEAD_DIM
IN_COLS = 2 * DIFF_QK_WIDTH + DIFF_WIDTH + 3 * FOX_WIDTH + FOX_HEADS
ROPE_THETA = 10000.0
N_GROUPS = 4
EXPERTS_PER_GROUP = 8
N_EXPERTS = N_GROUPS * EXPERTS_PER_GROUP
TOP_K_IN_GROUP = 2
D_EXPERT = D_MODEL // 2
MOE_BLOCK = 128
EPS = 1e-6
NEG_INF = -1e30

kernel_name = "hybrid_diff_fox_hmoe_block"

def rms_norm(x, g):
    xf = x.astype(jnp.float32)
    y = xf * lax.rsqrt(jnp.mean(xf * xf, axis=-1, keepdims=True) + EPS)
    return (y * g.astype(jnp.float32)).astype(x.dtype)

def rope_tables(seq_len, dtype):
    inv = 1.0 / (ROPE_THETA ** (jnp.arange(0, HEAD_DIM, 2, dtype=jnp.float32) / HEAD_DIM))
    ang = jnp.arange(seq_len, dtype=jnp.float32)[:, None] * inv[None, :]
    return jnp.cos(ang).astype(dtype), jnp.sin(ang).astype(dtype)

def apply_rope(x, cos, sin):
    x1, x2 = jnp.split(x, 2, axis=-1)
    c = cos[None, :, None, :]
    s = sin[None, :, None, :]
    return jnp.concatenate([x1 * c - x2 * s, x2 * c + x1 * s], axis=-1)

def diff_attention(q, k, v, lam, subln_g, lambda_init):
    B, S = q.shape[0], q.shape[1]
    scale = HEAD_DIM ** -0.5
    pos = jnp.arange(S)
    outs = []
    for i in range(S // Q_BLOCK):
        q0, q1 = i * Q_BLOCK, (i + 1) * Q_BLOCK
        s = jnp.einsum('bqhmd,bkhmd->bhmqk', q[:, q0:q1], k[:, :q1]).astype(jnp.float32) * scale
        mask = (pos[None, :q1] // CHUNK) <= (pos[q0:q1, None] // CHUNK)
        p = jax.nn.softmax(jnp.where(mask, s, NEG_INF), axis=-1)
        a = p[:, :, 0] - lam * p[:, :, 1]
        outs.append(jnp.einsum('bhqk,bkhe->bqhe', a.astype(v.dtype), v[:, :q1]))
    o = jnp.concatenate(outs, axis=1)
    return rms_norm(o, subln_g) * (1.0 - lambda_init)

def forgetting_attention(q, k, v, log_f):
    S = q.shape[1]
    scale = HEAD_DIM ** -0.5
    F = jnp.cumsum(log_f, axis=1).transpose(0, 2, 1)
    pos = jnp.arange(S)
    outs = []
    for i in range(S // Q_BLOCK):
        q0, q1 = i * Q_BLOCK, (i + 1) * Q_BLOCK
        s = jnp.einsum('bqhd,bkhd->bhqk', q[:, q0:q1], k[:, :q1]).astype(jnp.float32) * scale
        s = s + F[:, :, q0:q1, None] - F[:, :, None, :q1]
        mask = pos[None, :q1] <= pos[q0:q1, None]
        p = jax.nn.softmax(jnp.where(mask, s, NEG_INF), axis=-1)
        outs.append(jnp.einsum('bhqk,bkhd->bqhd', p.astype(v.dtype), v[:, :q1]))
    return jnp.concatenate(outs, axis=1)

def hierarchical_moe(h, w_group, b_group, w_router, b_router, w_gate, w_up, w_down):
    B, S, D = h.shape
    T = B * S
    xt = h.reshape(T, D)
    g_logits = (xt @ w_group).astype(jnp.float32) + b_group.astype(jnp.float32)
    g_prob = jax.nn.softmax(g_logits, axis=-1)
    g_idx = jnp.argmax(g_logits, axis=-1)
    g_w = jnp.take_along_axis(g_prob, g_idx[:, None], axis=1)[:, 0]
    e_logits = ((xt @ w_router).astype(jnp.float32) + b_router.astype(jnp.float32))
    e_logits = e_logits.reshape(T, N_GROUPS, EXPERTS_PER_GROUP)
    e_sel = jnp.take_along_axis(e_logits, g_idx[:, None, None], axis=1)[:, 0]
    top_v, top_i = lax.top_k(e_sel, TOP_K_IN_GROUP)
    weights = g_w[:, None] * jax.nn.softmax(top_v, axis=-1)
    expert_ids = g_idx[:, None] * EXPERTS_PER_GROUP + top_i
    M = T * TOP_K_IN_GROUP
    flat_e = expert_ids.reshape(M)
    flat_w = weights.reshape(M)
    flat_tok = jnp.arange(M) // TOP_K_IN_GROUP
    order = jnp.argsort(flat_e)
    e_sorted, tok_sorted, w_sorted = flat_e[order], flat_tok[order], flat_w[order]
    counts = jnp.bincount(flat_e, length=N_EXPERTS)
    start = jnp.cumsum(counts) - counts
    padded = ((counts + MOE_BLOCK - 1) // MOE_BLOCK) * MOE_BLOCK
    pend = jnp.cumsum(padded)
    pstart = pend - padded
    dest = pstart[e_sorted] + (jnp.arange(M) - start[e_sorted])
    n_blocks = -(-M // MOE_BLOCK) + N_EXPERTS
    P = n_blocks * MOE_BLOCK
    buf = jnp.zeros((P, D), h.dtype).at[dest].set(xt[tok_sorted])
    block_e = jnp.minimum(jnp.searchsorted(pend, jnp.arange(n_blocks) * MOE_BLOCK, side='right'),
                          N_EXPERTS - 1)

    def expert_block(args):
        xb, e = args
        a = xb @ w_gate[e]
        u = xb @ w_up[e]
        return (jax.nn.silu(a) * u) @ w_down[e]

    out = lax.map(expert_block, (buf.reshape(n_blocks, MOE_BLOCK, D), block_e))
    y_sorted = out.reshape(P, D)[dest] * w_sorted[:, None].astype(h.dtype)
    y = jax.ops.segment_sum(y_sorted, tok_sorted, num_segments=T)
    return y.reshape(B, S, D)

def setup_inputs(seed: int = 0) -> dict:
    key = jax.random.key(seed)
    ks = jax.random.split(key, 24)
    f32 = jnp.float32
    L, D, E, Fd = DEPTH, D_MODEL, N_EXPERTS, D_EXPERT
    nrm = lambda k, shape, s: jax.random.normal(k, shape, f32) * s
    gain = lambda k, shape: 1.0 + 0.01 * jax.random.normal(k, shape, f32)
    return {
        "x": jax.random.normal(ks[0], (BATCH, SEQ, D), f32),
        "c": jax.random.normal(ks[1], (BATCH, D), f32),
        "w_ada": nrm(ks[2], (L, D, 6 * D), 0.5 * D ** -0.5),
        "b_ada": nrm(ks[3], (L, 6 * D), 0.01),
        "g_pre_attn": gain(ks[4], (L, D)),
        "g_post_attn": gain(ks[5], (L, D)),
        "w_in": nrm(ks[6], (L, D, IN_COLS), D ** -0.5),
        "b_forget": 3.0 + 2.0 * jax.random.uniform(ks[7], (L, FOX_HEADS), f32),
        "lambda_q1": nrm(ks[8], (L, HEAD_DIM), 0.1),
        "lambda_k1": nrm(ks[9], (L, HEAD_DIM), 0.1),
        "lambda_q2": nrm(ks[10], (L, HEAD_DIM), 0.1),
        "lambda_k2": nrm(ks[11], (L, HEAD_DIM), 0.1),
        "g_diff_subln": gain(ks[12], (L, DIFF_V_DIM)),
        "w_out": nrm(ks[13], (L, MIX_WIDTH, D), MIX_WIDTH ** -0.5),
        "g_pre_ffn": gain(ks[14], (L, D)),
        "g_post_ffn": gain(ks[15], (L, D)),
        "w_group": nrm(ks[16], (L, D, N_GROUPS), D ** -0.5),
        "b_group": nrm(ks[17], (L, N_GROUPS), 0.01),
        "w_router": nrm(ks[18], (L, D, E), D ** -0.5),
        "b_router": nrm(ks[19], (L, E), 0.01),
        "w_gate": nrm(ks[20], (L, E, D, Fd), D ** -0.5),
        "w_up": nrm(ks[21], (L, E, D, Fd), D ** -0.5),
        "w_down": nrm(ks[22], (L, E, Fd, D), Fd ** -0.5),
    }

def reference(x, c, w_ada, b_ada, g_pre_attn, g_post_attn, w_in, b_forget,
              lambda_q1, lambda_k1, lambda_q2, lambda_k2, g_diff_subln, w_out,
              g_pre_ffn, g_post_ffn, w_group, b_group, w_router, b_router,
              w_gate, w_up, w_down):
    B, S, D = x.shape
    cos, sin = rope_tables(S, x.dtype)
    split_at = np.cumsum([DIFF_QK_WIDTH, DIFF_QK_WIDTH, DIFF_WIDTH,
                          FOX_WIDTH, FOX_WIDTH, FOX_WIDTH]).tolist()
    for l in range(DEPTH):
        lambda_init = 0.8 - 0.6 * math.exp(-0.3 * l)
        mod = (jax.nn.silu(c) @ w_ada[l] + b_ada[l])[:, None, :]
        sh_a, sc_a, gt_a, sh_f, sc_f, gt_f = jnp.split(mod, 6, axis=-1)

        h = rms_norm(x, g_pre_attn[l]) * (1.0 + sc_a) + sh_a
        proj = h @ w_in[l]
        dq, dk, dv, fq, fk, fv, f_logit = jnp.split(proj, split_at, axis=-1)

        dq = apply_rope(dq.reshape(B, S, 2 * DIFF_HEADS, HEAD_DIM), cos, sin)
        dk = apply_rope(dk.reshape(B, S, 2 * DIFF_HEADS, HEAD_DIM), cos, sin)
        dq = dq.reshape(B, S, DIFF_HEADS, 2, HEAD_DIM)
        dk = dk.reshape(B, S, DIFF_HEADS, 2, HEAD_DIM)
        dv = dv.reshape(B, S, DIFF_HEADS, DIFF_V_DIM)
        lam = (jnp.exp(jnp.sum(lambda_q1[l].astype(jnp.float32) * lambda_k1[l].astype(jnp.float32)))
               - jnp.exp(jnp.sum(lambda_q2[l].astype(jnp.float32) * lambda_k2[l].astype(jnp.float32)))
               + lambda_init)
        diff_out = diff_attention(dq, dk, dv, lam, g_diff_subln[l], lambda_init)

        log_f = jax.nn.log_sigmoid((f_logit + b_forget[l]).astype(jnp.float32))
        fox_out = forgetting_attention(fq.reshape(B, S, FOX_HEADS, HEAD_DIM),
                                       fk.reshape(B, S, FOX_HEADS, HEAD_DIM),
                                       fv.reshape(B, S, FOX_HEADS, HEAD_DIM), log_f)

        mixed = jnp.concatenate([diff_out.reshape(B, S, DIFF_WIDTH),
                                 fox_out.reshape(B, S, FOX_WIDTH)], axis=-1) @ w_out[l]
        x = x + gt_a * rms_norm(mixed, g_post_attn[l])

        h = rms_norm(x, g_pre_ffn[l]) * (1.0 + sc_f) + sh_f
        y = hierarchical_moe(h, w_group[l], b_group[l], w_router[l], b_router[l],
                             w_gate[l], w_up[l], w_down[l])
        x = x + gt_f * rms_norm(y, g_post_ffn[l])
    return x


_drawn_inputs = setup_inputs


def setup_inputs(seed=0):
    import zlib

    import numpy as np

    out = dict(_drawn_inputs(seed))
    spreads = {}
    factors = {'g_pre_attn': 3.212,
     'g_post_attn': 2.843,
     'lambda_k1': 6.511,
     'lambda_q2': 7.612,
     'g_diff_subln': 4.34,
     'g_post_ffn': 8.0,
     'b_router': 2.719}
    for name, (base, spread) in spreads.items():
        noise = np.random.default_rng([zlib.crc32(name.encode()), seed]).standard_normal(out[name].shape)
        drawn = base * np.exp(spread * noise) if base else spread * noise
        out[name] = __import__('jax').numpy.asarray(drawn.astype(out[name].dtype))
    for name, factor in factors.items():
        out[name] = (out[name] * factor).astype(out[name].dtype)
    return out
```

```python
from contextlib import ExitStack

import concourse.bass as bass
from concourse import mybir

P = 128
D = 1024
KT = D // P
S = 2048
TB = S // P
HD = 64
UNITS = 4
GROUPS = 4
PER_GROUP = 8
EXPERTS = GROUPS * PER_GROUP
LOGITS = GROUPS + EXPERTS
F = D // 2
FT = F // P
BANK = 512
CH = S // BANK
TPB = BANK // P
MAX_BLOCKS = 2 * S // P + EXPERTS
TABLE = MAX_BLOCKS + 2
EPS = 1e-6
LAMBDA_INIT = 0.2
QK_SCALE = HD ** -0.5
BIG = 3.0e38
MASKED = 1.0e30
COL = {"diff": (0, 512, 1024), "fox": (1536, 2048, 2560), "forget": 3072}
FOX_HEADS = 8
C_IDENT, C_ROT, C_BEFORE, C_MASKD, C_MASKF, C_IOTA, C_GDESC, C_EDESC, C_TOKEN, C_TRASH, C_END = (
    0, 128, 256, 384, 512, 640, 768, 772, 780, 796, 797)

ALU = mybir.AluOpType
ACT = mybir.ActivationFunctionType
F32 = mybir.dt.float32
BF16 = mybir.dt.bfloat16
I32 = mybir.dt.int32
U32 = mybir.dt.uint32
X = mybir.AxisListType.X


W_GATE, W_UP, W_DOWN, EXPERT_WORDS = 0, KT * F, 2 * KT * F, 2 * KT * F + FT * D


class Steps:

    def __init__(self, eng, sem):
        self.eng, self.sem, self.n, self.base = eng, sem, 0, 0

    def link(self, ins):
        ins.then_inc(self.sem, 1)
        self.n += 1
        self.eng.wait_ge(self.sem, self.base + self.n)


class Names:

    def __init__(self, nc, ctx, prefix=""):
        self.nc, self.ctx, self.prefix = nc, ctx, prefix

    def sb(self, name, shape, dt=F32):
        return self.ctx.enter_context(self.nc.sbuf_tensor(self.prefix + name, shape, dt))

    def ps(self, name, shape, dt=F32):
        return self.ctx.enter_context(self.nc.psum_tensor(self.prefix + name, shape, dt))

    def sem(self, name):
        return self.ctx.enter_context(self.nc.semaphore(self.prefix + name))


def modulate(nc, a, t):
    with ExitStack() as ctx:
        p = Names(nc, ctx, "mod_")
        NP = 6 * D // BANK
        RING = 2
        w_ada = [p.sb(f"w_ada{i}", [P, KT, BANK]) for i in range(RING)]
        b_ada = [p.sb(f"b_ada{i}", [P, BANK]) for i in range(RING)]
        xs = p.sb("xs", [P, TB, D])
        ccol = p.sb("ccol", [P, KT])
        cact = p.sb("cact", [P, KT])
        cwide = p.sb("cwide", [P, KT, P])
        gcol = p.sb("gcol", [P, KT])
        tmprow = p.sb("tmprow", [P, D])
        summed = p.sb("summed", [P, 2, BANK])
        ssq = p.sb("ssq", [P, TB])
        std = p.sb("std", [P, TB])
        rstd = p.sb("rstd", [P, TB])
        lamrow = p.sb("lamrow", [1, 4, HD])
        lamprod = p.sb("lamprod", [1, 2, HD])
        lamsum = p.sb("lamsum", [1, 2])
        lamexp = p.sb("lamexp", [1, 2])
        lamone = p.sb("lamone", [1, 1])
        onerow = p.sb("onerow", [1, P])
        junk = p.sb("junk", [P, D])
        modp = [p.ps(f"modp{i}", [P, BANK]) for i in range(2)]
        colp = p.ps("colp", [P, 2, P])
        lamp = p.ps("lamp", [P, 1])
        xtp = [p.ps(f"xtp{i}", [P, BANK]) for i in range(4)]
        s_small = p.sem("small_loaded")
        s_w = [p.sem(f"w_ada_loaded{i}") for i in range(RING)]
        s_x = [p.sem(f"x_loaded{i}") for i in range(4)]
        s_cact = p.sem("c_activated")
        s_cwide = p.sem("c_widened")
        s_mod = p.sem("mod_product")
        s_sum = p.sem("mod_summed")
        s_modrow = p.sem("mod_row_done")
        s_tr = p.sem("mod_transposed")
        s_col = p.sem("mod_column_done")
        s_sq = p.sem("x_squared")
        s_std = p.sem("std_done")
        s_xn = p.sem("x_normalised")
        s_xt = p.sem("x_transposed")
        s_hta = p.sem("hT_by_act")
        s_htv = p.sem("hT_by_dve")
        s_lam = p.sem("lambda_steps")
        s_lamexp = p.sem("lambda_exponentials")
        s_lamb = p.sem("lambda_broadcast")
        s_const = p.sem("constants_made")
        s_dve = p.sem("dve_steps")
        mod_of = {0: "sh_a", 1: "sc_a", 2: "gt_a", 3: "sh_f", 4: "sc_f", 5: "gt_f"}
        rows = {"sh_a": tmprow, "sc_a": tmprow, "gt_a": t.gate_attn, "sh_f": t.ffn_shift,
                "sc_f": t.ffn_gain, "gt_f": t.gate_ffn}
        NSMALL = 12

        with nc.Block() as block:

            @block.sync
            def _(sp):
                sp.dma_start(t.consts[:, :], a["consts"]).then_inc(s_small, 16)
                sp.dma_start(ccol[:, :], a["c"].rearrange("a (k p) -> p (a k)", p=P),
                             allow_slow_non_contiguous=True).then_inc(s_small, 16)
                sp.dma_start(gcol[:, :], a["g_pre_attn"].rearrange("a (k p) -> p (a k)", p=P),
                             allow_slow_non_contiguous=True).then_inc(s_small, 16)
                sp.dma_start(t.subln[:, :], a["g_diff_subln"].rearrange("a p -> p a"),
                             allow_slow_non_contiguous=True).then_inc(s_small, 16)
                for dst, name in ((t.gate_attn, "g_post_attn"), (t.ffn_gain, "g_pre_ffn"),
                                  (t.gate_ffn, "g_post_ffn")):
                    sp.dma_start(dst[:, :], a[name].to_broadcast([P, D])).then_inc(s_small, 16)
                for i, name in enumerate(("lambda_q1", "lambda_q2", "lambda_k1", "lambda_k2")):
                    sp.dma_start(lamrow[:, i, :], a[name]).then_inc(s_small, 16)
                sp.dma_start(t.bforget[:, :], a["b_forget"].rearrange("a h -> h a"),
                             allow_slow_non_contiguous=True).then_inc(s_small, 16)
                for n in range(NP):
                    if n >= RING:
                        sp.wait_ge(s_mod, n - RING + 1)
                        sp.wait_ge(s_sum, n - RING + 1)
                    cols = slice(n * BANK, (n + 1) * BANK)
                    sp.dma_start(w_ada[n % RING][:, :, :],
                                 a["w_ada"][0, :, cols].rearrange("(k p) n -> p k n", p=P)).then_inc(s_w[n % RING], 16)
                    sp.dma_start(b_ada[n % RING][:, :],
                                 a["b_ada"][:, cols].to_broadcast([P, BANK])).then_inc(s_w[n % RING], 16)

            @block.scalar
            def _(act):
                for i in range(4):
                    act.dma_start(xs[:, 4 * i:4 * i + 4, :],
                                  a["x"][0].rearrange("(t p) d -> p t d", p=P)[:, 4 * i:4 * i + 4, :]).then_inc(s_x[i], 16)
                act.wait_ge(s_small, 16 * NSMALL)
                act.activation(cact[:, :], ccol[:, :], ACT.Silu).then_inc(s_cact, 1)
                act.wait_ge(s_lam, 2)
                act.activation(lamexp[:, :], lamsum[:, :], ACT.Exp).then_inc(s_lamexp, 1)
                for i in range(TB):
                    if i % 4 == 0:
                        act.wait_ge(s_x[i // 4], 16)
                    if i:
                        act.wait_ge(s_sq, i)
                    act.activation(junk[:, :], xs[:, i, :], ACT.Square, accum_out=ssq[:, i:i + 1]).then_inc(s_sq, 1)
                act.wait_ge(s_sq, TB)
                act.wait_ge(s_const, 1)
                act.activation(std[:, :], ssq[:, :], ACT.Sqrt, scale=1.0 / D, bias=t.eps[:, :]).then_inc(s_std, 1)
                act.wait_ge(s_col, 16)
                for n in range(0, 4 * KT, 2):
                    tg, k = divmod(n, KT)
                    act.wait_ge(s_xt, n + 1)
                    act.activation(t.hT[:, k, tg * BANK:(tg + 1) * BANK], xtp[n % 4][:, :], ACT.Identity,
                                   scale=t.attn_gain[:, k:k + 1], bias=t.attn_shift[:, k:k + 1]).then_inc(s_hta, 1)

            @block.tensor
            def _(pe):
                pe.wait_ge(s_cwide, KT)
                for n in range(NP):
                    pe.wait_ge(s_w[n % RING], 32 * (n // RING + 1))
                    if n >= 2:
                        pe.wait_ge(s_sum, n - 1)
                    for k in range(KT):
                        mm = pe.matmul(modp[n % 2][:, :], cwide[:, k, :], w_ada[n % RING][:, k, :],
                                       start=(k == 0), stop=(k == KT - 1))
                    mm.then_inc(s_mod, 1)
                    if n < 4:
                        pe.wait_ge(s_modrow, n + 1)
                        for j in range(TPB):
                            m = n * TPB + j
                            if m >= 1:
                                pe.wait_ge(s_col, m)
                            pe.transpose(colp[:, 0, :], tmprow[:, (n % 2) * BANK + j * P:(n % 2) * BANK + (j + 1) * P],
                                         t.ident).then_inc(s_tr, 1)
                pe.wait_ge(s_lam, 4)
                pe.matmul(lamp[:, :], onerow[:, :], lamone[:, :], start=True, stop=True).then_inc(s_lamb, 1)
                for n in range(4 * KT):
                    tg, k = divmod(n, KT)
                    if k == 0:
                        pe.wait_ge(s_xn, 4 * tg + 4)
                    if n >= 4:
                        pe.wait_ge(s_hta if n % 2 == 0 else s_htv, (n - 4) // 2 + 1)
                    for j in range(4):
                        mm = pe.transpose(xtp[n % 4][:, j * P:(j + 1) * P], xs[:, 4 * tg + j, k * P:(k + 1) * P], t.ident)
                    mm.then_inc(s_xt, 1)

            @block.vector
            def _(dve):
                st = Steps(dve, s_dve)
                dve.memset(t.eps[:, :], EPS).then_inc(s_const, 1)
                st.link(dve.memset(cwide[:, :, :], 1.0))
                st.link(dve.memset(onerow[:, :], 1.0))
                dve.wait_ge(s_small, 16 * NSMALL)
                st.link(dve.tensor_copy(t.ident_bf[:, :], t.ident))
                st.link(dve.tensor_copy(t.mask["diff"][:, :], t.consts[:, C_MASKD:C_MASKD + P]))
                st.link(dve.tensor_copy(t.mask["fox"][:, :], t.consts[:, C_MASKF:C_MASKF + P]))
                st.link(dve.tensor_copy(t.before_bf[:, :], t.consts[:, C_BEFORE:C_BEFORE + P]))
                st.link(dve.memset(t.ones_bf[:, :], 1.0))
                st.link(dve.tensor_scalar(t.subln[:, :], t.subln[:, :], 1.0 - LAMBDA_INIT, None, ALU.mult))
                st.link(dve.tensor_tensor(lamprod[:, :, :], lamrow[:, 0:2, :], lamrow[:, 2:4, :], ALU.mult))
                dve.memset(lamsum[:, :], 0.0).then_inc(s_lam, 1)
                dve.wait_ge(s_lam, 1)
                dve.tensor_reduce(lamsum[:, :], lamprod[:, :, :], X, ALU.add).then_inc(s_lam, 1)
                dve.wait_ge(s_lamexp, 1)
                dve.tensor_tensor(lamone[:, :], lamexp[:, 1:2], lamexp[:, 0:1], ALU.subtract).then_inc(s_lam, 1)
                dve.wait_ge(s_lam, 3)
                dve.tensor_scalar(lamone[:, :], lamone[:, :], -LAMBDA_INIT, None, ALU.add).then_inc(s_lam, 1)
                dve.wait_ge(s_cact, 1)
                for k in range(KT):
                    dve.tensor_scalar(cwide[:, k, :], cwide[:, k, :], cact[:, k:k + 1], None, ALU.mult).then_inc(s_cwide, 1)
                for n in range(NP):
                    what = mod_of[n // 2]
                    half = slice((n % 2) * BANK, (n % 2 + 1) * BANK)
                    dve.wait_ge(s_mod, n + 1)
                    if n >= 2:
                        dve.wait_ge(s_modrow, n - 1)
                    dve.tensor_tensor(summed[:, n % 2, :], modp[n % 2][:, :], b_ada[n % RING][:, :], ALU.add).then_inc(s_sum, 1)
                    dve.wait_ge(s_sum, n + 1)
                    dst = rows[what][:, half]
                    if what in ("sh_a", "sh_f"):
                        ins = dve.tensor_copy(dst, summed[:, n % 2, :])
                    elif what == "sc_a":
                        ins = dve.tensor_scalar(dst, summed[:, n % 2, :], 1.0, None, ALU.add)
                    elif what == "sc_f":
                        ins = dve.scalar_tensor_tensor(out=dst, in0=summed[:, n % 2, :], scalar=1.0, in1=dst,
                                                       op0=ALU.add, op1=ALU.mult)
                    else:
                        ins = dve.tensor_tensor(dst, summed[:, n % 2, :], dst, ALU.mult)
                    ins.then_inc(s_modrow, 1)
                    if n < 4:
                        for j in range(TPB):
                            m = n * TPB + j
                            k = m % KT
                            dve.wait_ge(s_tr, m + 1)
                            if n < 2:
                                ins = dve.tensor_copy(t.attn_shift[:, k:k + 1], colp[:, 0, 0:1])
                            else:
                                ins = dve.tensor_tensor(t.attn_gain[:, k:k + 1], colp[:, 0, 0:1], gcol[:, k:k + 1], ALU.mult)
                            ins.then_inc(s_col, 1)
                    if n == 3:
                        dve.wait_ge(s_std, 1)
                        st.link(dve.reciprocal(rstd[:, :], std[:, :]))
                        for i in range(TB):
                            dve.tensor_scalar(xs[:, i, :], xs[:, i, :], rstd[:, i:i + 1], None, ALU.mult).then_inc(s_xn, 1)
                dve.wait_ge(s_lamb, 1)
                st.link(dve.tensor_copy(t.neg_lambda[:, :], lamp[:, :]))
                dve.wait_ge(s_col, 4 * TPB)
                for n in range(1, 4 * KT, 2):
                    tg, k = divmod(n, KT)
                    dve.wait_ge(s_xt, n + 1)
                    dve.tensor_scalar(t.hT[:, k, tg * BANK:(tg + 1) * BANK], xtp[n % 4][:, :],
                                      t.attn_gain[:, k:k + 1], t.attn_shift[:, k:k + 1], ALU.mult, ALU.add).then_inc(s_htv, 1)


def forget(nc, a, t):
    with ExitStack() as ctx:
        p = Names(nc, ctx, "fgt_")
        H = FOX_HEADS
        w = p.sb("w_forget", [P, KT, H])
        z = p.sb("z", [H, S])
        nz = p.sb("nz", [H, S])
        ez = p.sb("ez", [H, S])
        lg = p.sb("lg", [H, S])
        ones = p.sb("scan_ones", [H, S])
        ps = [p.ps(f"fp{i}", [H, BANK]) for i in range(CH)]
        s_w, s_p, s_v, s_a, s_out = (p.sem(n) for n in ("wf_loaded", "forget_product", "forget_dve", "forget_act", "neg_f_stored"))
        with nc.Block() as block:

            @block.sync
            def _(sp):
                c = COL["forget"]
                sp.dma_start(w[:, :, :], a["w_in"][0, :, c:c + H].rearrange("(k p) n -> p k n", p=P)).then_inc(s_w, 16)
                sp.wait_ge(s_v, CH + 7)
                sp.dma_start(t.neg_f, z[:, :]).then_inc(s_out, 16)
                sp.wait_ge(s_out, 16)

            @block.tensor
            def _(pe):
                pe.wait_ge(s_w, 16)
                for c in range(CH):
                    for k in range(KT):
                        mm = pe.matmul(ps[c][:, :], w[:, k, :], t.hT[:, k, c * BANK:(c + 1) * BANK],
                                       start=(k == 0), stop=(k == KT - 1))
                    mm.then_inc(s_p, 1)

            @block.vector
            def _(dve):
                st = Steps(dve, s_v)
                for c in range(CH):
                    dve.wait_ge(s_p, c + 1)
                    st.link(dve.tensor_scalar(z[:, c * BANK:(c + 1) * BANK], ps[c][:, :], t.bforget[:, 0:1], None, ALU.add))
                st.link(dve.memset(ones[:, :], 1.0))
                st.link(dve.scalar_tensor_tensor(out=nz[:, :], in0=z[:, :], scalar=-1.0, in1=z[:, :], op0=ALU.mult, op1=ALU.min))
                dve.wait_ge(s_a, 1)
                st.link(dve.tensor_scalar(ez[:, :], ez[:, :], 1.0, None, ALU.add))
                dve.wait_ge(s_a, 2)
                st.link(dve.tensor_scalar(z[:, :], z[:, :], 0.0, None, ALU.min))
                st.link(dve.tensor_tensor(lg[:, :], lg[:, :], z[:, :], ALU.subtract))
                st.link(dve.memset(nz[:, 0:1], 0.0))
                st.link(dve.tensor_tensor_scan(z[:, :], ones[:, :], lg[:, :], 0.0, ALU.mult, ALU.add))

            @block.scalar
            def _(act):
                act.wait_ge(s_v, CH + 2)
                act.activation(ez[:, :], nz[:, :], ACT.Exp).then_inc(s_a, 1)
                act.wait_ge(s_v, CH + 3)
                act.activation(lg[:, :], ez[:, :], ACT.Ln).then_inc(s_a, 1)


def attend(nc, a, t, kind):
    fox = kind == "fox"
    with ExitStack() as ctx:
        p = Names(nc, ctx, kind + "_")
        w = p.sb("w_unit", [P, 3, KT, P])
        qT = p.sb("qT", [P, S])
        kT = p.sb("kT", [P, S])
        v = p.sb("v", [P, TB, P])
        prob = [p.sb(f"prob{i}", [P, S]) for i in range(4)]
        probT = [p.sb(f"probT{i}", [P, TB, P]) for i in range(2)]
        if fox:
            negf = [p.sb(f"negf{m}", [P, S]) for m in range(2)]
        else:
            cos = p.sb("cos", [P, S])
            sin = p.sb("sin", [P, S])
            raw = [p.sb(f"raw{i}", [P, BANK]) for i in range(2)]
            rcos = [p.sb(f"rcos{i}", [P, BANK]) for i in range(2)]
            rsin = [p.sb(f"rsin{i}", [P, BANK]) for i in range(2)]
            rden = p.sb("rden", [P, 2, 2])
            ratio = p.sb("ratio", [P, 2])
        low = p.sb("low", [P, 4, CH])
        den = p.sb("den", [P, 4])
        rec = p.sb("rec", [P, 4])
        outs = [p.sb(f"outs{i}", [P, P]) for i in range(2)]
        sp_ = [p.ps(f"score{i}", [P, BANK]) for i in range(4)]
        tp_ = [p.ps(f"tposed{i}", [P, BANK]) for i in range(2)]
        op_ = [p.ps(f"value{i}", [P, P]) for i in range(2)]
        s_w = p.sem("w_unit_loaded")
        s_hold = p.sem("hold")
        s_rope = p.sem("rope_loaded")
        s_negf = p.sem("neg_f_loaded")
        s_proj = p.sem("projected")
        s_pcopy = p.sem("projection_copied")
        s_rot = p.sem("rotated")
        s_rcos = p.sem("cos_part")
        s_rsin = p.sem("sin_part")
        s_roped = p.sem("roped")
        s_score = p.sem("scored")
        s_scopy = p.sem("score_copied")
        s_exp = p.sem("exponentials")
        s_comb = p.sem("combine_steps")
        s_tr = p.sem("transposed")
        s_tca = p.sem("transpose_copied_act")
        s_tcv = p.sem("transpose_copied_dve")
        s_val = p.sem("values_done")
        s_rec = p.sem("reciprocals")
        s_ocopy = p.sem("output_copied")
        s_store = [p.sem(f"output_stored{i}") for i in range(2)]

        NPROJ = 12
        NROPE = 8
        def chunks(i):
            return i // TPB + 1
        def width(i, c):
            return min(BANK, (i + 1) * P - c * BANK)
        jobs = [(i, m) for i in range(TB) for m in range(2)]
        first_chunk = {}
        n = 0
        for j in jobs:
            first_chunk[j] = n
            n += chunks(j[0])
        NSC = n
        tjobs = jobs if fox else [(i, 0) for i in range(TB)]
        first_group = {}
        n = 0
        for j in tjobs:
            first_group[j] = n
            n += chunks(j[0])
        NTG = n
        NTJ = len(tjobs)
        def by_dve(g):
            return fox and g % 2 == 1
        A_T = sum(not by_dve(g) for g in range(NTG))
        V_T = NTG - A_T
        def copies_before(g, dve):
            return sum(by_dve(x) == dve for x in range(g))
        PER_COMB = 3

        def w_cols(u, part):
            c = COL[kind][part]
            return a["w_in"][0, :, bass.ds(u * P + c, P)].rearrange("(k p) n -> p k n", p=P)

        with nc.Block() as block:

            @block.gpsimd
            def _(pool):
                if not fox:
                    pool.dma_start(cos[:, :], a["rope_cos"]).then_inc(s_rope, 16)
                    pool.dma_start(sin[:, :], a["rope_sin"]).then_inc(s_rope, 16)
                with pool.Fori(0, UNITS) as u:
                    pool.wait_ge(s_proj, u * NPROJ)
                    for part in range(3):
                        pool.dma_start(w[:, part, :, :], w_cols(u, part)).then_inc(s_w, 16)
                    if fox:
                        pool.wait_ge(s_scopy, u * NSC)
                        for m in range(2):
                            pool.dma_start(negf[m][:, :], t.neg_f[bass.ds(u * 2 + m, 1), :].to_broadcast([P, S])).then_inc(s_negf, 16)
                    else:
                        for n in range(NROPE):
                            c = slice((n % CH) * BANK, (n % CH + 1) * BANK)
                            if n == 0:
                                pool.wait_ge(s_rope, 32)
                            pool.wait_ge(s_pcopy, u * NPROJ + n + 1)
                            if n >= 2:
                                pool.wait_ge(s_roped, u * NROPE + n - 1)
                            pool.tensor_tensor(rcos[n % 2][:, :], raw[n % 2][:, :], cos[:, c], ALU.mult).then_inc(s_rcos, 1)

            @block.sync
            def _(sp):
                with sp.Fori(0, UNITS) as u:
                    for i in range(TB):
                        sp.wait_ge(s_ocopy, u * NTJ + (2 * i + 2 if fox else i + 1))
                        c = 0 if not fox else UNITS * P
                        sp.dma_start(t.mixed[i * P:(i + 1) * P, bass.ds(u * P + c, P)], outs[i % 2][:, :]).then_inc(s_store[i % 2], 16)
                for b in range(2):
                    sp.wait_ge(s_store[b], 16 * UNITS * TB // 2)

            @block.tensor
            def _(pe):
                with pe.Fori(0, UNITS) as u:
                    def rotate(n):
                        pe.wait_ge(s_pcopy, u * NPROJ + n + 1)
                        if n >= 2:
                            pe.wait_ge(s_rsin, u * NROPE + n - 1)
                        pe.matmul(tp_[n % 2][:, :], t.rot, raw[n % 2][:, :], start=True, stop=True).then_inc(s_rot, 1)

                    pe.wait_ge(s_w, (u + 1) * 48)
                    for n in range(8):
                        part, c = divmod(n, CH)
                        if n < 4:
                            if n == 0:
                                pe.wait_ge(s_scopy, u * NSC)
                        else:
                            pe.wait_ge(s_pcopy, u * NPROJ + n - 3)
                        for k in range(KT):
                            mm = pe.matmul(sp_[n % 4][:, :], w[:, part, k, :], t.hT[:, k, c * BANK:(c + 1) * BANK],
                                           start=(k == 0), stop=(k == KT - 1))
                        mm.then_inc(s_proj, 1)
                        if not fox and n >= 1:
                            rotate(n - 1)
                    for n in range(8, NPROJ):
                        pe.wait_ge(s_pcopy, u * NPROJ + n - 3)
                        for j in range(TPB):
                            i = (n - 8) * TPB + j
                            for k in range(KT):
                                mm = pe.matmul(sp_[n % 4][:, j * P:(j + 1) * P], t.hT[:, k, i * P:(i + 1) * P],
                                               w[:, 2, k, :], start=(k == 0), stop=(k == KT - 1))
                        mm.then_inc(s_proj, 1)
                        if not fox and n == 8:
                            rotate(7)

                    def score(i, m):
                        for c in range(chunks(i)):
                            n = first_chunk[i, m] + c
                            if n < 4:
                                if n == 0:
                                    pe.wait_ge(s_pcopy, (u + 1) * NPROJ)
                                    if not fox:
                                        pe.wait_ge(s_roped, (u + 1) * NROPE)
                            else:
                                pe.wait_ge(s_scopy, u * NSC + n - 3)
                            wd = width(i, c)
                            last = c == chunks(i) - 1
                            mm = pe.matmul(sp_[n % 4][:, 0:wd], qT[HD * m:HD * m + HD, i * P:(i + 1) * P],
                                           kT[HD * m:HD * m + HD, c * BANK:c * BANK + wd], start=True, stop=not last)
                            if last:
                                mm = pe.matmul(sp_[n % 4][:, wd - P:wd], t.ident_bf[:, :], t.mask[kind][:, :], start=False, stop=True)
                            mm.then_inc(s_score, 1)

                    def group_copied(g):
                        if by_dve(g):
                            pe.wait_ge(s_tcv, u * V_T + copies_before(g, True) + 1)
                        else:
                            pe.wait_ge(s_tca, u * A_T + copies_before(g, False) + 1)

                    def turn(i, m, c):
                        g = first_group[i, m] + c
                        if g >= 2:
                            group_copied(g - 2)
                        src = prob[(i % 2) * 2 + m]
                        for b in range(c * TPB, min((c + 1) * TPB, i + 1)):
                            mm = pe.transpose(tp_[g % 2][:, (b % TPB) * P:(b % TPB + 1) * P], src[:, b * P:(b + 1) * P], t.ident)
                        mm.then_inc(s_tr, 1)

                    def value(i, m, c):
                        group_copied(first_group[i, m] + c)
                        n = tjobs.index((i, m))
                        if c == 0 and n >= 2:
                            pe.wait_ge(s_ocopy, u * NTJ + n - 1)
                        cols = slice(HD * m, HD * m + HD) if fox else slice(0, P)
                        o = op_[n % 2][:, 0:HD] if fox else op_[n % 2][:, :]
                        for b in range(c * TPB, min((c + 1) * TPB, i + 1)):
                            mm = pe.matmul(o, probT[n % 2][:, b, :], v[:, b, cols], start=(b == 0), stop=(b == i))
                        if c == chunks(i) - 1:
                            mm.then_inc(s_val, 1)

                    def mix(i):
                        for m in range(2 if fox else 1):
                            if fox:
                                pe.wait_ge(s_exp, u * 2 * TB + 2 * i + m + 1)
                            else:
                                pe.wait_ge(s_comb, u * TB * PER_COMB + (i + 1) * PER_COMB)
                            turn(i, m, 0)
                            for c in range(chunks(i)):
                                if c + 1 < chunks(i):
                                    turn(i, m, c + 1)
                                value(i, m, c)

                    score(0, 0)
                    score(0, 1)
                    for i in range(TB):
                        if i + 1 < TB:
                            score(i + 1, 0)
                            score(i + 1, 1)
                        mix(i)

            @block.scalar
            def _(act):
                with act.Fori(0, UNITS) as u:
                    for n in range(NPROJ):
                        act.wait_ge(s_proj, u * NPROJ + n + 1)
                        part, c = divmod(n, CH)
                        cols = slice(c * BANK, (c + 1) * BANK)
                        if part == 2:
                            act.activation(v[:, c * TPB:(c + 1) * TPB, :], sp_[n % 4][:, :].rearrange("p (b n) -> p b n", n=P),
                                           ACT.Copy).then_inc(s_pcopy, 1)
                            continue
                        if fox:
                            dst = (qT, kT)[part][:, cols]
                        else:
                            dst = raw[n % 2][:, :]
                            if n >= 2:
                                act.wait_ge(s_rot, u * NROPE + n - 1)
                                act.wait_ge(s_rcos, u * NROPE + n - 1)
                        act.activation(dst, sp_[n % 4][:, :], ACT.Copy, scale=QK_SCALE if part == 0 else 1.0).then_inc(s_pcopy, 1)

                    def exps(i):
                        for m in range(2):
                            b = (i % 2) * 2 + m
                            act.wait_ge(s_scopy, u * NSC + first_chunk[i, m] + chunks(i))
                            act.activation(prob[b][:, 0:(i + 1) * P], prob[b][:, 0:(i + 1) * P], ACT.Exp, scale=-1.0,
                                           bias=low[:, b, chunks(i) - 1:chunks(i)],
                                           accum_out=den[:, b:b + 1]).then_inc(s_exp, 1)

                    def copies(i):
                        for m in range(2 if fox else 1):
                            n = tjobs.index((i, m))
                            for c in range(chunks(i)):
                                g = first_group[i, m] + c
                                if by_dve(g):
                                    continue
                                act.wait_ge(s_tr, u * NTG + g + 1)
                                lo, hi = c * TPB, min((c + 1) * TPB, i + 1)
                                act.activation(probT[n % 2][:, lo:hi, :], tp_[g % 2][:, 0:(hi - lo) * P].rearrange("p (b n) -> p b n", n=P),
                                               ACT.Copy).then_inc(s_tca, 1)

                    exps(0)
                    for i in range(TB):
                        copies(i)
                        if i + 1 < TB:
                            exps(i + 1)

            @block.vector
            def _(dve):
                with dve.Fori(0, UNITS) as u:
                    if not fox:
                        for n in range(NROPE):
                            part, c = divmod(n, CH)
                            cols = slice(c * BANK, (c + 1) * BANK)
                            dve.wait_ge(s_rot, u * NROPE + n + 1)
                            if n == 0:
                                dve.wait_ge(s_rope, 32)
                            if n >= 2:
                                dve.wait_ge(s_roped, u * NROPE + n - 1)
                            dve.tensor_tensor(rsin[n % 2][:, :], tp_[n % 2][:, :], sin[:, cols], ALU.mult).then_inc(s_rsin, 1)
                            dve.wait_ge(s_rsin, u * NROPE + n + 1)
                            dve.wait_ge(s_rcos, u * NROPE + n + 1)
                            dve.tensor_tensor((qT, kT)[part][:, cols], rcos[n % 2][:, :], rsin[n % 2][:, :], ALU.add).then_inc(s_roped, 1)
                    else:
                        dve.wait_ge(s_negf, (u + 1) * 32)

                    def copy_scores(i, m):
                        b = (i % 2) * 2 + m
                        for c in range(chunks(i)):
                            n = first_chunk[i, m] + c
                            wd = width(i, c)
                            dve.wait_ge(s_score, u * NSC + n + 1)
                            if c:
                                dve.wait_ge(s_scopy, u * NSC + n)
                            init = low[:, b, c - 1:c] if c else BIG
                            if fox:
                                dve.sem_inc(s_hold, 1)
                                ins = dve.tensor_tensor_reduce(out=prob[b][:, c * BANK:c * BANK + wd], in0=sp_[n % 4][:, 0:wd],
                                                               in1=negf[m][:, c * BANK:c * BANK + wd], scale=-1.0, scalar=init,
                                                               op0=ALU.add, op1=ALU.min, accum_out=low[:, b, c:c + 1])
                            else:
                                ins = dve.tensor_scalar(prob[b][:, c * BANK:c * BANK + wd], sp_[n % 4][:, 0:wd], -1.0, init,
                                                        ALU.mult, ALU.min, accum_out=low[:, b, c:c + 1])
                            ins.then_inc(s_scopy, 1)

                    def combine(i):
                        b = (i % 2) * 2
                        r = i % 2
                        base = u * TB * PER_COMB + i * PER_COMB
                        dve.wait_ge(s_exp, u * 2 * TB + 2 * i + 2)
                        dve.reciprocal(rden[:, r, :], den[:, b:b + 2]).then_inc(s_comb, 1)
                        dve.wait_ge(s_comb, base + 1)
                        dve.scalar_tensor_tensor(out=ratio[:, r:r + 1], in0=rden[:, r, 1:2], scalar=den[:, b:b + 1],
                                                 in1=t.neg_lambda[:, :], op0=ALU.mult, op1=ALU.mult).then_inc(s_comb, 1)
                        dve.wait_ge(s_comb, base + 2)
                        dve.scalar_tensor_tensor(out=prob[b][:, 0:(i + 1) * P], in0=prob[b + 1][:, 0:(i + 1) * P],
                                                 scalar=ratio[:, r:r + 1], in1=prob[b][:, 0:(i + 1) * P],
                                                 op0=ALU.mult, op1=ALU.add).then_inc(s_comb, 1)

                    def copies(i, m):
                        n = tjobs.index((i, m))
                        for c in range(chunks(i)):
                            g = first_group[i, m] + c
                            if by_dve(g):
                                dve.wait_ge(s_tr, u * NTG + g + 1)
                                lo, hi = c * TPB, min((c + 1) * TPB, i + 1)
                                dve.tensor_copy(probT[n % 2][:, lo:hi, :],
                                                tp_[g % 2][:, 0:(hi - lo) * P].rearrange("p (b n) -> p b n", n=P)).then_inc(s_tcv, 1)

                    def output(i, m):
                        n = tjobs.index((i, m))
                        if m == 0:
                            dve.wait_ge(s_store[i % 2], u * (16 * TB // 2) + 16 * (i // 2))
                        if fox:
                            b = (i % 2) * 2 + m
                            dve.wait_ge(s_exp, u * 2 * TB + 2 * i + m + 1)
                            dve.reciprocal(rec[:, b:b + 1], den[:, b:b + 1]).then_inc(s_rec, 1)
                            dve.wait_ge(s_rec, u * 2 * TB + 2 * i + m + 1)
                            dve.wait_ge(s_val, u * NTJ + n + 1)
                            dve.tensor_scalar(outs[i % 2][:, HD * m:HD * m + HD], op_[n % 2][:, 0:HD], rec[:, b:b + 1], None,
                                              ALU.mult).then_inc(s_ocopy, 1)
                        else:
                            dve.wait_ge(s_val, u * NTJ + n + 1)
                            dve.tensor_scalar(outs[i % 2][:, :], op_[n % 2][:, :], rden[:, i % 2, 0:1], None,
                                              ALU.mult).then_inc(s_ocopy, 1)

                    copy_scores(0, 0)
                    copy_scores(0, 1)
                    for i in range(TB):
                        if i + 1 < TB:
                            copy_scores(i + 1, 0)
                            if not fox:
                                combine(i)
                            copy_scores(i + 1, 1)
                        elif not fox:
                            combine(i)
                        for m in range(2 if fox else 1):
                            copies(i, m)
                            output(i, m)


def load_expert(eng, a, t, e, slot, free=lambda name: None):
    for name, at, rows, cols in (("w_gate", W_GATE, KT, F), ("w_up", W_UP, KT, F), ("w_down", W_DOWN, FT, D)):
        free(name)
        eng.dma_start(t.weights[:, slot, at:at + rows * cols].rearrange("p (k n) -> p k n", n=cols),
                      a[name][0, bass.ds(e, 1)].rearrange("a (k p) n -> p (a k) n", p=P)).then_inc(t.s_w[name][slot], 16)


def merge(nc, a, t):
    with ExitStack() as ctx:
        p = Names(nc, ctx, "mrg_")
        spare = t.weights[:, 1, :]
        w_out = spare[:, 0:KT * D].rearrange("p (k n) -> p k n", n=D)
        xx, junk, mT, h2T = (spare[:, (KT + n) * D:(KT + n + 1) * D] for n in range(4))
        mT, h2T = (x.rearrange("p (k n) -> p k n", n=P) for x in (mT, h2T))
        w_rt = p.sb("w_router_sb", [P, KT, LOGITS])
        b_rt = p.sb("b_router_sb", [P, LOGITS])
        mx = p.sb("mx", [P, D])
        sq = p.sb("sq", [P, F])
        ssh = p.sb("ssh", [P, 4])
        stdh = p.sb("stdh", [P, 4])
        rh = p.sb("rh", [P, 4])
        o = p.sb("o", [P, D])
        h2 = p.sb("h2", [P, D])
        ss = p.sb("ss", [P, 2])
        sd = p.sb("sd", [P, 2])
        rr = p.sb("rr", [P, 2])
        mtp = [p.ps(f"mtp{i}", [P, BANK]) for i in range(2)]
        outp = p.ps("outp", [P, 2, BANK])
        htp = [p.ps(f"htp{i}", [P, BANK]) for i in range(2)]
        rtp = p.ps("rtp", [P, LOGITS])
        names = ("w_loaded mixed_loaded x_loaded head_squares head_std heads_scaled mixed_turned mT_copied "
                 "projected_out out_copied out_squares out_std x1_steps x1_squares x1_std h2_steps h2_stored "
                 "h2_turned h2T_copied router_product logits_done dve_links").split()
        s = {n: p.sem("m_" + n) for n in names}

        with nc.Block() as block:

            @block.gpsimd
            def _(pool):
                pool.dma_start(w_rt[:, :, 0:GROUPS], a["w_group"][0].rearrange("(k p) n -> p k n", p=P)).then_inc(s["w_loaded"], 16)
                pool.dma_start(w_rt[:, :, GROUPS:], a["w_router"][0].rearrange("(k p) n -> p k n", p=P)).then_inc(s["w_loaded"], 16)
                pool.dma_start(b_rt[:, 0:GROUPS], a["b_group"].to_broadcast([P, GROUPS])).then_inc(s["w_loaded"], 16)
                pool.dma_start(b_rt[:, GROUPS:], a["b_router"].to_broadcast([P, EXPERTS])).then_inc(s["w_loaded"], 16)
                pool.dma_start(w_out[:, :, :], a["w_out"][0].rearrange("(k p) n -> p k n", p=P)).then_inc(s["w_loaded"], 16)
                with pool.Fori(0, TB) as i:
                    pool.wait_ge(s["x1_steps"], 2 * i)
                    pool.dma_start(xx[:, :], a["x"][0, bass.ds(i * P, P), :]).then_inc(s["x_loaded"], 16)

            @block.sync
            def _(sp):
                sp.dma_start(mx[:, :], t.mixed[0:P, :]).then_inc(s["mixed_loaded"], 16)
                load_expert(sp, a, t, 0, 0)
                with sp.Fori(0, TB - 1) as i:
                    sp.wait_ge(s["mixed_turned"], 2 * i + 2)
                    sp.dma_start(mx[:, :], t.mixed[bass.ds(i * P + P, P), :]).then_inc(s["mixed_loaded"], 16)
                    sp.wait_ge(s["h2_steps"], 2 * i + 2)
                    sp.dma_start(t.h2[bass.ds(i * P, P), :], h2[:, :]).then_inc(s["h2_stored"], 16)
                sp.wait_ge(s["h2_steps"], 2 * TB)
                sp.dma_start(t.h2[(TB - 1) * P:, :], h2[:, :]).then_inc(s["h2_stored"], 16)
                sp.wait_ge(s["h2_stored"], 16 * TB)

            @block.tensor
            def _(pe):
                def turn(i):
                    pe.wait_ge(s["heads_scaled"], i + 1)
                    pe.wait_ge(s["mT_copied"], i * 2)
                    for h in range(2):
                        for j in range(TPB):
                            mm = pe.transpose(mtp[h][:, j * P:(j + 1) * P], mx[:, (h * TPB + j) * P:(h * TPB + j + 1) * P], t.ident)
                        mm.then_inc(s["mixed_turned"], 1)

                def project(i):
                    pe.wait_ge(s["mT_copied"], i * 2 + 2)
                    pe.wait_ge(s["out_copied"], i)
                    for h in range(2):
                        for k in range(KT):
                            mm = pe.matmul(outp[:, h, :], mT[:, k, :], w_out[:, k, h * BANK:(h + 1) * BANK],
                                           start=(k == 0), stop=(k == KT - 1))
                    mm.then_inc(s["projected_out"], 1)

                def router(i):
                    pe.wait_ge(s["h2_steps"], i * 2 + 2)
                    pe.wait_ge(s["h2T_copied"], i * 2)
                    for h in range(2):
                        for j in range(TPB):
                            mm = pe.transpose(htp[h][:, j * P:(j + 1) * P], h2[:, (h * TPB + j) * P:(h * TPB + j + 1) * P], t.ident)
                        mm.then_inc(s["h2_turned"], 1)
                    pe.wait_ge(s["h2T_copied"], i * 2 + 2)
                    pe.wait_ge(s["logits_done"], i)
                    for k in range(KT):
                        mm = pe.matmul(rtp[:, :], h2T[:, k, :], w_rt[:, k, :], start=(k == 0), stop=(k == KT - 1))
                    mm.then_inc(s["router_product"], 1)

                pe.wait_ge(s["w_loaded"], 80)
                turn(0)
                project(0)
                turn(1)
                with pe.Fori(1, TB - 1) as i:
                    project(i)
                    turn(i + 1)
                    router(i - 1)
                project(TB - 1)
                router(TB - 2)
                router(TB - 1)

            @block.scalar
            def _(act):
                def head_std(i):
                    act.wait_ge(s["head_squares"], 2 * i + 2)
                    act.activation(stdh[:, :], ssh[:, :], ACT.Sqrt, scale=1.0 / P, bias=t.eps[:, :]).then_inc(s["head_std"], 1)

                def copy_turned(i):
                    act.wait_ge(s["mixed_turned"], 2 * i + 1)
                    act.activation(mT[:, 0:TPB, :], mtp[0][:, :].rearrange("p (b n) -> p b n", n=P), ACT.Identity,
                                   scale=t.subln[:, :]).then_inc(s["mT_copied"], 1)
                    act.wait_ge(s["mixed_turned"], 2 * i + 2)
                    act.activation(mT[:, TPB:, :], mtp[1][:, :].rearrange("p (b n) -> p b n", n=P), ACT.Copy).then_inc(s["mT_copied"], 1)

                def stds(i):
                    act.wait_ge(s["out_copied"], i + 1)
                    act.wait_ge(s["x1_squares"], i)
                    act.activation(junk[:, :], o[:, :], ACT.Square, accum_out=ss[:, 0:1]).then_inc(s["out_squares"], 1)
                    act.wait_ge(s["out_squares"], i + 1)
                    act.activation(sd[:, 0:1], ss[:, 0:1], ACT.Sqrt, scale=1.0 / D, bias=t.eps[:, :]).then_inc(s["out_std"], 1)
                    act.wait_ge(s["x1_steps"], 2 * i + 2)
                    act.activation(junk[:, :], t.x1[:, bass.ds(i, 1), :].rearrange("p a d -> p (a d)"), ACT.Square,
                                   accum_out=ss[:, 1:2]).then_inc(s["x1_squares"], 1)
                    act.wait_ge(s["x1_squares"], i + 1)
                    act.activation(sd[:, 1:2], ss[:, 1:2], ACT.Sqrt, scale=1.0 / D, bias=t.eps[:, :]).then_inc(s["x1_std"], 1)

                def copy_h2(i):
                    for h in range(2):
                        act.wait_ge(s["h2_turned"], 2 * i + h + 1)
                        act.activation(h2T[:, h * TPB:(h + 1) * TPB, :], htp[h][:, :].rearrange("p (b n) -> p b n", n=P),
                                       ACT.Copy).then_inc(s["h2T_copied"], 1)

                head_std(0)
                copy_turned(0)
                head_std(1)
                copy_turned(1)
                stds(0)
                with act.Fori(1, TB - 1) as i:
                    head_std(i + 1)
                    copy_turned(i + 1)
                    copy_h2(i - 1)
                    stds(i)
                copy_h2(TB - 2)
                stds(TB - 1)
                copy_h2(TB - 1)

            @block.vector
            def _(dve):
                heads = mx[:, 0:F].rearrange("p (h e) -> p h e", e=P)

                def head_part(i, links):
                    dve.wait_ge(s["mixed_loaded"], 16 * (i + 1))
                    dve.tensor_tensor(sq[:, :], mx[:, 0:F], mx[:, 0:F], ALU.mult).then_inc(s["head_squares"], 1)
                    dve.wait_ge(s["head_squares"], 2 * i + 1)
                    dve.tensor_reduce(ssh[:, :], sq[:, :].rearrange("p (h e) -> p h e", e=P), X, ALU.add).then_inc(s["head_squares"], 1)
                    dve.wait_ge(s["head_std"], i + 1)
                    dve.reciprocal(rh[:, :], stdh[:, :]).then_inc(s["dve_links"], 1)
                    dve.wait_ge(s["dve_links"], links + 1)
                    dve.tensor_tensor(heads, heads, rh[:, :].unsqueeze(2).to_broadcast([P, 4, P]), ALU.mult).then_inc(s["heads_scaled"], 1)

                def row_part(i, links):
                    x1 = t.x1[:, bass.ds(i, 1), :].rearrange("p a d -> p (a d)")
                    dve.wait_ge(s["projected_out"], i + 1)
                    dve.tensor_copy(o[:, :], outp[:, :, :].rearrange("p a d -> p (a d)")).then_inc(s["out_copied"], 1)
                    dve.wait_ge(s["out_std"], i + 1)
                    dve.reciprocal(rr[:, 0:1], sd[:, 0:1]).then_inc(s["dve_links"], 1)
                    dve.wait_ge(s["dve_links"], links + 1)
                    dve.scalar_tensor_tensor(out=x1, in0=o[:, :], scalar=rr[:, 0:1], in1=t.gate_attn[:, :],
                                             op0=ALU.mult, op1=ALU.mult).then_inc(s["x1_steps"], 1)
                    dve.wait_ge(s["x1_steps"], 2 * i + 1)
                    dve.wait_ge(s["x_loaded"], 16 * (i + 1))
                    dve.tensor_tensor(x1, x1, xx[:, :], ALU.add).then_inc(s["x1_steps"], 1)
                    dve.wait_ge(s["x1_std"], i + 1)
                    dve.reciprocal(rr[:, 1:2], sd[:, 1:2]).then_inc(s["dve_links"], 1)
                    dve.wait_ge(s["dve_links"], links + 2)
                    dve.wait_ge(s["h2_stored"], 16 * i)
                    dve.wait_ge(s["h2_turned"], 2 * i)
                    dve.scalar_tensor_tensor(out=h2[:, :], in0=x1, scalar=rr[:, 1:2], in1=t.ffn_gain[:, :],
                                             op0=ALU.mult, op1=ALU.mult).then_inc(s["h2_steps"], 1)
                    dve.wait_ge(s["h2_steps"], 2 * i + 1)
                    dve.tensor_tensor(h2[:, :], h2[:, :], t.ffn_shift[:, :], ALU.add).then_inc(s["h2_steps"], 1)

                def logits(i):
                    dve.wait_ge(s["router_product"], i + 1)
                    dve.tensor_tensor(t.logits[:, bass.ds(i, 1), :].rearrange("p a n -> p (a n)"), rtp[:, :], b_rt[:, :],
                                      ALU.add).then_inc(s["logits_done"], 1)

                head_part(0, 0)
                head_part(1, 1)
                row_part(0, 2)
                with dve.Fori(1, TB - 1) as i:
                    head_part(i + 1, 3 * i + 1)
                    row_part(i, 3 * i + 2)
                    logits(i - 1)
                row_part(TB - 1, 3 * TB - 2)
                logits(TB - 2)
                logits(TB - 1)


def route(nc, a, t):
    with ExitStack() as ctx:
        p = Names(nc, ctx, "rt_")
        G, E8, E = GROUPS, PER_GROUP, EXPERTS
        def tile(name, *shape, dt=F32):
            return p.sb(name, [P, *shape], dt)
        gmax, gpick, gw, m1, m2, pick = (tile(n, TB) for n in ("gmax", "gpick", "gw", "m1", "m2", "pick"))
        geq, goh, gexp = (tile(n, TB, G) for n in ("geq", "goh", "gexp"))
        emask = tile("emask", TB, G, E8)
        esel, eeq, oh1, oh2, esel2 = (tile(n, TB, E8) for n in ("esel", "eeq", "oh1", "oh2", "esel2"))
        gap, egap, dsum = (tile(n, TB) for n in ("gap", "egap", "dsum"))
        E1, E2, off, rank = (row[:, h * TB * E:(h + 1) * TB * E].rearrange("p (t e) -> p t e", e=E)
                             for row in (t.gate_attn, t.ffn_gain) for h in range(2))
        both = tile("both", TB, E, dt=BF16)
        prod = tile("prod", TB, E)
        cnt = tile("cnt", E)
        cnti, nbi = tile("cnti", E, dt=I32), tile("nbi", E, dt=I32)
        nb, ones = tile("nb", E), tile("ones_e", E)
        ended = tile("ended", TABLE, E, dt=BF16)
        owner = tile("owner", TABLE)
        owneri, half = tile("owneri", TABLE, dt=I32), tile("half", TABLE, dt=I32)
        cum = tile("cum", E + 1)
        dest = tile("dest", 2, TB)
        desti, pi, bi = (tile(n, 2, TB, dt=I32) for n in ("desti", "pi", "bi"))
        pf, bf = tile("pf", 2, TB), tile("bf", 2, TB)
        vals = tile("vals", 2, TB)
        tab, second, unused = (tile(n, TABLE) for n in ("tab", "second", "unused"))
        at_p = [tile(f"at_p{i}", P) for i in range(2)]
        at_b = [tile(f"at_b{i}", TABLE) for i in range(2)]
        prefix = p.ps("prefix", [P, TB * E])
        totals = p.ps("totals", [P, TB * E])
        table = p.ps("table", [P, TABLE])
        s_v, s_a, s_cnt, s_at, s_tab = (p.sem(n) for n in
                                        ("r_dve", "r_exp", "r_counted", "r_onehots", "r_table"))
        READY_G, READY_E, READY_B = [0], [0], [0]

        with nc.Block() as block:

            @block.sync
            def _(sp):
                load_expert(sp, a, t, 1, 1)

            @block.vector
            def _(dve):
                st = Steps(dve, s_v)
                L = st.link
                gl = t.logits[:, :, 0:G]
                el = t.logits[:, :, G:].rearrange("p t (g e) -> p t g e", g=G)
                gdesc = t.consts[:, C_GDESC:C_GDESC + G].unsqueeze(1).to_broadcast([P, TB, G])
                edesc = t.consts[:, C_EDESC:C_EDESC + E8].unsqueeze(1).to_broadcast([P, TB, E8])

                def wide(x, n):
                    return x[:, :].unsqueeze(2).to_broadcast([P, TB, n])

                def first_max(src, value, equal, chosen, desc, n):
                    L(dve.tensor_reduce(value[:, :], src, X, ALU.max))
                    L(dve.tensor_tensor(equal[:, :, :], src, wide(value, n), ALU.is_equal))
                    L(dve.tensor_tensor(equal[:, :, :], equal[:, :, :], desc, ALU.mult))
                    L(dve.tensor_reduce(pick[:, :], equal[:, :, :], X, ALU.max))
                    L(dve.tensor_tensor(chosen[:, :, :], equal[:, :, :], wide(pick, n), ALU.is_equal))

                first_max(gl, gmax, geq, goh, gdesc, G)
                L(dve.tensor_tensor(gexp[:, :, :], gl, wide(gmax, G), ALU.subtract))
                READY_G[0] = st.n
                for g in range(G):
                    L(dve.tensor_tensor(emask[:, :, g, :], el[:, :, g, :], goh[:, :, g:g + 1].to_broadcast([P, TB, E8]), ALU.mult))
                L(dve.tensor_reduce(esel[:, :, :], emask[:, :, :, :].rearrange("p t g e -> p t e g"), X, ALU.add))
                first_max(esel[:, :, :], m1, eeq, oh1, edesc, E8)
                L(dve.scalar_tensor_tensor(out=esel2[:, :, :], in0=oh1[:, :, :], scalar=-BIG, in1=esel[:, :, :], op0=ALU.mult, op1=ALU.add))
                first_max(esel2[:, :, :], m2, eeq, oh2, edesc, E8)
                L(dve.tensor_tensor(gap[:, :], m2[:, :], m1[:, :], ALU.subtract))
                READY_E[0] = st.n
                for g in range(G):
                    gb = goh[:, :, g:g + 1].to_broadcast([P, TB, E8])
                    L(dve.tensor_tensor(E1[:, :, g * E8:(g + 1) * E8], oh1[:, :, :], gb, ALU.mult))
                    L(dve.tensor_tensor(E2[:, :, g * E8:(g + 1) * E8], oh2[:, :, :], gb, ALU.mult))
                L(dve.tensor_tensor(both[:, :, :], E1[:, :, :], E2[:, :, :], ALU.add))
                READY_B[0] = st.n
                dve.wait_ge(s_a, 1)
                L(dve.tensor_reduce(gw[:, :], gexp[:, :, :], X, ALU.add))
                L(dve.reciprocal(gw[:, :], gw[:, :]))
                dve.wait_ge(s_a, 2)
                L(dve.tensor_scalar(dsum[:, :], egap[:, :], 1.0, None, ALU.add))
                L(dve.reciprocal(dsum[:, :], dsum[:, :]))
                L(dve.tensor_tensor(t.weight[:, 0, :], gw[:, :], dsum[:, :], ALU.mult))
                L(dve.tensor_tensor(t.weight[:, 1, :], t.weight[:, 0, :], egap[:, :], ALU.mult))
                dve.wait_ge(s_cnt, 2)
                tot = totals[:, :].rearrange("p (t e) -> p t e", e=E)
                L(dve.memset(off[:, 0, :], 0.0))
                for i in range(1, TB):
                    L(dve.tensor_tensor(off[:, i, :], off[:, i - 1, :], tot[:, i - 1, :], ALU.add))
                L(dve.tensor_tensor(cnt[:, :], off[:, TB - 1, :], tot[:, TB - 1, :], ALU.add))
                L(dve.tensor_tensor(rank[:, :, :], off[:, :, :], prefix[:, :].rearrange("p (t e) -> p t e", e=E), ALU.add))
                L(dve.tensor_scalar(cnti[:, :], cnt[:, :], float(P - 1), None, ALU.add))
                L(dve.tensor_scalar(nbi[:, :], cnti[:, :], P.bit_length() - 1, None, ALU.logical_shift_right))
                L(dve.tensor_scalar(nb[:, :], nbi[:, :], 1.0, None, ALU.max))
                L(dve.memset(ones[:, :], 1.0))
                L(dve.memset(cum[:, 0:1], 0.0))
                L(dve.tensor_tensor_scan(cum[:, 1:E + 1], ones[:, :], nb[:, :], 0.0, ALU.mult, ALU.add))
                L(dve.tensor_copy(t.cum_blocks[:, 0:E + 1], cum[:, :]))
                L(dve.tensor_scalar(t.cum_blocks[:, E + 1:E + 2], cum[:, E:E + 1], -1.0, None, ALU.add))
                L(dve.memset(t.cum_prev[:, 0:1], 0))
                L(dve.tensor_copy(t.cum_prev[:, 1:E], cum[:, 0:E - 1]))
                L(dve.tensor_tensor(ended[:, :, :], cum[:, 1:E + 1].unsqueeze(1).to_broadcast([P, TABLE, E]),
                                    t.consts[:, C_IOTA:C_IOTA + TABLE].unsqueeze(2).to_broadcast([P, TABLE, E]), ALU.is_le))
                L(dve.tensor_reduce(owner[:, :], ended[:, :, :], X, ALU.add))
                L(dve.tensor_copy(owneri[:, :], owner[:, :]))
                L(dve.tensor_scalar(t.slot[:, :], owneri[:, :], 1, None, ALU.bitwise_and))
                L(dve.tensor_scalar(half[:, :], owneri[:, :], 1, None, ALU.logical_shift_right))
                L(dve.tensor_scalar(t.loads[:, 0, :], half[:, :], 1.0, 16.0, ALU.add, ALU.mult))
                L(dve.tensor_scalar(owneri[:, :], owneri[:, :], 1.0, None, ALU.add))
                L(dve.tensor_scalar(half[:, :], owneri[:, :], 1, None, ALU.logical_shift_right))
                L(dve.tensor_scalar(t.loads[:, 1, :], half[:, :], 16.0, None, ALU.mult))
                L(dve.tensor_scalar(cum[:, :], cum[:, :], float(P), None, ALU.mult))
                L(dve.tensor_tensor(rank[:, :, :], rank[:, :, :], cum[:, 0:E].unsqueeze(1).to_broadcast([P, TB, E]), ALU.add))
                for n, oh in enumerate((E1, E2)):
                    L(dve.tensor_tensor(prod[:, :, :], oh[:, :, :], rank[:, :, :], ALU.mult))
                    L(dve.tensor_reduce(dest[:, n, :], prod[:, :, :], X, ALU.add))
                L(dve.tensor_copy(desti[:, :, :], dest[:, :, :]))
                L(dve.tensor_scalar(pi[:, :, :], desti[:, :, :], P - 1, None, ALU.bitwise_and))
                L(dve.tensor_scalar(bi[:, :, :], desti[:, :, :], P.bit_length() - 1, None, ALU.logical_shift_right))
                L(dve.tensor_copy(pf[:, :, :], pi[:, :, :]))
                L(dve.tensor_copy(bf[:, :, :], bi[:, :, :]))
                L(dve.tensor_scalar(vals[:, 0, :], t.consts[:, C_TOKEN:C_TOKEN + TB], 1.0, None, ALU.add))
                L(dve.tensor_scalar(vals[:, 1, :], t.consts[:, C_TOKEN:C_TOKEN + TB], 1.0 + S, None, ALU.add))
                for q in range(2 * TB):
                    n, i = divmod(q, TB)
                    if q >= 2:
                        dve.wait_ge(s_tab, q - 1)
                    dve.tensor_scalar(at_p[q % 2][:, :], t.consts[:, C_IOTA:C_IOTA + P], pf[:, n, i:i + 1], None,
                                      ALU.is_equal).then_inc(s_at, 1)
                    dve.tensor_scalar(at_b[q % 2][:, :], t.consts[:, C_IOTA:C_IOTA + TABLE], bf[:, n, i:i + 1],
                                      vals[:, n, i:i + 1], ALU.is_equal, ALU.mult).then_inc(s_at, 1)
                dve.wait_ge(s_tab, 2 * TB)
                L(dve.tensor_copy(tab[:, :], table[:, :]))
                L(dve.tensor_scalar(second[:, :], tab[:, :], S + 0.5, float(-S), ALU.is_gt, ALU.mult))
                L(dve.scalar_tensor_tensor(out=second[:, :], in0=tab[:, :], scalar=-1.0, in1=second[:, :], op0=ALU.add, op1=ALU.add))
                L(dve.tensor_scalar(t.ids[:, :], second[:, :], 0.0, None, ALU.max))
                L(dve.tensor_scalar(unused[:, :], tab[:, :], 0.5, None, ALU.is_lt))
                L(dve.tensor_scalar(unused[:, :], unused[:, :], t.consts[:, C_TRASH:C_TRASH + 1], None, ALU.mult))
                L(dve.scalar_tensor_tensor(out=t.rows[:, :], in0=tab[:, :], scalar=-1.0, in1=unused[:, :], op0=ALU.add, op1=ALU.add))

            @block.scalar
            def _(act):
                act.wait_ge(s_v, READY_G[0])
                act.activation(gexp[:, :, :], gexp[:, :, :], ACT.Exp).then_inc(s_a, 1)
                act.wait_ge(s_v, READY_E[0])
                act.activation(egap[:, :], gap[:, :], ACT.Exp).then_inc(s_a, 1)

            @block.tensor
            def _(pe):
                pe.wait_ge(s_v, READY_B[0])
                flat = both[:, :, :].rearrange("p t e -> p (t e)")
                pe.matmul(prefix[:, :], t.before_bf[:, :], flat, start=True, stop=True).then_inc(s_cnt, 1)
                pe.matmul(totals[:, :], t.ones_bf[:, :], flat, start=True, stop=True).then_inc(s_cnt, 1)
                for q in range(2 * TB):
                    pe.wait_ge(s_at, 2 * q + 2)
                    pe.matmul(table[:, :], at_p[q % 2][:, :], at_b[q % 2][:, :], start=(q == 0), stop=(q == 2 * TB - 1)).then_inc(s_tab, 1)


def experts(nc, a, t):
    with ExitStack() as ctx:
        p = Names(nc, ctx, "ex_")
        ids = p.sb("ids_now", [P, 1], U32)
        rows = p.sb("rows_now", [P, 1], U32)
        xg = p.sb("xg", [P, D])
        xT = p.sb("xT", [P, KT, P])
        gate = p.sb("gate", [P, F])
        hid = p.sb("hid", [P, F])
        hidT = p.sb("hidT", [P, FT, P])
        y = p.sb("y", [P, D])
        xtp = [p.ps(f"ext{i}", [P, BANK]) for i in range(2)]
        gp = p.ps("gp", [P, F])
        up = p.ps("up", [P, F])
        hp = p.ps("hp", [P, F])
        yp = [p.ps(f"yp{i}", [P, BANK]) for i in range(2)]
        names = ("hold ids_ready rows_ready gathered x_turned x_copied gate_product up_product gate_activated hidden hidden_turned "
                 "hidden_copied down_product y_copied_a y_copied_v y_stored").split()
        s = {n: p.sem("e_" + n) for n in names}
        reader = {"w_gate": "gate_product", "w_up": "up_product", "w_down": "down_product"}

        def total_blocks(eng):
            return eng.value_load(t.cum_blocks[0:1, EXPERTS:EXPERTS + 1], min_val=EXPERTS, max_val=MAX_BLOCKS)

        def last_block(eng):
            return eng.value_load(t.cum_blocks[0:1, EXPERTS + 1:EXPERTS + 2], min_val=0, max_val=MAX_BLOCKS)

        with nc.Block() as block:

            @block.sync
            def _(sp):
                with sp.Fori(1, EXPERTS // 2) as pair:
                    for b in range(2):
                        e = pair * 2 + b
                        prev = sp.value_load(t.cum_prev[0:1, bass.ds(e, 1)], min_val=0, max_val=MAX_BLOCKS)
                        load_expert(sp, a, t, e, b, lambda name: sp.wait_ge(s[reader[name]], prev))

            @block.gpsimd
            def _(pool):
                def fetch(g):
                    pool.wait_ge(s["x_turned"], 2 * g)
                    pool.tensor_copy(ids[:, :], t.ids[:, bass.ds(g, 1)]).then_inc(s["ids_ready"], 1)
                    pool.wait_ge(s["ids_ready"], g + 1)
                    pool.sem_inc(s["hold"], 1)
                    pool.indirect_dma_start(out=xg[:, :], out_offset=None, in_=t.h2,
                                            in_offset=bass.IndirectOffsetOnAxis(ap=ids[:, 0:1], axis=0)).then_inc(s["gathered"], 16)

                fetch(0)
                fetch(1)
                total = total_blocks(pool)
                with pool.Fori(0, total) as g:
                    fetch(g + 2)
                    pool.wait_ge(s["y_stored"], 16 * g)
                    pool.tensor_copy(rows[:, :], t.rows[:, bass.ds(g, 1)]).then_inc(s["rows_ready"], 1)
                    pool.wait_ge(s["rows_ready"], g + 1)
                    pool.wait_ge(s["y_copied_a"], g + 1)
                    pool.wait_ge(s["y_copied_v"], g + 1)
                    pool.sem_inc(s["hold"], 1)
                    pool.indirect_dma_start(out=t.y, out_offset=bass.IndirectOffsetOnAxis(ap=rows[:, 0:1], axis=0),
                                            in_=y[:, :], in_offset=None).then_inc(s["y_stored"], 16)
                pool.wait_ge(s["gathered"], total * 16 + 32)
                pool.wait_ge(s["y_stored"], total * 16)
                pool.sem_inc(s["hold"], 1)
                pool.tensor_copy(ids[:, :], t.ids[:, 0:1]).then_inc(s["ids_ready"], 1)

            @block.tensor
            def _(pe):
                def slot_of(g):
                    return pe.value_load(t.slot[0:1, bass.ds(g, 1)], min_val=0, max_val=1)

                def weight(slot, at, cols, k, lo, n):
                    return t.weights[:, bass.ds(slot, 1), at + k * cols + lo:at + k * cols + lo + n].rearrange("p a n -> p (a n)")

                def turn(g):
                    pe.wait_ge(s["gathered"], 16 * g + 16)
                    pe.wait_ge(s["x_copied"], 2 * g)
                    for h in range(2):
                        for j in range(TPB):
                            mm = pe.transpose(xtp[h][:, j * P:(j + 1) * P], xg[:, (h * TPB + j) * P:(h * TPB + j + 1) * P], t.ident)
                        mm.then_inc(s["x_turned"], 1)

                def loads_for(g):
                    return [pe.value_load(t.loads[0:1, b, bass.ds(g, 1)], min_val=0, max_val=16 * (EXPERTS // 2 + 1))
                            for b in range(2)]

                def loaded(name, loads):
                    for b in range(2):
                        pe.wait_ge(t.s_w[name][b], loads[b])

                def gate_product(g, slot, loads):
                    loaded("w_gate", loads)
                    pe.wait_ge(s["x_copied"], 2 * g + 2)
                    pe.wait_ge(s["gate_activated"], g)
                    for k in range(KT):
                        mm = pe.matmul(gp[:, :], xT[:, k, :], weight(slot, W_GATE, F, k, 0, F), start=(k == 0), stop=(k == KT - 1))
                    mm.then_inc(s["gate_product"], 1)

                def up_product(g, slot, loads):
                    loaded("w_up", loads)
                    pe.wait_ge(s["hidden"], g)
                    for k in range(KT):
                        mm = pe.matmul(up[:, :], xT[:, k, :], weight(slot, W_UP, F, k, 0, F), start=(k == 0), stop=(k == KT - 1))
                    mm.then_inc(s["up_product"], 1)

                def turn_hidden(g):
                    pe.wait_ge(s["hidden"], g + 1)
                    pe.wait_ge(s["hidden_copied"], g)
                    for k in range(FT):
                        mm = pe.transpose(hp[:, k * P:(k + 1) * P], hid[:, k * P:(k + 1) * P], t.ident)
                    mm.then_inc(s["hidden_turned"], 1)

                def down_product(g, slot, loads):
                    loaded("w_down", loads)
                    pe.wait_ge(s["hidden_copied"], g + 1)
                    pe.wait_ge(s["y_copied_a"], g)
                    pe.wait_ge(s["y_copied_v"], g)
                    for h in range(2):
                        for k in range(FT):
                            mm = pe.matmul(yp[h][:, :], hidT[:, k, :], weight(slot, W_DOWN, D, k, h * BANK, BANK),
                                           start=(k == 0), stop=(k == FT - 1))
                    mm.then_inc(s["down_product"], 1)

                turn(0)
                first = slot_of(0)
                loads = loads_for(0)
                gate_product(0, first, loads)
                up_product(0, first, loads)
                turn(1)
                total = total_blocks(pe)
                with pe.Fori(1, total) as g:
                    slot = slot_of(g)
                    last = slot_of(g - 1)
                    loads = loads_for(g)
                    last_loads = loads_for(g - 1)
                    gate_product(g, slot, loads)
                    turn_hidden(g - 1)
                    up_product(g, slot, loads)
                    turn(g + 1)
                    down_product(g - 1, last, last_loads)
                end = last_block(pe)
                last = slot_of(end)
                last_loads = loads_for(end)
                turn_hidden(end)
                down_product(end, last, last_loads)

            @block.scalar
            def _(act):
                def copy_x(g):
                    for h in range(2):
                        act.wait_ge(s["x_turned"], 2 * g + h + 1)
                        act.wait_ge(s["up_product"], g)
                        act.activation(xT[:, h * TPB:(h + 1) * TPB, :], xtp[h][:, :].rearrange("p (b n) -> p b n", n=P),
                                       ACT.Copy).then_inc(s["x_copied"], 1)

                def activate(g):
                    act.wait_ge(s["gate_product"], g + 1)
                    act.wait_ge(s["hidden"], g)
                    act.activation(gate[:, :], gp[:, :], ACT.Silu).then_inc(s["gate_activated"], 1)

                def copy_y(g):
                    act.wait_ge(s["down_product"], g + 1)
                    act.wait_ge(s["y_stored"], 16 * g)
                    act.activation(y[:, 0:BANK], yp[0][:, :], ACT.Copy).then_inc(s["y_copied_a"], 1)

                copy_x(0)
                activate(0)
                copy_x(1)
                total = total_blocks(act)
                with act.Fori(1, total) as g:
                    activate(g)
                    copy_x(g + 1)
                    copy_y(g - 1)
                copy_y(last_block(act))

            @block.vector
            def _(dve):
                def multiply(g):
                    dve.wait_ge(s["gate_activated"], g + 1)
                    dve.wait_ge(s["up_product"], g + 1)
                    dve.wait_ge(s["hidden_turned"], g)
                    dve.tensor_tensor(hid[:, :], gate[:, :], up[:, :], ALU.mult).then_inc(s["hidden"], 1)

                def copy_hidden(g):
                    dve.wait_ge(s["hidden_turned"], g + 1)
                    dve.wait_ge(s["down_product"], g)
                    dve.tensor_copy(hidT[:, :, :], hp[:, :].rearrange("p (b n) -> p b n", n=P)).then_inc(s["hidden_copied"], 1)

                def copy_y(g):
                    dve.wait_ge(s["down_product"], g + 1)
                    dve.wait_ge(s["y_stored"], 16 * g)
                    dve.tensor_copy(y[:, BANK:], yp[1][:, :]).then_inc(s["y_copied_v"], 1)

                multiply(0)
                total = total_blocks(dve)
                with dve.Fori(1, total) as g:
                    copy_hidden(g - 1)
                    multiply(g)
                    copy_y(g - 1)
                end = last_block(dve)
                copy_hidden(end)
                copy_y(end)


def combine(nc, a, t, out):
    with ExitStack() as ctx:
        p = Names(nc, ctx, "cb_")
        NB = 2
        y1 = [p.sb(f"y1_{i}", [P, D]) for i in range(NB)]
        y2 = [p.sb(f"y2_{i}", [P, D]) for i in range(NB)]
        res = [p.sb(f"res{i}", [P, D]) for i in range(NB)]
        junk = p.sb("junk3", [P, D])
        ss, sd, rr = (p.sb(n, [P, TB]) for n in ("ss3", "sd3", "rr3"))
        s_g1 = [p.sem(f"c_first_rows{i}") for i in range(NB)]
        s_g2 = [p.sem(f"c_second_rows{i}") for i in range(NB)]
        s_first, s_sum, s_sq, s_std, s_rec, s_scaled, s_out = (p.sem(n) for n in (
            "c_first_weighted", "c_summed", "c_squared", "c_std", "c_reciprocal", "c_scaled", "c_result"))
        s_store = [p.sem(f"c_stored{i}") for i in range(NB)]
        with nc.Block() as block:

            @block.gpsimd
            def _(pool):
                for i in range(TB):
                    b = i % NB
                    if i >= NB:
                        pool.wait_ge(s_sum, i - NB + 1)
                    pool.dma_start(y1[b][:, :], t.y[i * P:(i + 1) * P, :]).then_inc(s_g1[b], 16)
                    pool.dma_start(y2[b][:, :], t.y[S + i * P:S + (i + 1) * P, :]).then_inc(s_g2[b], 16)

            @block.scalar
            def _(act):
                for i in range(TB):
                    b = i % NB
                    act.wait_ge(s_g1[b], 16 * (i // NB + 1))
                    act.activation(y1[b][:, :], y1[b][:, :], ACT.Copy, scale=t.weight[:, 0, i:i + 1]).then_inc(s_first, 1)
                    act.wait_ge(s_sum, i + 1)
                    if i:
                        act.wait_ge(s_sq, i)
                    act.activation(junk[:, :], res[b][:, :], ACT.Square, accum_out=ss[:, i:i + 1]).then_inc(s_sq, 1)
                    act.wait_ge(s_sq, i + 1)
                    act.activation(sd[:, i:i + 1], ss[:, i:i + 1], ACT.Sqrt, scale=1.0 / D, bias=t.eps[:, :]).then_inc(s_std, 1)

            @block.vector
            def _(dve):
                for i in range(TB):
                    b = i % NB
                    dve.wait_ge(s_first, i + 1)
                    dve.wait_ge(s_g2[b], 16 * (i // NB + 1))
                    if i >= NB:
                        dve.wait_ge(s_store[b], 16 * (i // NB))
                    dve.scalar_tensor_tensor(out=res[b][:, :], in0=y2[b][:, :], scalar=t.weight[:, 1, i:i + 1], in1=y1[b][:, :],
                                             op0=ALU.mult, op1=ALU.add).then_inc(s_sum, 1)
                    dve.wait_ge(s_std, i + 1)
                    dve.reciprocal(rr[:, i:i + 1], sd[:, i:i + 1]).then_inc(s_rec, 1)
                    dve.wait_ge(s_rec, i + 1)
                    dve.scalar_tensor_tensor(out=res[b][:, :], in0=res[b][:, :], scalar=rr[:, i:i + 1], in1=t.gate_ffn[:, :],
                                             op0=ALU.mult, op1=ALU.mult).then_inc(s_scaled, 1)
                    dve.wait_ge(s_scaled, i + 1)
                    dve.tensor_tensor(res[b][:, :], res[b][:, :], t.x1[:, i, :], ALU.add).then_inc(s_out, 1)

            @block.sync
            def _(sp):
                for i in range(TB):
                    sp.wait_ge(s_out, i + 1)
                    sp.dma_start(out[0, i * P:(i + 1) * P, :], res[i % NB][:, :]).then_inc(s_store[i % NB], 16)
                for b in range(NB):
                    sp.wait_ge(s_store[b], 16 * (TB // NB))


def kernel_program(nc, a, out):
    with ExitStack() as ctx:
        p = Names(nc, ctx)

        class T:
            pass
        t = T()
        t.consts = p.sb("consts_sb", [P, C_END])
        t.ident = t.consts[:, C_IDENT:C_IDENT + P]
        t.rot = t.consts[:, C_ROT:C_ROT + P]
        t.ident_bf = p.sb("ident_bf", [P, P], BF16)
        t.before_bf = p.sb("before_bf", [P, P], BF16)
        t.ones_bf = p.sb("ones_bf", [P, P], BF16)
        t.mask = {k: p.sb(f"mask_{k}", [P, P], BF16) for k in ("diff", "fox")}
        t.eps = p.sb("eps", [P, 1])
        t.subln = p.sb("subln", [P, 1])
        t.bforget = p.sb("bforget", [FOX_HEADS, 1])
        t.neg_lambda = p.sb("neg_lambda", [P, 1])
        t.attn_gain = p.sb("attn_gain", [P, KT])
        t.attn_shift = p.sb("attn_shift", [P, KT])
        t.gate_attn = p.sb("gate_attn", [P, D])
        t.ffn_gain = p.sb("ffn_gain", [P, D])
        t.ffn_shift = p.sb("ffn_shift", [P, D])
        t.gate_ffn = p.sb("gate_ffn", [P, D])
        t.logits = p.sb("logits", [P, TB, LOGITS])
        t.weight = p.sb("weight", [P, 2, TB])
        t.cum_blocks = p.sb("cum_blocks", [P, EXPERTS + 2], I32)
        t.cum_prev = p.sb("cum_prev", [P, EXPERTS], I32)
        t.slot = p.sb("slot", [P, TABLE], I32)
        t.loads = p.sb("loads", [P, 2, TABLE], I32)
        t.ids = p.sb("ids", [P, TABLE], U32)
        t.rows = p.sb("rows", [P, TABLE], U32)
        t.mixed = nc.dram_tensor("mixed_d", (S, D), F32, kind="Internal").ap()
        t.neg_f = nc.dram_tensor("neg_f_d", (FOX_HEADS, S), F32, kind="Internal").ap()
        t.h2 = nc.dram_tensor("h2_d", (S, D), F32, kind="Internal").ap()
        t.y = nc.dram_tensor("y_d", (2 * S + P, D), F32, kind="Internal").ap()
        big = p.sb("big", [P, KT * S])
        t.hT = big[:, :].rearrange("p (k s) -> p k s", k=KT)
        t.x1 = big[:, :].rearrange("p (t d) -> p t d", t=TB)
        modulate(nc, a, t)
        forget(nc, a, t)
        attend(nc, a, t, "diff")
        attend(nc, a, t, "fox")
        with ExitStack() as inner:
            q = Names(nc, inner, "ex_")
            t.weights = q.sb("weights", [P, 2, EXPERT_WORDS])
            t.s_w = {n: [q.sem(f"{n}_loaded{i}") for i in range(2)] for n in ("w_gate", "w_up", "w_down")}
            merge(nc, a, t)
            route(nc, a, t)
            experts(nc, a, t)
        combine(nc, a, t, out)


_INS = ["x", "c", "w_ada", "b_ada", "g_pre_attn", "g_post_attn", "w_in", "b_forget", "lambda_q1", "lambda_k1",
        "lambda_q2", "lambda_k2", "g_diff_subln", "w_out", "g_pre_ffn", "g_post_ffn", "w_group", "b_group",
        "w_router", "b_router", "w_gate", "w_up", "w_down"]


def _constants():
    import numpy as np
    inv = (1.0 / (10000.0 ** (np.arange(0, HD, 2, dtype=np.float32) / np.float32(HD)))).astype(np.float32)
    ang = (np.arange(S, dtype=np.float32)[:, None] * inv[None, :]).astype(np.float32)
    reps = (P // (HD // 2), 1)
    cos = np.ascontiguousarray(np.tile(np.cos(ang).astype(np.float32).T, reps))
    sin = np.ascontiguousarray(np.tile(np.sin(ang).astype(np.float32).T, reps))
    k = np.zeros((P, C_END), np.float32)
    at = np.arange(P)
    k[:, C_IDENT:C_IDENT + P] = np.eye(P)
    for m in range(P):
        first = m % HD < HD // 2
        k[m + HD // 2 if first else m - HD // 2, C_ROT + m] = -1.0 if first else 1.0
    k[:, C_BEFORE:C_BEFORE + P] = at[:, None] < at[None, :]
    k[:, C_MASKD:C_MASKD + P] = -1e30 * (at[None, :] // 64 > at[:, None] // 64)
    k[:, C_MASKF:C_MASKF + P] = -1e30 * (at[None, :] > at[:, None])
    k[:, C_IOTA:C_IOTA + P] = at[None, :]
    k[:, C_GDESC:C_GDESC + GROUPS] = np.arange(GROUPS, 0, -1)
    k[:, C_EDESC:C_EDESC + PER_GROUP] = np.arange(PER_GROUP, 0, -1)
    k[:, C_TOKEN:C_TOKEN + TB] = np.arange(TB)[None, :] * P + at[:, None]
    k[:, C_TRASH] = 2 * S + 1 + at
    return {"consts": k, "rope_cos": cos, "rope_sin": sin}


def kernel(**inputs):
    import numpy as np
    import concourse.bacc as bacc
    from concourse.bass_utils import run_bass_kernel_spmd

    nc = bacc.Bacc("TRN2", target_bir_lowering=False, num_devices=1)
    arrays, args = {}, {}
    for name, x in {**{n: inputs[n] for n in _INS}, **_constants()}.items():
        x = np.ascontiguousarray(x)
        arrays[f"in_{name}"] = x
        args[name] = nc.dram_tensor(f"in_{name}", x.shape, mybir.dt.from_np(x.dtype), kind="ExternalInput").ap()
    out = nc.dram_tensor("out_0", (1, S, D), F32, kind="ExternalOutput").ap()
    kernel_program(nc, args, out)
    r = run_bass_kernel_spmd(nc, [arrays], core_ids=[0])
    return r.results[0]["out_0"]
```

```python
from contextlib import ExitStack

import concourse.bass as bass
from concourse import mybir

P = 128
D = 1024
KT = D // P
S = 2048
TB = S // P
HD = 64
UNITS = 4
GROUPS = 4
PER_GROUP = 8
EXPERTS = GROUPS * PER_GROUP
LOGITS = GROUPS + EXPERTS
F = D // 2
FT = F // P
BANK = 512
CH = S // BANK
TPB = BANK // P
MAX_BLOCKS = 2 * S // P + EXPERTS
TABLE = MAX_BLOCKS + 2
EPS = 1e-6
LAMBDA_INIT = 0.2
QK_SCALE = HD ** -0.5
BIG = 3.0e38
MASKED = 1.0e30
COL = {"diff": (0, 512, 1024), "fox": (1536, 2048, 2560), "forget": 3072}
FOX_HEADS = 8
C_IDENT, C_ROT, C_BEFORE, C_MASKD, C_MASKF, C_IOTA, C_GDESC, C_EDESC, C_TOKEN, C_TRASH, C_END = (
    0, 128, 256, 384, 512, 640, 768, 772, 780, 796, 797)

ALU = mybir.AluOpType
ACT = mybir.ActivationFunctionType
F32 = mybir.dt.float32
F32R = mybir.dt.float32r
BF16 = mybir.dt.bfloat16
I32 = mybir.dt.int32
U32 = mybir.dt.uint32
X = mybir.AxisListType.X


W_GATE, W_UP, W_DOWN, EXPERT_WORDS = 0, KT * F, 2 * KT * F, 2 * KT * F + FT * D


ROWS = ("gate_attn", "ffn_gain", "ffn_shift", "gate_ffn")


class Steps:

    def __init__(self, eng, sem):
        self.eng, self.sem, self.n, self.base = eng, sem, 0, 0

    def link(self, ins):
        ins.then_inc(self.sem, 1)
        self.n += 1
        self.eng.wait_ge(self.sem, self.base + self.n)


class Names:

    def __init__(self, nc, ctx, prefix=""):
        self.nc, self.ctx, self.prefix = nc, ctx, prefix

    def sb(self, name, shape, dt=F32):
        return self.ctx.enter_context(self.nc.sbuf_tensor(self.prefix + name, shape, dt))

    def ps(self, name, shape, dt=F32):
        return self.ctx.enter_context(self.nc.psum_tensor(self.prefix + name, shape, dt))

    def sem(self, name):
        return self.ctx.enter_context(self.nc.semaphore(self.prefix + name))


def modulate(nc, a, t):
    with ExitStack() as ctx:
        p = Names(nc, ctx, "mod_")
        NP = 6 * D // BANK
        RING = 2
        w_ada = [p.sb(f"w_ada{i}", [P, KT, BANK]) for i in range(RING)]
        b_ada = [p.sb(f"b_ada{i}", [P, BANK]) for i in range(RING)]
        xs = p.sb("xs", [P, TB, D])
        ccol = p.sb("ccol", [P, KT])
        cact = p.sb("cact", [P, KT])
        cwide = p.sb("cwide", [P, KT, P])
        gcol = p.sb("gcol", [P, KT])
        tmprow = p.sb("tmprow", [P, D])
        summed = p.sb("summed", [P, 2, BANK])
        ssq = p.sb("ssq", [P, TB])
        std = p.sb("std", [P, TB])
        rstd = p.sb("rstd", [P, TB])
        lamrow = p.sb("lamrow", [1, 4, HD])
        lamprod = p.sb("lamprod", [1, 2, HD])
        lamsum = p.sb("lamsum", [1, 2])
        lamexp = p.sb("lamexp", [1, 2])
        lamone = p.sb("lamone", [1, 1])
        onerow = p.sb("onerow", [1, P])
        junk = p.sb("junk", [P, D])
        modp = [p.ps(f"modp{i}", [P, BANK]) for i in range(2)]
        colp = p.ps("colp", [P, 2, P])
        lamp = p.ps("lamp", [P, 1])
        xtp = [p.ps(f"xtp{i}", [P, BANK]) for i in range(4)]
        s_small = p.sem("small_loaded")
        s_w = [p.sem(f"w_ada_loaded{i}") for i in range(RING)]
        s_x = [p.sem(f"x_loaded{i}") for i in range(4)]
        s_cact = p.sem("c_activated")
        s_cwide = p.sem("c_widened")
        s_mod = p.sem("mod_product")
        s_sum = p.sem("mod_summed")
        s_modrow = p.sem("mod_row_done")
        s_tr = p.sem("mod_transposed")
        s_col = p.sem("mod_column_done")
        s_sq = p.sem("x_squared")
        s_std = p.sem("std_done")
        s_xn = p.sem("x_normalised")
        s_xt = p.sem("x_transposed")
        s_hta = p.sem("hT_by_act")
        s_htv = p.sem("hT_by_dve")
        s_lam = p.sem("lambda_steps")
        s_lamexp = p.sem("lambda_exponentials")
        s_lamb = p.sem("lambda_broadcast")
        s_const = p.sem("constants_made")
        s_dve = p.sem("dve_steps")
        mod_of = {0: "sh_a", 1: "sc_a", 2: "gt_a", 3: "sh_f", 4: "sc_f", 5: "gt_f"}
        row = {name: p.sb(name, [P, D]) for name in ROWS}
        rows = {"sh_a": tmprow, "sc_a": tmprow, "gt_a": row["gate_attn"], "sh_f": row["ffn_shift"],
                "sc_f": row["ffn_gain"], "gt_f": row["gate_ffn"]}
        s_rows = p.sem("rows_stored")
        NSMALL = 12

        with nc.Block() as block:

            @block.sync
            def _(sp):
                sp.dma_start(t.consts[:, :], a["consts"]).then_inc(s_small, 16)
                sp.dma_start(ccol[:, :], a["c"].rearrange("a (k p) -> p (a k)", p=P),
                             allow_slow_non_contiguous=True).then_inc(s_small, 16)
                sp.dma_start(gcol[:, :], a["g_pre_attn"].rearrange("a (k p) -> p (a k)", p=P),
                             allow_slow_non_contiguous=True).then_inc(s_small, 16)
                sp.dma_start(t.subln[:, :], a["g_diff_subln"].rearrange("a p -> p a"),
                             allow_slow_non_contiguous=True).then_inc(s_small, 16)
                for dst, name in ((row["gate_attn"], "g_post_attn"), (row["ffn_gain"], "g_pre_ffn"),
                                  (row["gate_ffn"], "g_post_ffn")):
                    sp.dma_start(dst[:, :], a[name].to_broadcast([P, D])).then_inc(s_small, 16)
                for i, name in enumerate(("lambda_q1", "lambda_q2", "lambda_k1", "lambda_k2")):
                    sp.dma_start(lamrow[:, i, :], a[name]).then_inc(s_small, 16)
                sp.dma_start(t.bforget[:, :], a["b_forget"].rearrange("a h -> h a"),
                             allow_slow_non_contiguous=True).then_inc(s_small, 16)
                for n in range(NP):
                    if n >= RING:
                        sp.wait_ge(s_mod, n - RING + 1)
                        sp.wait_ge(s_sum, n - RING + 1)
                    cols = slice(n * BANK, (n + 1) * BANK)
                    sp.dma_start(w_ada[n % RING][:, :, :],
                                 a["w_ada"][0, :, cols].rearrange("(k p) n -> p k n", p=P)).then_inc(s_w[n % RING], 16)
                    sp.dma_start(b_ada[n % RING][:, :],
                                 a["b_ada"][:, cols].to_broadcast([P, BANK])).then_inc(s_w[n % RING], 16)
                sp.wait_ge(s_modrow, NP)
                for i, name in enumerate(ROWS):
                    sp.dma_start(t.row_dram[i:i + 1, :], row[name][0:1, :]).then_inc(s_rows, 16)
                sp.wait_ge(s_rows, 16 * len(ROWS))

            @block.scalar
            def _(act):
                for i in range(4):
                    act.dma_start(xs[:, 4 * i:4 * i + 4, :],
                                  a["x"][0].rearrange("(t p) d -> p t d", p=P)[:, 4 * i:4 * i + 4, :]).then_inc(s_x[i], 16)
                act.wait_ge(s_small, 16 * NSMALL)
                act.activation(cact[:, :], ccol[:, :], ACT.Silu).then_inc(s_cact, 1)
                act.wait_ge(s_lam, 2)
                act.activation(lamexp[:, :], lamsum[:, :], ACT.Exp).then_inc(s_lamexp, 1)
                for i in range(TB):
                    if i % 4 == 0:
                        act.wait_ge(s_x[i // 4], 16)
                    if i:
                        act.wait_ge(s_sq, i)
                    act.activation(junk[:, :], xs[:, i, :], ACT.Square, accum_out=ssq[:, i:i + 1]).then_inc(s_sq, 1)
                act.wait_ge(s_sq, TB)
                act.wait_ge(s_const, 1)
                act.activation(std[:, :], ssq[:, :], ACT.Sqrt, scale=1.0 / D, bias=t.eps[:, :]).then_inc(s_std, 1)
                act.wait_ge(s_col, 16)
                for n in range(0, 4 * KT, 2):
                    tg, k = divmod(n, KT)
                    act.wait_ge(s_xt, n + 1)
                    act.activation(t.hT[:, k, tg * BANK:(tg + 1) * BANK], xtp[n % 4][:, :], ACT.Identity,
                                   scale=t.attn_gain[:, k:k + 1], bias=t.attn_shift[:, k:k + 1]).then_inc(s_hta, 1)

            @block.tensor
            def _(pe):
                pe.wait_ge(s_cwide, KT)
                for n in range(NP):
                    pe.wait_ge(s_w[n % RING], 32 * (n // RING + 1))
                    if n >= 2:
                        pe.wait_ge(s_sum, n - 1)
                    for k in range(KT):
                        mm = pe.matmul(modp[n % 2][:, :], cwide[:, k, :], w_ada[n % RING][:, k, :],
                                       start=(k == 0), stop=(k == KT - 1))
                    mm.then_inc(s_mod, 1)
                    if n < 4:
                        pe.wait_ge(s_modrow, n + 1)
                        for j in range(TPB):
                            m = n * TPB + j
                            if m >= 1:
                                pe.wait_ge(s_col, m)
                            pe.transpose(colp[:, 0, :], tmprow[:, (n % 2) * BANK + j * P:(n % 2) * BANK + (j + 1) * P],
                                         t.ident).then_inc(s_tr, 1)
                pe.wait_ge(s_lam, 4)
                pe.matmul(lamp[:, :], onerow[:, :], lamone[:, :], start=True, stop=True).then_inc(s_lamb, 1)
                for n in range(4 * KT):
                    tg, k = divmod(n, KT)
                    if k == 0:
                        pe.wait_ge(s_xn, 4 * tg + 4)
                    if n >= 4:
                        pe.wait_ge(s_hta if n % 2 == 0 else s_htv, (n - 4) // 2 + 1)
                    for j in range(4):
                        mm = pe.transpose(xtp[n % 4][:, j * P:(j + 1) * P], xs[:, 4 * tg + j, k * P:(k + 1) * P], t.ident)
                    mm.then_inc(s_xt, 1)

            @block.vector
            def _(dve):
                st = Steps(dve, s_dve)
                dve.memset(t.eps[:, :], EPS).then_inc(s_const, 1)
                st.link(dve.memset(cwide[:, :, :], 1.0))
                st.link(dve.memset(onerow[:, :], 1.0))
                dve.wait_ge(s_small, 16 * NSMALL)
                st.link(dve.tensor_copy(t.ident_bf[:, :], t.ident))
                st.link(dve.tensor_copy(t.mask["diff"][:, :], t.consts[:, C_MASKD:C_MASKD + P]))
                st.link(dve.tensor_copy(t.mask["fox"][:, :], t.consts[:, C_MASKF:C_MASKF + P]))
                st.link(dve.tensor_copy(t.before_bf[:, :], t.consts[:, C_BEFORE:C_BEFORE + P]))
                st.link(dve.memset(t.ones_bf[:, :], 1.0))
                st.link(dve.tensor_scalar(t.subln[:, :], t.subln[:, :], 1.0 - LAMBDA_INIT, None, ALU.mult))
                st.link(dve.tensor_tensor(lamprod[:, :, :], lamrow[:, 0:2, :], lamrow[:, 2:4, :], ALU.mult))
                dve.memset(lamsum[:, :], 0.0).then_inc(s_lam, 1)
                dve.wait_ge(s_lam, 1)
                dve.tensor_reduce(lamsum[:, :], lamprod[:, :, :], X, ALU.add).then_inc(s_lam, 1)
                dve.wait_ge(s_lamexp, 1)
                dve.tensor_tensor(lamone[:, :], lamexp[:, 1:2], lamexp[:, 0:1], ALU.subtract).then_inc(s_lam, 1)
                dve.wait_ge(s_lam, 3)
                dve.tensor_scalar(lamone[:, :], lamone[:, :], -LAMBDA_INIT, None, ALU.add).then_inc(s_lam, 1)
                dve.wait_ge(s_cact, 1)
                for k in range(KT):
                    dve.tensor_scalar(cwide[:, k, :], cwide[:, k, :], cact[:, k:k + 1], None, ALU.mult).then_inc(s_cwide, 1)
                for n in range(NP):
                    what = mod_of[n // 2]
                    half = slice((n % 2) * BANK, (n % 2 + 1) * BANK)
                    dve.wait_ge(s_mod, n + 1)
                    if n >= 2:
                        dve.wait_ge(s_modrow, n - 1)
                    dve.tensor_tensor(summed[:, n % 2, :], modp[n % 2][:, :], b_ada[n % RING][:, :], ALU.add).then_inc(s_sum, 1)
                    dve.wait_ge(s_sum, n + 1)
                    dst = rows[what][:, half]
                    if what in ("sh_a", "sh_f"):
                        ins = dve.tensor_copy(dst, summed[:, n % 2, :])
                    elif what == "sc_a":
                        ins = dve.tensor_scalar(dst, summed[:, n % 2, :], 1.0, None, ALU.add)
                    elif what == "sc_f":
                        ins = dve.scalar_tensor_tensor(out=dst, in0=summed[:, n % 2, :], scalar=1.0, in1=dst,
                                                       op0=ALU.add, op1=ALU.mult)
                    else:
                        ins = dve.tensor_tensor(dst, summed[:, n % 2, :], dst, ALU.mult)
                    ins.then_inc(s_modrow, 1)
                    if n < 4:
                        for j in range(TPB):
                            m = n * TPB + j
                            k = m % KT
                            dve.wait_ge(s_tr, m + 1)
                            if n < 2:
                                ins = dve.tensor_copy(t.attn_shift[:, k:k + 1], colp[:, 0, 0:1])
                            else:
                                ins = dve.tensor_tensor(t.attn_gain[:, k:k + 1], colp[:, 0, 0:1], gcol[:, k:k + 1], ALU.mult)
                            ins.then_inc(s_col, 1)
                    if n == 3:
                        dve.wait_ge(s_std, 1)
                        st.link(dve.reciprocal(rstd[:, :], std[:, :]))
                        for i in range(TB):
                            dve.tensor_scalar(xs[:, i, :], xs[:, i, :], rstd[:, i:i + 1], None, ALU.mult).then_inc(s_xn, 1)
                dve.wait_ge(s_lamb, 1)
                st.link(dve.tensor_copy(t.neg_lambda[:, :], lamp[:, :]))
                dve.wait_ge(s_col, 4 * TPB)
                for n in range(1, 4 * KT, 2):
                    tg, k = divmod(n, KT)
                    dve.wait_ge(s_xt, n + 1)
                    dve.tensor_scalar(t.hT[:, k, tg * BANK:(tg + 1) * BANK], xtp[n % 4][:, :],
                                      t.attn_gain[:, k:k + 1], t.attn_shift[:, k:k + 1], ALU.mult, ALU.add).then_inc(s_htv, 1)


def split(nc, a, t):
    with ExitStack() as ctx:
        p = Names(nc, ctx, "spl_")
        s_hi, s_lo = p.sem("hT_hi"), p.sem("hT_lo")
        with nc.Block() as block:

            @block.scalar
            def _(act):
                for k in range(KT):
                    act.activation(t.h_hi[:, k, :], t.hT[:, k, :], ACT.Copy).then_inc(s_hi, 1)

            @block.vector
            def _(dve):
                for k in range(KT):
                    dve.wait_ge(s_hi, k + 1)
                    dve.tensor_tensor(t.h_lo[:, k, :], t.hT[:, k, :], t.h_hi[:, k, :].bitcast(F32), ALU.subtract).then_inc(s_lo, 1)


def project(nc, a, t):
    with ExitStack() as ctx:
        p = Names(nc, ctx, "prj_")
        H = FOX_HEADS
        h_hi, h_lo = t.h_hi, t.h_lo
        w_raw = p.sb("w_raw", [P, KT, P])
        w_lo = [p.sb(f"w_lo{i}", [P, KT, P], F32R) for i in range(3)]
        w_hi = [p.sb(f"w_hi{i}", [P, KT, P], F32R) for i in range(3)]
        cos = p.sb("cos", [P, S])
        sin = p.sb("sin", [P, S])
        raw = [p.sb(f"raw{i}", [P, BANK]) for i in range(2)]
        rsin = [p.sb(f"rsin{i}", [P, BANK]) for i in range(2)]
        hi = [p.sb(f"hi{i}", [P, BANK], F32R) for i in range(2)]
        lo = [p.sb(f"lo{i}", [P, BANK], F32R) for i in range(2)]
        full = [p.sb(f"full{i}", [P, BANK]) for i in range(2)]
        z = [p.sb(f"z{i}", [H, BANK]) for i in range(2)]
        ez = [p.sb(f"ez{i}", [H, BANK]) for i in range(2)]
        ones = p.sb("scan_ones", [H, 1])
        acc = [p.ps(f"acc{i}", [P, BANK]) for i in range(4)]
        tp_ = [p.ps(f"tposed{i}", [P, BANK]) for i in range(2)]
        names = ("rope_loaded weights_loaded weights_hi weights_lo projected copied rotated sin_part cos_part roped "
                 "chunk_hi chunk_lo v_turned v_copied forget_loaded forget_hi forget_lo "
                 "forget_product forget_dve forget_act").split()
        s = {n: p.sem(n) for n in names}
        s_store = [p.sem(f"chunk_stored{i}") for i in range(2)]
        s_vstore = [p.sem(f"v_stored{i}") for i in range(2)]
        s_fstore = [p.sem(f"neg_f_stored{i}") for i in range(2)]
        NPROJ, NQK = 3 * CH, 2 * CH
        ALL = 2 * UNITS
        FSTEPS = 6

        def units(eng, body):
            for kind, base in (("diff", 0), ("fox", UNITS)):
                with eng.Fori(0, UNITS - 1) as u:
                    body(kind, u, u + base, (kind, u + 1))
                body(kind, UNITS - 1, UNITS - 1 + base, ("fox", 0) if kind == "diff" else None)

        def load_weights(eng, part, kind, u, U):
            eng.wait_ge(s["forget_lo"], 1)
            eng.wait_ge(s["weights_lo"], 3 * U + part)
            eng.dma_start(w_raw[:, :, :], a["w_in"][0, :, bass.ds(u * P + COL[kind][part], P)].rearrange("(k p) n -> p k n", p=P)
                          ).then_inc(s["weights_loaded"], 16)

        def wait_weights_free(eng, part, U):
            if part == 2:
                eng.wait_ge(s["forget_product"], CH)
                eng.wait_ge(s["projected"], U * NPROJ)
            else:
                eng.wait_ge(s["projected"], (U - 1) * NPROJ + (part + 1) * CH)

        def hi_lo_products(pe, bank, w, rhs_cols):
            for k in range(KT):
                for a_, b_ in ((w_hi[w], h_hi), (w_hi[w], h_lo), (w_lo[w], h_hi)):
                    mm = pe.matmul(bank, a_[:, k, :], b_[:, k, rhs_cols],
                                   start=(k == 0 and a_ is w_hi[w] and b_ is h_hi), stop=(k == KT - 1 and a_ is w_lo[w]))
            return mm

        with nc.Block() as block:

            @block.gpsimd
            def _(pool):
                for part in range(2):
                    load_weights(pool, part, "diff", 0, 0)
                pool.dma_start(cos[:, :], a["rope_cos"]).then_inc(s["rope_loaded"], 16)
                pool.dma_start(sin[:, :], a["rope_sin"]).then_inc(s["rope_loaded"], 16)

                def body(kind, u, U, after):
                    for n in range(NPROJ):
                        if n == 0:
                            load_weights(pool, 2, kind, u, U)
                        if n in (CH, 2 * CH) and after:
                            load_weights(pool, n // CH - 1, *after, U + 1)
                        if kind == "diff" and n < NQK:
                            c = slice((n % CH) * BANK, (n % CH + 1) * BANK)
                            if n == 0:
                                pool.wait_ge(s["rope_loaded"], 32)
                            pool.wait_ge(s["copied"], U * NPROJ + n + 1)
                            if n >= 2:
                                pool.wait_ge(s["chunk_lo"], U * NQK + n - 1)
                            else:
                                pool.wait_ge(s_vstore[n % 2], 16 * U * (CH // 2))
                            pool.tensor_tensor(full[n % 2][:, :], raw[n % 2][:, :], cos[:, c], ALU.mult).then_inc(s["cos_part"], 1)

                units(pool, body)

            @block.sync
            def _(sp):
                c = COL["forget"]
                sp.dma_start(w_raw[:, :, H:], a["zeros"].unsqueeze(1).to_broadcast([P, KT, P - H])).then_inc(s["forget_loaded"], 16)
                sp.dma_start(w_raw[:, :, 0:H], a["w_in"][0, :, c:c + H].rearrange("(k p) n -> p k n", p=P)).then_inc(s["forget_loaded"], 16)
                for c in range(CH):
                    sp.wait_ge(s["forget_dve"], 1 + FSTEPS * (c + 1))
                    sp.dma_start(t.neg_f[:, c * BANK:(c + 1) * BANK], z[c % 2][:, :]).then_inc(s_fstore[c % 2], 16)

                def body(kind, u, U, after):
                    for n in range(NQK):
                        part, c = divmod(n, CH)
                        cols = slice(c * BANK, (c + 1) * BANK)
                        sp.wait_ge(s["chunk_lo"], U * NQK + n + 1)
                        for dst, src in ((t.hi[kind][part], hi[n % 2][:, :].bitcast(F32)), (t.lo[kind][part], lo[n % 2][:, :].bitcast(F32))):
                            sp.dma_start(dst[bass.ds(u * P, P), cols], src).then_inc(s_store[n % 2], 16)
                    for c in range(CH):
                        sp.wait_ge(s["v_copied"], U * CH + c + 1)
                        sp.dma_start(t.v[kind][bass.ds(u * P, P), c * BANK:(c + 1) * BANK], full[c % 2][:, :]).then_inc(s_vstore[c % 2], 16)

                units(sp, body)
                for b in range(2):
                    sp.wait_ge(s_store[b], 32 * ALL * CH)
                    sp.wait_ge(s_vstore[b], 16 * ALL * CH // 2)
                    sp.wait_ge(s_fstore[b], 16 * CH // 2)

            @block.tensor
            def _(pe):
                pe.wait_ge(s["forget_lo"], 1)
                for c in range(CH):
                    hi_lo_products(pe, acc[c][:, :], 2, slice(c * BANK, (c + 1) * BANK)).then_inc(s["forget_product"], 1)

                def body(kind, u, U, after):
                    def rotate(n):
                        pe.wait_ge(s["copied"], U * NPROJ + n + 1)
                        if n < 2:
                            pe.wait_ge(s["v_copied"], U * CH)
                        else:
                            pe.wait_ge(s["sin_part"], U * NQK + n - 1)
                        pe.matmul(tp_[n % 2][:, :], t.rot, raw[n % 2][:, :], start=True, stop=True).then_inc(s["rotated"], 1)

                    def turn_v(c):
                        pe.wait_ge(s["copied"], U * NPROJ + NQK + c + 1)
                        if c >= 2:
                            pe.wait_ge(s["v_copied"], U * CH + c - 1)
                        else:
                            pe.wait_ge(s["sin_part"], (U + 1) * NQK if kind == "diff" else UNITS * NQK)
                            pe.wait_ge(s["v_copied"], U * CH)
                        for j in range(TPB):
                            mm = pe.transpose(tp_[c % 2][:, j * P:(j + 1) * P], raw[c % 2][:, j * P:(j + 1) * P], t.ident)
                        mm.then_inc(s["v_turned"], 1)

                    for n in range(NPROJ):
                        part, c = divmod(n, CH)
                        if c == 0:
                            pe.wait_ge(s["weights_lo"], 3 * U + part + 1)
                        if n == 0:
                            pe.wait_ge(s["forget_dve"], 2 + FSTEPS * (CH - 1))
                            pe.wait_ge(s["copied"], U * NPROJ)
                        if n >= 4:
                            pe.wait_ge(s["copied"], U * NPROJ + n - 3)
                        hi_lo_products(pe, acc[n % 4][:, :], part, slice(c * BANK, (c + 1) * BANK)).then_inc(s["projected"], 1)
                        if kind == "diff" and 1 <= n <= NQK:
                            rotate(n - 1)
                        if n > NQK:
                            turn_v(n - NQK - 1)
                    turn_v(CH - 1)

                units(pe, body)

            @block.scalar
            def _(act):
                def split_weights(part, U, free=True):
                    act.wait_ge(s["weights_loaded"], 16 * (3 * U + part + 1))
                    if free:
                        wait_weights_free(act, part, U)
                    act.activation(w_hi[part][:, :, :], w_raw[:, :, :], ACT.Copy).then_inc(s["weights_hi"], 1)

                act.wait_ge(s["forget_loaded"], 32)
                act.activation(w_hi[2][:, :, :], w_raw[:, :, :], ACT.Copy).then_inc(s["forget_hi"], 1)
                split_weights(0, 0, free=False)
                split_weights(1, 0, free=False)
                for c in range(CH):
                    act.wait_ge(s["forget_dve"], 1 + FSTEPS * c + 2)
                    act.activation(ez[c % 2][:, :], ez[c % 2][:, :], ACT.Exp).then_inc(s["forget_act"], 1)
                    act.wait_ge(s["forget_dve"], 1 + FSTEPS * c + 3)
                    act.activation(ez[c % 2][:, :], ez[c % 2][:, :], ACT.Ln).then_inc(s["forget_act"], 1)

                def body(kind, u, U, after):
                    for n in range(NPROJ):
                        act.wait_ge(s["projected"], U * NPROJ + n + 1)
                        scale = QK_SCALE if n < CH else 1.0
                        if kind == "diff" or n >= NQK:
                            if n < NQK:
                                if n < 2:
                                    act.wait_ge(s["v_turned"], U * CH)
                                else:
                                    act.wait_ge(s["rotated"], U * NQK + n - 1)
                                    act.wait_ge(s["cos_part"], U * NQK + n - 1)
                            elif n < NQK + 2:
                                done = (U + 1) * NQK if kind == "diff" else UNITS * NQK
                                act.wait_ge(s["rotated"], done)
                                act.wait_ge(s["cos_part"], done)
                                act.wait_ge(s["v_turned"], U * CH)
                            else:
                                act.wait_ge(s["v_turned"], U * CH + n - NQK - 1)
                            act.activation(raw[n % 2][:, :], acc[n % 4][:, :], ACT.Copy, scale=scale).then_inc(s["copied"], 1)
                        else:
                            act.wait_ge(s_store[n % 2], 32 * (U * CH + n // 2))
                            act.activation(hi[n % 2][:, :], acc[n % 4][:, :], ACT.Copy, scale=scale).then_inc(s["chunk_hi"], 1)
                            act.wait_ge(s["chunk_lo"], U * NQK + n + 1)
                            act.sem_inc(s["copied"], 1)
                        if kind == "diff" and 2 <= n < NQK + 2:
                            m = n - 2
                            act.wait_ge(s["roped"], U * NQK + m + 1)
                            act.wait_ge(s_store[m % 2], 32 * (U * CH + m // 2))
                            act.activation(hi[m % 2][:, :], full[m % 2][:, :], ACT.Copy).then_inc(s["chunk_hi"], 1)
                        if n == CH - 1:
                            split_weights(2, U)
                        elif n % CH == CH - 1 and after:
                            split_weights(n // CH - 1, U + 1)

                units(act, body)

            @block.vector
            def _(dve):
                f = s["forget_dve"]

                def split_weights(n_split, part):
                    dve.wait_ge(s["weights_hi"], n_split)
                    dve.tensor_tensor(w_lo[part][:, :, :], w_raw[:, :, :], w_hi[part][:, :, :].bitcast(F32), ALU.subtract
                                      ).then_inc(s["weights_lo"], 1)

                dve.memset(ones[:, :], 1.0).then_inc(f, 1)
                dve.wait_ge(s["forget_hi"], 1)
                dve.tensor_tensor(w_lo[2][:, :, :], w_raw[:, :, :], w_hi[2][:, :, :].bitcast(F32), ALU.subtract).then_inc(s["forget_lo"], 1)
                split_weights(1, 0)
                split_weights(2, 1)
                for c in range(CH):
                    zc, ec = z[c % 2][:, :], ez[c % 2][:, :]
                    base = 1 + FSTEPS * c
                    dve.wait_ge(s["forget_product"], c + 1)
                    if c >= 2:
                        dve.wait_ge(s_fstore[c % 2], 16)
                        dve.wait_ge(f, base)
                    dve.tensor_scalar(zc, acc[c][0:H, :], t.bforget[:, 0:1], None, ALU.add).then_inc(f, 1)
                    dve.wait_ge(f, base + 1)
                    dve.scalar_tensor_tensor(out=ec, in0=zc, scalar=-1.0, in1=zc, op0=ALU.mult, op1=ALU.min).then_inc(f, 1)
                    dve.wait_ge(s["forget_act"], 2 * c + 1)
                    dve.tensor_scalar(ec, ec, 1.0, None, ALU.add).then_inc(f, 1)
                    dve.tensor_scalar(zc, zc, 0.0, None, ALU.min).then_inc(f, 1)
                    dve.wait_ge(f, base + 4)
                    dve.wait_ge(s["forget_act"], 2 * c + 2)
                    dve.tensor_tensor(ec, ec, zc, ALU.subtract).then_inc(f, 1)
                    dve.wait_ge(f, base + 5)
                    start = z[(c - 1) % 2][:, BANK - 1:BANK] if c else 0.0
                    dve.tensor_tensor_scan(zc, ones[:, :].to_broadcast([H, BANK]), ec, start, ALU.mult, ALU.add).then_inc(f, 1)

                def body(kind, u, U, after):
                    def lo_part(n):
                        dve.wait_ge(s["chunk_hi"], U * NQK + n + 1)
                        dve.tensor_tensor(lo[n % 2][:, :], full[n % 2][:, :], hi[n % 2][:, :].bitcast(F32), ALU.subtract
                                          ).then_inc(s["chunk_lo"], 1)

                    for n in range(NPROJ):
                        c = n % CH
                        if kind == "diff" and n < NQK:
                            if n == 0:
                                dve.wait_ge(s["rope_loaded"], 32)
                            dve.wait_ge(s["rotated"], U * NQK + n + 1)
                            if n >= 2:
                                dve.wait_ge(s["roped"], U * NQK + n - 1)
                            else:
                                dve.wait_ge(s["roped"], U * NQK)
                            dve.tensor_tensor(rsin[n % 2][:, :], tp_[n % 2][:, :], sin[:, c * BANK:(c + 1) * BANK], ALU.mult
                                              ).then_inc(s["sin_part"], 1)
                            dve.wait_ge(s["sin_part"], U * NQK + n + 1)
                            dve.wait_ge(s["cos_part"], U * NQK + n + 1)
                            dve.tensor_tensor(full[n % 2][:, :], full[n % 2][:, :], rsin[n % 2][:, :], ALU.add).then_inc(s["roped"], 1)
                            if n:
                                lo_part(n - 1)
                            if n == NQK - 1:
                                lo_part(n)
                        elif n < NQK:
                            dve.wait_ge(s["chunk_hi"], U * NQK + n + 1)
                            dve.scalar_tensor_tensor(out=lo[n % 2][:, :], in0=acc[n % 4][:, :], scalar=QK_SCALE if n < CH else 1.0,
                                                     in1=hi[n % 2][:, :].bitcast(F32), op0=ALU.mult, op1=ALU.subtract
                                                     ).then_inc(s["chunk_lo"], 1)
                        else:
                            dve.wait_ge(s["v_turned"], U * CH + c + 1)
                            dve.wait_ge(s_vstore[c % 2], 16 * (U * (CH // 2) + c // 2))
                            if kind == "diff" and c < 2:
                                dve.wait_ge(s["chunk_lo"], (U + 1) * NQK)
                            dve.tensor_copy(full[c % 2][:, :], tp_[c % 2][:, :]).then_inc(s["v_copied"], 1)
                        if n == CH - 1:
                            split_weights(3 * U + 3, 2)
                        elif n % CH == CH - 1 and after:
                            split_weights(3 * U + 3 + n // CH, n // CH - 1)

                units(dve, body)


def attend(nc, a, t, kind):
    fox = kind == "fox"
    with ExitStack() as ctx:
        p = Names(nc, ctx, kind + "_")
        AHEAD = 2
        RING = AHEAD + 1
        q_hi, q_lo, k_both = ([[p.sb(f"{n}{b}{m}", [P, S], F32R) for m in range(2)] for b in range(2)]
                              for n in ("q_hi", "q_lo", "k_both"))
        v = [p.sb(f"v{b}", [P, TB, P]) for b in range(2)]
        prob = [p.sb(f"prob{i}", [P, S]) for i in range(2 * RING)]
        probT = [p.sb(f"probT{i}", [P, TB, P]) for i in range(2)]
        if fox:
            negf = [p.sb(f"negf{m}", [P, S]) for m in range(2)]
        else:
            rden = p.sb("rden", [P, 2, 2])
            ratio = p.sb("ratio", [P, 2])
        low = p.sb("low", [P, 2 * RING, CH])
        den = p.sb("den", [P, 2 * RING])
        rec = p.sb("rec", [P, 4])
        outs = [p.sb(f"outs{i}", [P, P]) for i in range(2)]
        sp_ = [p.ps(f"score{i}", [P, BANK]) for i in range(4)]
        tp_ = [p.ps(f"tposed{i}", [P, BANK]) for i in range(2)]
        op_ = [p.ps(f"value{i}", [P, P]) for i in range(2)]
        s_in = [p.sem(f"unit_loaded{i}") for i in range(2)]
        s_hold = p.sem("hold")
        s_negf = p.sem("neg_f_loaded")
        s_score = p.sem("scored")
        s_scopy = p.sem("score_copied")
        s_exp = p.sem("exponentials")
        s_comb = p.sem("combine_steps")
        s_tr = p.sem("transposed")
        s_tca = p.sem("transpose_copied_act")
        s_tcv = p.sem("transpose_copied_dve")
        s_val = p.sem("values_done")
        s_rec = p.sem("reciprocals")
        s_ocopy = p.sem("output_copied")
        s_store = [p.sem(f"output_stored{i}") for i in range(2)]

        def chunks(i):
            return i // TPB + 1
        def width(i, c):
            return min(BANK, (i + 1) * P - c * BANK)
        def ring(i, m):
            return (i % RING) * 2 + m
        jobs = [(i, m) for i in range(TB) for m in range(2)]
        first_chunk = {}
        n = 0
        for j in jobs:
            first_chunk[j] = n
            n += chunks(j[0])
        NSC = n
        tjobs = jobs if fox else [(i, 0) for i in range(TB)]
        first_group = {}
        n = 0
        for j in tjobs:
            first_group[j] = n
            n += chunks(j[0])
        NTG = n
        NTJ = len(tjobs)
        def by_dve(g):
            return fox and g % 2 == 1
        A_T = sum(not by_dve(g) for g in range(NTG))
        V_T = NTG - A_T
        def copies_before(g, dve):
            return sum(by_dve(x) == dve for x in range(g))
        PER_COMB = 3
        LOADS = 13

        def scores_of(i):
            return [("score", i, m, c) for m in range(2) for c in range(chunks(i))] if i < TB else []

        def order(i):
            groups = [(i, m, c) for m in range(2 if fox else 1) for c in range(chunks(i))]
            mine = [("turn", *groups[0])]
            for g, group in enumerate(groups):
                if g + 1 < len(groups):
                    mine.append(("turn", *groups[g + 1]))
                mine.append(("value", *group))
            ahead = scores_of(i + AHEAD)
            steps = []
            for x, step in enumerate(mine):
                steps.append(step)
                steps += ahead[len(ahead) * x // len(mine):len(ahead) * (x + 1) // len(mine)]
            return steps

        def units(eng, body):
            with eng.Fori(0, UNITS // 2) as pair:
                for b in range(2):
                    body(pair * 2 + b, b, pair)

        with nc.Block() as block:

            @block.gpsimd
            def _(pool):
                def load(u, b):
                    rows = lambda x, m: x[bass.ds(u * P + m * HD, HD), :]
                    for m in range(2):
                        for at in (slice(0, HD), slice(HD, P)):
                            pool.dma_start(q_hi[b][m][at, :].bitcast(F32), rows(t.hi[kind][0], m)).then_inc(s_in[b], 16)
                            pool.dma_start(q_lo[b][m][at, :].bitcast(F32), rows(t.lo[kind][0], m)).then_inc(s_in[b], 16)
                        pool.dma_start(k_both[b][m][0:HD, :].bitcast(F32), rows(t.hi[kind][1], m)).then_inc(s_in[b], 16)
                        pool.dma_start(k_both[b][m][HD:P, :].bitcast(F32), rows(t.lo[kind][1], m)).then_inc(s_in[b], 16)
                    pool.dma_start(v[b][:, :, :], t.v[kind][bass.ds(u * P, P), :].rearrange("p (b n) -> p b n", n=P)).then_inc(s_in[b], 16)

                def load_negf(u):
                    pool.wait_ge(s_scopy, u * NSC)
                    for m in range(2):
                        pool.dma_start(negf[m][:, :], t.neg_f[bass.ds(u * 2 + m, 1), :].to_broadcast([P, S])).then_inc(s_negf, 16)

                if fox:
                    load_negf(0)
                load(0, 0)
                load(1, 1)
                with pool.Fori(1, UNITS // 2) as pair:
                    if fox:
                        load_negf(pair * 2 - 1)
                    for b in range(2):
                        pool.wait_ge(s_val, (pair * 2 + b - 1) * NTJ)
                        load(pair * 2 + b, b)
                        if fox and b == 0:
                            load_negf(pair * 2)
                if fox:
                    load_negf(UNITS - 1)

            @block.sync
            def _(sp):
                def body(u, b, pair):
                    for i in range(TB):
                        sp.wait_ge(s_ocopy, u * NTJ + (2 * i + 2 if fox else i + 1))
                        c = 0 if not fox else UNITS * P
                        sp.dma_start(t.mixed[i * P:(i + 1) * P, bass.ds(u * P + c, P)], outs[i % 2][:, :]).then_inc(s_store[i % 2], 16)

                units(sp, body)
                for b in range(2):
                    sp.wait_ge(s_store[b], 16 * UNITS * TB // 2)

            @block.tensor
            def _(pe):
                def body(u, b, pair):
                    def score(i, m, c):
                        n = first_chunk[i, m] + c
                        if n == 0:
                            pe.wait_ge(s_in[b], (pair + 1) * (16 * LOADS))
                            pe.wait_ge(s_scopy, u * NSC)
                        elif n >= 4:
                            pe.wait_ge(s_scopy, u * NSC + n - 3)
                        wd = width(i, c)
                        wide = max(wd, 2 * P)
                        rows, cols = slice(i * P, (i + 1) * P), slice(c * BANK, c * BANK + wide)
                        last = c == chunks(i) - 1
                        pe.matmul(sp_[n % 4][:, 0:wide], q_hi[b][m][:, rows], k_both[b][m][:, cols], start=True, stop=False)
                        mm = pe.matmul(sp_[n % 4][:, 0:wide], q_lo[b][m][:, rows], k_both[b][m][:, cols], start=False, stop=not last)
                        if last:
                            mm = pe.matmul(sp_[n % 4][:, wd - P:wd], t.ident_bf[:, :], t.mask[kind][:, :], start=False, stop=True)
                        mm.then_inc(s_score, 1)

                    def group_copied(g):
                        if by_dve(g):
                            pe.wait_ge(s_tcv, u * V_T + copies_before(g, True) + 1)
                        else:
                            pe.wait_ge(s_tca, u * A_T + copies_before(g, False) + 1)

                    def turn(i, m, c):
                        g = first_group[i, m] + c
                        if c == 0:
                            if fox:
                                pe.wait_ge(s_exp, u * 2 * TB + 2 * i + m + 1)
                            else:
                                pe.wait_ge(s_comb, u * TB * PER_COMB + (i + 1) * PER_COMB)
                        if g >= 2:
                            group_copied(g - 2)
                        for k in range(c * TPB, min((c + 1) * TPB, i + 1)):
                            mm = pe.transpose(tp_[g % 2][:, (k % TPB) * P:(k % TPB + 1) * P], prob[ring(i, m)][:, k * P:(k + 1) * P], t.ident)
                        mm.then_inc(s_tr, 1)

                    def value(i, m, c):
                        group_copied(first_group[i, m] + c)
                        n = tjobs.index((i, m))
                        if c == 0 and n >= 2:
                            pe.wait_ge(s_ocopy, u * NTJ + n - 1)
                        cols = slice(HD * m, HD * m + HD) if fox else slice(0, P)
                        o = op_[n % 2][:, 0:HD] if fox else op_[n % 2][:, :]
                        for k in range(c * TPB, min((c + 1) * TPB, i + 1)):
                            mm = pe.matmul(o, probT[n % 2][:, k, :], v[b][:, k, cols], start=(k == 0), stop=(k == i))
                        if c == chunks(i) - 1:
                            mm.then_inc(s_val, 1)

                    do = {"score": score, "turn": turn, "value": value}
                    for i in range(AHEAD):
                        for step in scores_of(i):
                            score(*step[1:])
                    for i in range(TB):
                        for step in order(i):
                            do[step[0]](*step[1:])

                units(pe, body)

            @block.scalar
            def _(act):
                def body(u, b, pair):
                    def exps(i, m):
                        r = ring(i, m)
                        act.wait_ge(s_scopy, u * NSC + first_chunk[i, m] + chunks(i))
                        act.activation(prob[r][:, 0:(i + 1) * P], prob[r][:, 0:(i + 1) * P], ACT.Exp, scale=-1.0,
                                       bias=low[:, r, chunks(i) - 1:chunks(i)],
                                       accum_out=den[:, r:r + 1]).then_inc(s_exp, 1)

                    def copy(i, m, c):
                        n = tjobs.index((i, m))
                        g = first_group[i, m] + c
                        if not by_dve(g):
                            act.wait_ge(s_tr, u * NTG + g + 1)
                            lo, hi = c * TPB, min((c + 1) * TPB, i + 1)
                            act.activation(probT[n % 2][:, lo:hi, :], tp_[g % 2][:, 0:(hi - lo) * P].rearrange("p (b n) -> p b n", n=P),
                                           ACT.Copy).then_inc(s_tca, 1)

                    for i in range(AHEAD):
                        exps(i, 0)
                        if i + 1 < AHEAD:
                            exps(i, 1)
                    for i in range(TB):
                        for x, (what, *step) in enumerate(order(i)):
                            if what == "turn":
                                copy(*step)
                            if x == 0 and i + AHEAD - 1 < TB:
                                exps(i + AHEAD - 1, 1)
                            if what == "score" and step[1:] == [0, chunks(step[0]) - 1]:
                                exps(step[0], 0)

                units(act, body)

            @block.vector
            def _(dve):
                def body(u, b, pair):
                    def copy_score(i, m, c):
                        r = ring(i, m)
                        n = first_chunk[i, m] + c
                        wd = width(i, c)
                        dve.wait_ge(s_score, u * NSC + n + 1)
                        if c:
                            dve.wait_ge(s_scopy, u * NSC + n)
                        init = low[:, r, c - 1:c] if c else BIG
                        if fox:
                            if n == 0:
                                dve.wait_ge(s_negf, (u + 1) * 32)
                            dve.sem_inc(s_hold, 1)
                            ins = dve.tensor_tensor_reduce(out=prob[r][:, c * BANK:c * BANK + wd], in0=sp_[n % 4][:, 0:wd],
                                                           in1=negf[m][:, c * BANK:c * BANK + wd], scale=-1.0, scalar=init,
                                                           op0=ALU.add, op1=ALU.min, accum_out=low[:, r, c:c + 1])
                        else:
                            ins = dve.tensor_scalar(prob[r][:, c * BANK:c * BANK + wd], sp_[n % 4][:, 0:wd], -1.0, init,
                                                    ALU.mult, ALU.min, accum_out=low[:, r, c:c + 1])
                        ins.then_inc(s_scopy, 1)

                    def combine(i):
                        q = ring(i, 0)
                        r = i % 2
                        base = u * TB * PER_COMB + i * PER_COMB
                        dve.wait_ge(s_exp, u * 2 * TB + 2 * i + 2)
                        dve.reciprocal(rden[:, r, :], den[:, q:q + 2]).then_inc(s_comb, 1)
                        dve.wait_ge(s_comb, base + 1)
                        dve.scalar_tensor_tensor(out=ratio[:, r:r + 1], in0=rden[:, r, 1:2], scalar=den[:, q:q + 1],
                                                 in1=t.neg_lambda[:, :], op0=ALU.mult, op1=ALU.mult).then_inc(s_comb, 1)
                        dve.wait_ge(s_comb, base + 2)
                        dve.scalar_tensor_tensor(out=prob[q][:, 0:(i + 1) * P], in0=prob[q + 1][:, 0:(i + 1) * P],
                                                 scalar=ratio[:, r:r + 1], in1=prob[q][:, 0:(i + 1) * P],
                                                 op0=ALU.mult, op1=ALU.add).then_inc(s_comb, 1)

                    def copy(i, m, c):
                        n = tjobs.index((i, m))
                        g = first_group[i, m] + c
                        if by_dve(g):
                            dve.wait_ge(s_tr, u * NTG + g + 1)
                            lo, hi = c * TPB, min((c + 1) * TPB, i + 1)
                            dve.tensor_copy(probT[n % 2][:, lo:hi, :],
                                            tp_[g % 2][:, 0:(hi - lo) * P].rearrange("p (b n) -> p b n", n=P)).then_inc(s_tcv, 1)

                    def output(i, m):
                        n = tjobs.index((i, m))
                        if m == 0:
                            dve.wait_ge(s_store[i % 2], u * (16 * TB // 2) + 16 * (i // 2))
                        if fox:
                            q = n % 4
                            r = ring(i, m)
                            dve.wait_ge(s_exp, u * 2 * TB + 2 * i + m + 1)
                            dve.reciprocal(rec[:, q:q + 1], den[:, r:r + 1]).then_inc(s_rec, 1)
                            dve.wait_ge(s_rec, u * 2 * TB + 2 * i + m + 1)
                            dve.wait_ge(s_val, u * NTJ + n + 1)
                            dve.tensor_scalar(outs[i % 2][:, HD * m:HD * m + HD], op_[n % 2][:, 0:HD], rec[:, q:q + 1], None,
                                              ALU.mult).then_inc(s_ocopy, 1)
                        else:
                            dve.wait_ge(s_val, u * NTJ + n + 1)
                            dve.tensor_scalar(outs[i % 2][:, :], op_[n % 2][:, :], rden[:, i % 2, 0:1], None,
                                              ALU.mult).then_inc(s_ocopy, 1)

                    for i in range(AHEAD):
                        for step in scores_of(i):
                            copy_score(*step[1:])
                    if not fox:
                        combine(0)
                    for i in range(TB):
                        steps = order(i)
                        for x, (what, *step) in enumerate(steps):
                            if x == len(steps) // 2 and not fox and i + 1 < TB:
                                combine(i + 1)
                            if what == "score":
                                copy_score(*step)
                            elif what == "turn":
                                copy(*step)
                            elif step[2] == chunks(i) - 1:
                                output(i, step[1])

                units(dve, body)


def load_expert(eng, a, t, e, slot, free=lambda name: None):
    for name, at, rows, cols in (("w_gate", W_GATE, KT, F), ("w_up", W_UP, KT, F), ("w_down", W_DOWN, FT, D)):
        free(name)
        eng.dma_start(t.weights[:, slot, at:at + rows * cols].rearrange("p (k n) -> p k n", n=cols),
                      a[name][0, bass.ds(e, 1)].rearrange("a (k p) n -> p (a k) n", p=P)).then_inc(t.s_w[name][slot], 16)


def merge(nc, a, t):
    with ExitStack() as ctx:
        p = Names(nc, ctx, "mrg_")
        spare = t.weights[:, 1, :]
        w_out = spare[:, 0:KT * D].rearrange("p (k n) -> p k n", n=D)
        xx, junk, mT, h2T = (spare[:, (KT + n) * D:(KT + n + 1) * D] for n in range(4))
        mT, h2T = (x.rearrange("p (k n) -> p k n", n=P) for x in (mT, h2T))
        w_rt = p.sb("w_router_sb", [P, KT, LOGITS])
        b_rt = p.sb("b_router_sb", [P, LOGITS])
        mx = p.sb("mx", [P, D])
        sq = p.sb("sq", [P, F])
        ssh = p.sb("ssh", [P, 4])
        stdh = p.sb("stdh", [P, 4])
        rh = p.sb("rh", [P, 4])
        o = p.sb("o", [P, D])
        h2 = p.sb("h2", [P, D])
        ss = p.sb("ss", [P, 2])
        sd = p.sb("sd", [P, 2])
        rr = p.sb("rr", [P, 2])
        mtp = [p.ps(f"mtp{i}", [P, BANK]) for i in range(2)]
        outp = p.ps("outp", [P, 2, BANK])
        htp = [p.ps(f"htp{i}", [P, BANK]) for i in range(2)]
        rtp = p.ps("rtp", [P, LOGITS])
        names = ("rows_loaded w_loaded mixed_loaded x_loaded head_squares head_std heads_scaled mixed_turned mT_copied "
                 "projected_out out_copied out_squares out_std x1_steps x1_squares x1_std h2_steps h2_stored "
                 "h2_turned h2T_copied router_product logits_done dve_links").split()
        s = {n: p.sem("m_" + n) for n in names}

        with nc.Block() as block:

            @block.gpsimd
            def _(pool):
                pool.dma_start(w_rt[:, :, 0:GROUPS], a["w_group"][0].rearrange("(k p) n -> p k n", p=P)).then_inc(s["w_loaded"], 16)
                pool.dma_start(w_rt[:, :, GROUPS:], a["w_router"][0].rearrange("(k p) n -> p k n", p=P)).then_inc(s["w_loaded"], 16)
                pool.dma_start(b_rt[:, 0:GROUPS], a["b_group"].to_broadcast([P, GROUPS])).then_inc(s["w_loaded"], 16)
                pool.dma_start(b_rt[:, GROUPS:], a["b_router"].to_broadcast([P, EXPERTS])).then_inc(s["w_loaded"], 16)
                pool.dma_start(w_out[:, :, :], a["w_out"][0].rearrange("(k p) n -> p k n", p=P)).then_inc(s["w_loaded"], 16)
                with pool.Fori(0, TB) as i:
                    pool.wait_ge(s["x1_steps"], 2 * i)
                    pool.dma_start(xx[:, :], a["x"][0, bass.ds(i * P, P), :]).then_inc(s["x_loaded"], 16)

            @block.sync
            def _(sp):
                sp.dma_start(mx[:, :], t.mixed[0:P, :]).then_inc(s["mixed_loaded"], 16)
                for i, name in enumerate(ROWS):
                    sp.dma_start(t.row[name][:, :], t.row_dram[i:i + 1, :].to_broadcast([P, D])).then_inc(s["rows_loaded"], 16)
                load_expert(sp, a, t, 0, 0)
                with sp.Fori(0, TB - 1) as i:
                    sp.wait_ge(s["mixed_turned"], 2 * i + 2)
                    sp.dma_start(mx[:, :], t.mixed[bass.ds(i * P + P, P), :]).then_inc(s["mixed_loaded"], 16)
                    sp.wait_ge(s["h2_steps"], 2 * i + 2)
                    sp.dma_start(t.h2[bass.ds(i * P, P), :], h2[:, :]).then_inc(s["h2_stored"], 16)
                sp.wait_ge(s["h2_steps"], 2 * TB)
                sp.dma_start(t.h2[(TB - 1) * P:, :], h2[:, :]).then_inc(s["h2_stored"], 16)
                sp.wait_ge(s["h2_stored"], 16 * TB)

            @block.tensor
            def _(pe):
                def turn(i):
                    pe.wait_ge(s["heads_scaled"], i + 1)
                    pe.wait_ge(s["mT_copied"], i * 2)
                    for h in range(2):
                        for j in range(TPB):
                            mm = pe.transpose(mtp[h][:, j * P:(j + 1) * P], mx[:, (h * TPB + j) * P:(h * TPB + j + 1) * P], t.ident)
                        mm.then_inc(s["mixed_turned"], 1)

                def project(i):
                    pe.wait_ge(s["mT_copied"], i * 2 + 2)
                    pe.wait_ge(s["out_copied"], i)
                    for h in range(2):
                        for k in range(KT):
                            mm = pe.matmul(outp[:, h, :], mT[:, k, :], w_out[:, k, h * BANK:(h + 1) * BANK],
                                           start=(k == 0), stop=(k == KT - 1))
                    mm.then_inc(s["projected_out"], 1)

                def router(i):
                    pe.wait_ge(s["h2_steps"], i * 2 + 2)
                    pe.wait_ge(s["h2T_copied"], i * 2)
                    for h in range(2):
                        for j in range(TPB):
                            mm = pe.transpose(htp[h][:, j * P:(j + 1) * P], h2[:, (h * TPB + j) * P:(h * TPB + j + 1) * P], t.ident)
                        mm.then_inc(s["h2_turned"], 1)
                    pe.wait_ge(s["h2T_copied"], i * 2 + 2)
                    pe.wait_ge(s["logits_done"], i)
                    for k in range(KT):
                        mm = pe.matmul(rtp[:, :], h2T[:, k, :], w_rt[:, k, :], start=(k == 0), stop=(k == KT - 1))
                    mm.then_inc(s["router_product"], 1)

                pe.wait_ge(s["w_loaded"], 80)
                turn(0)
                project(0)
                turn(1)
                with pe.Fori(1, TB - 1) as i:
                    project(i)
                    turn(i + 1)
                    router(i - 1)
                project(TB - 1)
                router(TB - 2)
                router(TB - 1)

            @block.scalar
            def _(act):
                def head_std(i):
                    act.wait_ge(s["head_squares"], 2 * i + 2)
                    act.activation(stdh[:, :], ssh[:, :], ACT.Sqrt, scale=1.0 / P, bias=t.eps[:, :]).then_inc(s["head_std"], 1)

                def copy_turned(i):
                    act.wait_ge(s["mixed_turned"], 2 * i + 1)
                    act.activation(mT[:, 0:TPB, :], mtp[0][:, :].rearrange("p (b n) -> p b n", n=P), ACT.Identity,
                                   scale=t.subln[:, :]).then_inc(s["mT_copied"], 1)
                    act.wait_ge(s["mixed_turned"], 2 * i + 2)
                    act.activation(mT[:, TPB:, :], mtp[1][:, :].rearrange("p (b n) -> p b n", n=P), ACT.Copy).then_inc(s["mT_copied"], 1)

                def stds(i):
                    act.wait_ge(s["out_copied"], i + 1)
                    act.wait_ge(s["x1_squares"], i)
                    act.activation(junk[:, :], o[:, :], ACT.Square, accum_out=ss[:, 0:1]).then_inc(s["out_squares"], 1)
                    act.wait_ge(s["out_squares"], i + 1)
                    act.activation(sd[:, 0:1], ss[:, 0:1], ACT.Sqrt, scale=1.0 / D, bias=t.eps[:, :]).then_inc(s["out_std"], 1)
                    act.wait_ge(s["x1_steps"], 2 * i + 2)
                    act.activation(junk[:, :], t.x1[:, bass.ds(i, 1), :].rearrange("p a d -> p (a d)"), ACT.Square,
                                   accum_out=ss[:, 1:2]).then_inc(s["x1_squares"], 1)
                    act.wait_ge(s["x1_squares"], i + 1)
                    act.activation(sd[:, 1:2], ss[:, 1:2], ACT.Sqrt, scale=1.0 / D, bias=t.eps[:, :]).then_inc(s["x1_std"], 1)

                def copy_h2(i):
                    for h in range(2):
                        act.wait_ge(s["h2_turned"], 2 * i + h + 1)
                        act.activation(h2T[:, h * TPB:(h + 1) * TPB, :], htp[h][:, :].rearrange("p (b n) -> p b n", n=P),
                                       ACT.Copy).then_inc(s["h2T_copied"], 1)

                head_std(0)
                copy_turned(0)
                head_std(1)
                copy_turned(1)
                stds(0)
                with act.Fori(1, TB - 1) as i:
                    head_std(i + 1)
                    copy_turned(i + 1)
                    copy_h2(i - 1)
                    stds(i)
                copy_h2(TB - 2)
                stds(TB - 1)
                copy_h2(TB - 1)

            @block.vector
            def _(dve):
                heads = mx[:, 0:F].rearrange("p (h e) -> p h e", e=P)

                def head_part(i, links):
                    dve.wait_ge(s["mixed_loaded"], 16 * (i + 1))
                    dve.tensor_tensor(sq[:, :], mx[:, 0:F], mx[:, 0:F], ALU.mult).then_inc(s["head_squares"], 1)
                    dve.wait_ge(s["head_squares"], 2 * i + 1)
                    dve.tensor_reduce(ssh[:, :], sq[:, :].rearrange("p (h e) -> p h e", e=P), X, ALU.add).then_inc(s["head_squares"], 1)
                    dve.wait_ge(s["head_std"], i + 1)
                    dve.reciprocal(rh[:, :], stdh[:, :]).then_inc(s["dve_links"], 1)
                    dve.wait_ge(s["dve_links"], links + 1)
                    dve.tensor_tensor(heads, heads, rh[:, :].unsqueeze(2).to_broadcast([P, 4, P]), ALU.mult).then_inc(s["heads_scaled"], 1)

                def row_part(i, links):
                    x1 = t.x1[:, bass.ds(i, 1), :].rearrange("p a d -> p (a d)")
                    dve.wait_ge(s["projected_out"], i + 1)
                    dve.tensor_copy(o[:, :], outp[:, :, :].rearrange("p a d -> p (a d)")).then_inc(s["out_copied"], 1)
                    dve.wait_ge(s["out_std"], i + 1)
                    dve.reciprocal(rr[:, 0:1], sd[:, 0:1]).then_inc(s["dve_links"], 1)
                    dve.wait_ge(s["dve_links"], links + 1)
                    dve.scalar_tensor_tensor(out=x1, in0=o[:, :], scalar=rr[:, 0:1], in1=t.row["gate_attn"][:, :],
                                             op0=ALU.mult, op1=ALU.mult).then_inc(s["x1_steps"], 1)
                    dve.wait_ge(s["x1_steps"], 2 * i + 1)
                    dve.wait_ge(s["x_loaded"], 16 * (i + 1))
                    dve.tensor_tensor(x1, x1, xx[:, :], ALU.add).then_inc(s["x1_steps"], 1)
                    dve.wait_ge(s["x1_std"], i + 1)
                    dve.reciprocal(rr[:, 1:2], sd[:, 1:2]).then_inc(s["dve_links"], 1)
                    dve.wait_ge(s["dve_links"], links + 2)
                    dve.wait_ge(s["h2_stored"], 16 * i)
                    dve.wait_ge(s["h2_turned"], 2 * i)
                    dve.scalar_tensor_tensor(out=h2[:, :], in0=x1, scalar=rr[:, 1:2], in1=t.row["ffn_gain"][:, :],
                                             op0=ALU.mult, op1=ALU.mult).then_inc(s["h2_steps"], 1)
                    dve.wait_ge(s["h2_steps"], 2 * i + 1)
                    dve.tensor_tensor(h2[:, :], h2[:, :], t.row["ffn_shift"][:, :], ALU.add).then_inc(s["h2_steps"], 1)

                def logits(i):
                    dve.wait_ge(s["router_product"], i + 1)
                    dve.tensor_tensor(t.logits[:, bass.ds(i, 1), :].rearrange("p a n -> p (a n)"), rtp[:, :], b_rt[:, :],
                                      ALU.add).then_inc(s["logits_done"], 1)

                dve.wait_ge(s["rows_loaded"], 16 * len(ROWS))
                head_part(0, 0)
                head_part(1, 1)
                row_part(0, 2)
                with dve.Fori(1, TB - 1) as i:
                    head_part(i + 1, 3 * i + 1)
                    row_part(i, 3 * i + 2)
                    logits(i - 1)
                row_part(TB - 1, 3 * TB - 2)
                logits(TB - 2)
                logits(TB - 1)


def route(nc, a, t):
    with ExitStack() as ctx:
        p = Names(nc, ctx, "rt_")
        G, E8, E = GROUPS, PER_GROUP, EXPERTS
        def tile(name, *shape, dt=F32):
            return p.sb(name, [P, *shape], dt)
        gmax, gpick, gw, m1, m2, pick = (tile(n, TB) for n in ("gmax", "gpick", "gw", "m1", "m2", "pick"))
        geq, goh, gexp = (tile(n, TB, G) for n in ("geq", "goh", "gexp"))
        emask = tile("emask", TB, G, E8)
        esel, eeq, oh1, oh2, esel2 = (tile(n, TB, E8) for n in ("esel", "eeq", "oh1", "oh2", "esel2"))
        gap, egap, dsum = (tile(n, TB) for n in ("gap", "egap", "dsum"))
        E1, E2, off, rank = (row[:, h * TB * E:(h + 1) * TB * E].rearrange("p (t e) -> p t e", e=E)
                             for row in (t.row["gate_attn"], t.row["ffn_gain"]) for h in range(2))
        both = tile("both", TB, E, dt=BF16)
        prod = tile("prod", TB, E)
        cnt = tile("cnt", E)
        cnti, nbi = tile("cnti", E, dt=I32), tile("nbi", E, dt=I32)
        nb, ones = tile("nb", E), tile("ones_e", E)
        ended = tile("ended", TABLE, E, dt=BF16)
        owner = tile("owner", TABLE)
        owneri, half = tile("owneri", TABLE, dt=I32), tile("half", TABLE, dt=I32)
        cum = tile("cum", E + 1)
        dest = tile("dest", 2, TB)
        desti, pi, bi = (tile(n, 2, TB, dt=I32) for n in ("desti", "pi", "bi"))
        pf, bf = tile("pf", 2, TB), tile("bf", 2, TB)
        vals = tile("vals", 2, TB)
        tab, second, unused = (tile(n, TABLE) for n in ("tab", "second", "unused"))
        at_p = [tile(f"at_p{i}", P) for i in range(2)]
        at_b = [tile(f"at_b{i}", TABLE) for i in range(2)]
        prefix = p.ps("prefix", [P, TB * E])
        totals = p.ps("totals", [P, TB * E])
        table = p.ps("table", [P, TABLE])
        s_v, s_a, s_cnt, s_at, s_tab = (p.sem(n) for n in
                                        ("r_dve", "r_exp", "r_counted", "r_onehots", "r_table"))
        READY_G, READY_E, READY_B = [0], [0], [0]

        with nc.Block() as block:

            @block.sync
            def _(sp):
                load_expert(sp, a, t, 1, 1)

            @block.vector
            def _(dve):
                st = Steps(dve, s_v)
                L = st.link
                gl = t.logits[:, :, 0:G]
                el = t.logits[:, :, G:].rearrange("p t (g e) -> p t g e", g=G)
                gdesc = t.consts[:, C_GDESC:C_GDESC + G].unsqueeze(1).to_broadcast([P, TB, G])
                edesc = t.consts[:, C_EDESC:C_EDESC + E8].unsqueeze(1).to_broadcast([P, TB, E8])

                def wide(x, n):
                    return x[:, :].unsqueeze(2).to_broadcast([P, TB, n])

                def first_max(src, value, equal, chosen, desc, n):
                    L(dve.tensor_reduce(value[:, :], src, X, ALU.max))
                    L(dve.tensor_tensor(equal[:, :, :], src, wide(value, n), ALU.is_equal))
                    L(dve.tensor_tensor(equal[:, :, :], equal[:, :, :], desc, ALU.mult))
                    L(dve.tensor_reduce(pick[:, :], equal[:, :, :], X, ALU.max))
                    L(dve.tensor_tensor(chosen[:, :, :], equal[:, :, :], wide(pick, n), ALU.is_equal))

                first_max(gl, gmax, geq, goh, gdesc, G)
                L(dve.tensor_tensor(gexp[:, :, :], gl, wide(gmax, G), ALU.subtract))
                READY_G[0] = st.n
                for g in range(G):
                    L(dve.tensor_tensor(emask[:, :, g, :], el[:, :, g, :], goh[:, :, g:g + 1].to_broadcast([P, TB, E8]), ALU.mult))
                L(dve.tensor_reduce(esel[:, :, :], emask[:, :, :, :].rearrange("p t g e -> p t e g"), X, ALU.add))
                first_max(esel[:, :, :], m1, eeq, oh1, edesc, E8)
                L(dve.scalar_tensor_tensor(out=esel2[:, :, :], in0=oh1[:, :, :], scalar=-BIG, in1=esel[:, :, :], op0=ALU.mult, op1=ALU.add))
                first_max(esel2[:, :, :], m2, eeq, oh2, edesc, E8)
                L(dve.tensor_tensor(gap[:, :], m2[:, :], m1[:, :], ALU.subtract))
                READY_E[0] = st.n
                for g in range(G):
                    gb = goh[:, :, g:g + 1].to_broadcast([P, TB, E8])
                    L(dve.tensor_tensor(E1[:, :, g * E8:(g + 1) * E8], oh1[:, :, :], gb, ALU.mult))
                    L(dve.tensor_tensor(E2[:, :, g * E8:(g + 1) * E8], oh2[:, :, :], gb, ALU.mult))
                L(dve.tensor_tensor(both[:, :, :], E1[:, :, :], E2[:, :, :], ALU.add))
                READY_B[0] = st.n
                dve.wait_ge(s_a, 1)
                L(dve.tensor_reduce(gw[:, :], gexp[:, :, :], X, ALU.add))
                L(dve.reciprocal(gw[:, :], gw[:, :]))
                dve.wait_ge(s_a, 2)
                L(dve.tensor_scalar(dsum[:, :], egap[:, :], 1.0, None, ALU.add))
                L(dve.reciprocal(dsum[:, :], dsum[:, :]))
                L(dve.tensor_tensor(t.weight[:, 0, :], gw[:, :], dsum[:, :], ALU.mult))
                L(dve.tensor_tensor(t.weight[:, 1, :], t.weight[:, 0, :], egap[:, :], ALU.mult))
                dve.wait_ge(s_cnt, 2)
                tot = totals[:, :].rearrange("p (t e) -> p t e", e=E)
                L(dve.memset(off[:, 0, :], 0.0))
                for i in range(1, TB):
                    L(dve.tensor_tensor(off[:, i, :], off[:, i - 1, :], tot[:, i - 1, :], ALU.add))
                L(dve.tensor_tensor(cnt[:, :], off[:, TB - 1, :], tot[:, TB - 1, :], ALU.add))
                L(dve.tensor_tensor(rank[:, :, :], off[:, :, :], prefix[:, :].rearrange("p (t e) -> p t e", e=E), ALU.add))
                L(dve.tensor_scalar(cnti[:, :], cnt[:, :], float(P - 1), None, ALU.add))
                L(dve.tensor_scalar(nbi[:, :], cnti[:, :], P.bit_length() - 1, None, ALU.logical_shift_right))
                L(dve.tensor_scalar(nb[:, :], nbi[:, :], 1.0, None, ALU.max))
                L(dve.memset(ones[:, :], 1.0))
                L(dve.memset(cum[:, 0:1], 0.0))
                L(dve.tensor_tensor_scan(cum[:, 1:E + 1], ones[:, :], nb[:, :], 0.0, ALU.mult, ALU.add))
                L(dve.tensor_copy(t.cum_blocks[:, 0:E + 1], cum[:, :]))
                L(dve.tensor_scalar(t.cum_blocks[:, E + 1:E + 2], cum[:, E:E + 1], -1.0, None, ALU.add))
                L(dve.memset(t.cum_prev[:, 0:1], 0))
                L(dve.tensor_copy(t.cum_prev[:, 1:E], cum[:, 0:E - 1]))
                L(dve.tensor_tensor(ended[:, :, :], cum[:, 1:E + 1].unsqueeze(1).to_broadcast([P, TABLE, E]),
                                    t.consts[:, C_IOTA:C_IOTA + TABLE].unsqueeze(2).to_broadcast([P, TABLE, E]), ALU.is_le))
                L(dve.tensor_reduce(owner[:, :], ended[:, :, :], X, ALU.add))
                L(dve.tensor_copy(owneri[:, :], owner[:, :]))
                L(dve.tensor_scalar(t.slot[:, :], owneri[:, :], 1, None, ALU.bitwise_and))
                L(dve.tensor_scalar(half[:, :], owneri[:, :], 1, None, ALU.logical_shift_right))
                L(dve.tensor_scalar(t.loads[:, 0, :], half[:, :], 1.0, 16.0, ALU.add, ALU.mult))
                L(dve.tensor_scalar(owneri[:, :], owneri[:, :], 1.0, None, ALU.add))
                L(dve.tensor_scalar(half[:, :], owneri[:, :], 1, None, ALU.logical_shift_right))
                L(dve.tensor_scalar(t.loads[:, 1, :], half[:, :], 16.0, None, ALU.mult))
                L(dve.tensor_scalar(cum[:, :], cum[:, :], float(P), None, ALU.mult))
                L(dve.tensor_tensor(rank[:, :, :], rank[:, :, :], cum[:, 0:E].unsqueeze(1).to_broadcast([P, TB, E]), ALU.add))
                for n, oh in enumerate((E1, E2)):
                    L(dve.tensor_tensor(prod[:, :, :], oh[:, :, :], rank[:, :, :], ALU.mult))
                    L(dve.tensor_reduce(dest[:, n, :], prod[:, :, :], X, ALU.add))
                L(dve.tensor_copy(desti[:, :, :], dest[:, :, :]))
                L(dve.tensor_scalar(pi[:, :, :], desti[:, :, :], P - 1, None, ALU.bitwise_and))
                L(dve.tensor_scalar(bi[:, :, :], desti[:, :, :], P.bit_length() - 1, None, ALU.logical_shift_right))
                L(dve.tensor_copy(pf[:, :, :], pi[:, :, :]))
                L(dve.tensor_copy(bf[:, :, :], bi[:, :, :]))
                L(dve.tensor_scalar(vals[:, 0, :], t.consts[:, C_TOKEN:C_TOKEN + TB], 1.0, None, ALU.add))
                L(dve.tensor_scalar(vals[:, 1, :], t.consts[:, C_TOKEN:C_TOKEN + TB], 1.0 + S, None, ALU.add))
                for q in range(2 * TB):
                    n, i = divmod(q, TB)
                    if q >= 2:
                        dve.wait_ge(s_tab, q - 1)
                    dve.tensor_scalar(at_p[q % 2][:, :], t.consts[:, C_IOTA:C_IOTA + P], pf[:, n, i:i + 1], None,
                                      ALU.is_equal).then_inc(s_at, 1)
                    dve.tensor_scalar(at_b[q % 2][:, :], t.consts[:, C_IOTA:C_IOTA + TABLE], bf[:, n, i:i + 1],
                                      vals[:, n, i:i + 1], ALU.is_equal, ALU.mult).then_inc(s_at, 1)
                dve.wait_ge(s_tab, 2 * TB)
                L(dve.tensor_copy(tab[:, :], table[:, :]))
                L(dve.tensor_scalar(second[:, :], tab[:, :], S + 0.5, float(-S), ALU.is_gt, ALU.mult))
                L(dve.scalar_tensor_tensor(out=second[:, :], in0=tab[:, :], scalar=-1.0, in1=second[:, :], op0=ALU.add, op1=ALU.add))
                L(dve.tensor_scalar(t.ids[:, :], second[:, :], 0.0, None, ALU.max))
                L(dve.tensor_scalar(unused[:, :], tab[:, :], 0.5, None, ALU.is_lt))
                L(dve.tensor_scalar(unused[:, :], unused[:, :], t.consts[:, C_TRASH:C_TRASH + 1], None, ALU.mult))
                L(dve.scalar_tensor_tensor(out=t.rows[:, :], in0=tab[:, :], scalar=-1.0, in1=unused[:, :], op0=ALU.add, op1=ALU.add))

            @block.scalar
            def _(act):
                act.wait_ge(s_v, READY_G[0])
                act.activation(gexp[:, :, :], gexp[:, :, :], ACT.Exp).then_inc(s_a, 1)
                act.wait_ge(s_v, READY_E[0])
                act.activation(egap[:, :], gap[:, :], ACT.Exp).then_inc(s_a, 1)

            @block.tensor
            def _(pe):
                pe.wait_ge(s_v, READY_B[0])
                flat = both[:, :, :].rearrange("p t e -> p (t e)")
                pe.matmul(prefix[:, :], t.before_bf[:, :], flat, start=True, stop=True).then_inc(s_cnt, 1)
                pe.matmul(totals[:, :], t.ones_bf[:, :], flat, start=True, stop=True).then_inc(s_cnt, 1)
                for q in range(2 * TB):
                    pe.wait_ge(s_at, 2 * q + 2)
                    pe.matmul(table[:, :], at_p[q % 2][:, :], at_b[q % 2][:, :], start=(q == 0), stop=(q == 2 * TB - 1)).then_inc(s_tab, 1)


def experts(nc, a, t):
    with ExitStack() as ctx:
        p = Names(nc, ctx, "ex_")
        ids = p.sb("ids_now", [P, 1], U32)
        rows = p.sb("rows_now", [P, 1], U32)
        xg = p.sb("xg", [P, D])
        xT = p.sb("xT", [P, KT, P])
        gate = p.sb("gate", [P, F])
        hid = p.sb("hid", [P, F])
        hidT = p.sb("hidT", [P, FT, P])
        y = p.sb("y", [P, D])
        xtp = [p.ps(f"ext{i}", [P, BANK]) for i in range(2)]
        gp = p.ps("gp", [P, F])
        up = p.ps("up", [P, F])
        hp = p.ps("hp", [P, F])
        yp = [p.ps(f"yp{i}", [P, BANK]) for i in range(2)]
        names = ("hold ids_ready rows_ready gathered x_turned x_copied gate_product up_product gate_activated hidden hidden_turned "
                 "hidden_copied down_product y_copied_a y_copied_v y_stored").split()
        s = {n: p.sem("e_" + n) for n in names}
        reader = {"w_gate": "gate_product", "w_up": "up_product", "w_down": "down_product"}

        def total_blocks(eng):
            return eng.value_load(t.cum_blocks[0:1, EXPERTS:EXPERTS + 1], min_val=EXPERTS, max_val=MAX_BLOCKS)

        def last_block(eng):
            return eng.value_load(t.cum_blocks[0:1, EXPERTS + 1:EXPERTS + 2], min_val=0, max_val=MAX_BLOCKS)

        with nc.Block() as block:

            @block.sync
            def _(sp):
                with sp.Fori(1, EXPERTS // 2) as pair:
                    for b in range(2):
                        e = pair * 2 + b
                        prev = sp.value_load(t.cum_prev[0:1, bass.ds(e, 1)], min_val=0, max_val=MAX_BLOCKS)
                        load_expert(sp, a, t, e, b, lambda name: sp.wait_ge(s[reader[name]], prev))

            @block.gpsimd
            def _(pool):
                def fetch(g):
                    pool.wait_ge(s["x_turned"], 2 * g)
                    pool.tensor_copy(ids[:, :], t.ids[:, bass.ds(g, 1)]).then_inc(s["ids_ready"], 1)
                    pool.wait_ge(s["ids_ready"], g + 1)
                    pool.sem_inc(s["hold"], 1)
                    pool.indirect_dma_start(out=xg[:, :], out_offset=None, in_=t.h2,
                                            in_offset=bass.IndirectOffsetOnAxis(ap=ids[:, 0:1], axis=0)).then_inc(s["gathered"], 16)

                fetch(0)
                fetch(1)
                total = total_blocks(pool)
                with pool.Fori(0, total) as g:
                    fetch(g + 2)
                    pool.wait_ge(s["y_stored"], 16 * g)
                    pool.tensor_copy(rows[:, :], t.rows[:, bass.ds(g, 1)]).then_inc(s["rows_ready"], 1)
                    pool.wait_ge(s["rows_ready"], g + 1)
                    pool.wait_ge(s["y_copied_a"], g + 1)
                    pool.wait_ge(s["y_copied_v"], g + 1)
                    pool.sem_inc(s["hold"], 1)
                    pool.indirect_dma_start(out=t.y, out_offset=bass.IndirectOffsetOnAxis(ap=rows[:, 0:1], axis=0),
                                            in_=y[:, :], in_offset=None).then_inc(s["y_stored"], 16)
                pool.wait_ge(s["gathered"], total * 16 + 32)
                pool.wait_ge(s["y_stored"], total * 16)
                pool.sem_inc(s["hold"], 1)
                pool.tensor_copy(ids[:, :], t.ids[:, 0:1]).then_inc(s["ids_ready"], 1)

            @block.tensor
            def _(pe):
                def slot_of(g):
                    return pe.value_load(t.slot[0:1, bass.ds(g, 1)], min_val=0, max_val=1)

                def weight(slot, at, cols, k, lo, n):
                    return t.weights[:, bass.ds(slot, 1), at + k * cols + lo:at + k * cols + lo + n].rearrange("p a n -> p (a n)")

                def turn(g):
                    pe.wait_ge(s["gathered"], 16 * g + 16)
                    pe.wait_ge(s["x_copied"], 2 * g)
                    for h in range(2):
                        for j in range(TPB):
                            mm = pe.transpose(xtp[h][:, j * P:(j + 1) * P], xg[:, (h * TPB + j) * P:(h * TPB + j + 1) * P], t.ident)
                        mm.then_inc(s["x_turned"], 1)

                def loads_for(g):
                    return [pe.value_load(t.loads[0:1, b, bass.ds(g, 1)], min_val=0, max_val=16 * (EXPERTS // 2 + 1))
                            for b in range(2)]

                def loaded(name, loads):
                    for b in range(2):
                        pe.wait_ge(t.s_w[name][b], loads[b])

                def gate_product(g, slot, loads):
                    loaded("w_gate", loads)
                    pe.wait_ge(s["x_copied"], 2 * g + 2)
                    pe.wait_ge(s["gate_activated"], g)
                    for k in range(KT):
                        mm = pe.matmul(gp[:, :], xT[:, k, :], weight(slot, W_GATE, F, k, 0, F), start=(k == 0), stop=(k == KT - 1))
                    mm.then_inc(s["gate_product"], 1)

                def up_product(g, slot, loads):
                    loaded("w_up", loads)
                    pe.wait_ge(s["hidden"], g)
                    for k in range(KT):
                        mm = pe.matmul(up[:, :], xT[:, k, :], weight(slot, W_UP, F, k, 0, F), start=(k == 0), stop=(k == KT - 1))
                    mm.then_inc(s["up_product"], 1)

                def turn_hidden(g):
                    pe.wait_ge(s["hidden"], g + 1)
                    pe.wait_ge(s["hidden_copied"], g)
                    for k in range(FT):
                        mm = pe.transpose(hp[:, k * P:(k + 1) * P], hid[:, k * P:(k + 1) * P], t.ident)
                    mm.then_inc(s["hidden_turned"], 1)

                def down_product(g, slot, loads):
                    loaded("w_down", loads)
                    pe.wait_ge(s["hidden_copied"], g + 1)
                    pe.wait_ge(s["y_copied_a"], g)
                    pe.wait_ge(s["y_copied_v"], g)
                    for h in range(2):
                        for k in range(FT):
                            mm = pe.matmul(yp[h][:, :], hidT[:, k, :], weight(slot, W_DOWN, D, k, h * BANK, BANK),
                                           start=(k == 0), stop=(k == FT - 1))
                    mm.then_inc(s["down_product"], 1)

                turn(0)
                first = slot_of(0)
                loads = loads_for(0)
                gate_product(0, first, loads)
                up_product(0, first, loads)
                turn(1)
                total = total_blocks(pe)
                with pe.Fori(1, total) as g:
                    slot = slot_of(g)
                    last = slot_of(g - 1)
                    loads = loads_for(g)
                    last_loads = loads_for(g - 1)
                    gate_product(g, slot, loads)
                    turn_hidden(g - 1)
                    up_product(g, slot, loads)
                    turn(g + 1)
                    down_product(g - 1, last, last_loads)
                end = last_block(pe)
                last = slot_of(end)
                last_loads = loads_for(end)
                turn_hidden(end)
                down_product(end, last, last_loads)

            @block.scalar
            def _(act):
                def copy_x(g):
                    for h in range(2):
                        act.wait_ge(s["x_turned"], 2 * g + h + 1)
                        act.wait_ge(s["up_product"], g)
                        act.activation(xT[:, h * TPB:(h + 1) * TPB, :], xtp[h][:, :].rearrange("p (b n) -> p b n", n=P),
                                       ACT.Copy).then_inc(s["x_copied"], 1)

                def activate(g):
                    act.wait_ge(s["gate_product"], g + 1)
                    act.wait_ge(s["hidden"], g)
                    act.activation(gate[:, :], gp[:, :], ACT.Silu).then_inc(s["gate_activated"], 1)

                def copy_y(g):
                    act.wait_ge(s["down_product"], g + 1)
                    act.wait_ge(s["y_stored"], 16 * g)
                    act.activation(y[:, 0:BANK], yp[0][:, :], ACT.Copy).then_inc(s["y_copied_a"], 1)

                copy_x(0)
                activate(0)
                copy_x(1)
                total = total_blocks(act)
                with act.Fori(1, total) as g:
                    activate(g)
                    copy_x(g + 1)
                    copy_y(g - 1)
                copy_y(last_block(act))

            @block.vector
            def _(dve):
                def multiply(g):
                    dve.wait_ge(s["gate_activated"], g + 1)
                    dve.wait_ge(s["up_product"], g + 1)
                    dve.wait_ge(s["hidden_turned"], g)
                    dve.tensor_tensor(hid[:, :], gate[:, :], up[:, :], ALU.mult).then_inc(s["hidden"], 1)

                def copy_hidden(g):
                    dve.wait_ge(s["hidden_turned"], g + 1)
                    dve.wait_ge(s["down_product"], g)
                    dve.tensor_copy(hidT[:, :, :], hp[:, :].rearrange("p (b n) -> p b n", n=P)).then_inc(s["hidden_copied"], 1)

                def copy_y(g):
                    dve.wait_ge(s["down_product"], g + 1)
                    dve.wait_ge(s["y_stored"], 16 * g)
                    dve.tensor_copy(y[:, BANK:], yp[1][:, :]).then_inc(s["y_copied_v"], 1)

                multiply(0)
                total = total_blocks(dve)
                with dve.Fori(1, total) as g:
                    copy_hidden(g - 1)
                    multiply(g)
                    copy_y(g - 1)
                end = last_block(dve)
                copy_hidden(end)
                copy_y(end)


def combine(nc, a, t, out):
    with ExitStack() as ctx:
        p = Names(nc, ctx, "cb_")
        NB = 2
        y1 = [p.sb(f"y1_{i}", [P, D]) for i in range(NB)]
        y2 = [p.sb(f"y2_{i}", [P, D]) for i in range(NB)]
        res = [p.sb(f"res{i}", [P, D]) for i in range(NB)]
        junk = p.sb("junk3", [P, D])
        ss, sd, rr = (p.sb(n, [P, TB]) for n in ("ss3", "sd3", "rr3"))
        s_g1 = [p.sem(f"c_first_rows{i}") for i in range(NB)]
        s_g2 = [p.sem(f"c_second_rows{i}") for i in range(NB)]
        s_first, s_sum, s_sq, s_std, s_rec, s_scaled, s_out = (p.sem(n) for n in (
            "c_first_weighted", "c_summed", "c_squared", "c_std", "c_reciprocal", "c_scaled", "c_result"))
        s_store = [p.sem(f"c_stored{i}") for i in range(NB)]
        with nc.Block() as block:

            @block.gpsimd
            def _(pool):
                for i in range(TB):
                    b = i % NB
                    if i >= NB:
                        pool.wait_ge(s_sum, i - NB + 1)
                    pool.dma_start(y1[b][:, :], t.y[i * P:(i + 1) * P, :]).then_inc(s_g1[b], 16)
                    pool.dma_start(y2[b][:, :], t.y[S + i * P:S + (i + 1) * P, :]).then_inc(s_g2[b], 16)

            @block.scalar
            def _(act):
                for i in range(TB):
                    b = i % NB
                    act.wait_ge(s_g1[b], 16 * (i // NB + 1))
                    act.activation(y1[b][:, :], y1[b][:, :], ACT.Copy, scale=t.weight[:, 0, i:i + 1]).then_inc(s_first, 1)
                    act.wait_ge(s_sum, i + 1)
                    if i:
                        act.wait_ge(s_sq, i)
                    act.activation(junk[:, :], res[b][:, :], ACT.Square, accum_out=ss[:, i:i + 1]).then_inc(s_sq, 1)
                    act.wait_ge(s_sq, i + 1)
                    act.activation(sd[:, i:i + 1], ss[:, i:i + 1], ACT.Sqrt, scale=1.0 / D, bias=t.eps[:, :]).then_inc(s_std, 1)

            @block.vector
            def _(dve):
                for i in range(TB):
                    b = i % NB
                    dve.wait_ge(s_first, i + 1)
                    dve.wait_ge(s_g2[b], 16 * (i // NB + 1))
                    if i >= NB:
                        dve.wait_ge(s_store[b], 16 * (i // NB))
                    dve.scalar_tensor_tensor(out=res[b][:, :], in0=y2[b][:, :], scalar=t.weight[:, 1, i:i + 1], in1=y1[b][:, :],
                                             op0=ALU.mult, op1=ALU.add).then_inc(s_sum, 1)
                    dve.wait_ge(s_std, i + 1)
                    dve.reciprocal(rr[:, i:i + 1], sd[:, i:i + 1]).then_inc(s_rec, 1)
                    dve.wait_ge(s_rec, i + 1)
                    dve.scalar_tensor_tensor(out=res[b][:, :], in0=res[b][:, :], scalar=rr[:, i:i + 1], in1=t.row["gate_ffn"][:, :],
                                             op0=ALU.mult, op1=ALU.mult).then_inc(s_scaled, 1)
                    dve.wait_ge(s_scaled, i + 1)
                    dve.tensor_tensor(res[b][:, :], res[b][:, :], t.x1[:, i, :], ALU.add).then_inc(s_out, 1)

            @block.sync
            def _(sp):
                for i in range(TB):
                    sp.wait_ge(s_out, i + 1)
                    sp.dma_start(out[0, i * P:(i + 1) * P, :], res[i % NB][:, :]).then_inc(s_store[i % NB], 16)
                for b in range(NB):
                    sp.wait_ge(s_store[b], 16 * (TB // NB))


def kernel_program(nc, a, out):
    with ExitStack() as ctx:
        p = Names(nc, ctx)

        class T:
            pass
        t = T()
        t.consts = p.sb("consts_sb", [P, C_END])
        t.ident = t.consts[:, C_IDENT:C_IDENT + P]
        t.rot = t.consts[:, C_ROT:C_ROT + P]
        t.ident_bf = p.sb("ident_bf", [P, P], BF16)
        t.before_bf = p.sb("before_bf", [P, P], BF16)
        t.ones_bf = p.sb("ones_bf", [P, P], BF16)
        t.mask = {k: p.sb(f"mask_{k}", [P, P], BF16) for k in ("diff", "fox")}
        t.eps = p.sb("eps", [P, 1])
        t.subln = p.sb("subln", [P, 1])
        t.bforget = p.sb("bforget", [FOX_HEADS, 1])
        t.neg_lambda = p.sb("neg_lambda", [P, 1])
        t.attn_gain = p.sb("attn_gain", [P, KT])
        t.attn_shift = p.sb("attn_shift", [P, KT])
        t.mixed = nc.dram_tensor("mixed_d", (S, D), F32, kind="Internal").ap()
        t.neg_f = nc.dram_tensor("neg_f_d", (FOX_HEADS, S), F32, kind="Internal").ap()
        t.row_dram = nc.dram_tensor("mod_rows_d", (len(ROWS), D), F32, kind="Internal").ap()
        t.h2 = nc.dram_tensor("h2_d", (S, D), F32, kind="Internal").ap()
        t.y = nc.dram_tensor("y_d", (2 * S + P, D), F32, kind="Internal").ap()
        t.hi, t.lo = ({kind: [nc.dram_tensor(f"{'qk'[part]}_{n}_{kind}_d", (UNITS * P, S), F32, kind="Internal").ap()
                              for part in range(2)] for kind in ("diff", "fox")} for n in ("hi", "lo"))
        t.v = {kind: nc.dram_tensor(f"v_{kind}_d", (UNITS * P, TB * P), F32, kind="Internal").ap() for kind in ("diff", "fox")}
        with ExitStack() as inner:
            with ExitStack() as first:
                t.hT = first.enter_context(nc.sbuf_tensor("hT", [P, KT, S], F32, side="right"))
                modulate(nc, a, t)
                h = Names(nc, inner)
                t.h_hi, t.h_lo = (h.sb(n, [P, KT, S], F32R) for n in ("h_hi", "h_lo"))
                split(nc, a, t)
            project(nc, a, t)
        attend(nc, a, t, "diff")
        attend(nc, a, t, "fox")
        t.logits = p.sb("logits", [P, TB, LOGITS])
        t.weight = p.sb("weight", [P, 2, TB])
        t.cum_blocks = p.sb("cum_blocks", [P, EXPERTS + 2], I32)
        t.cum_prev = p.sb("cum_prev", [P, EXPERTS], I32)
        t.slot = p.sb("slot", [P, TABLE], I32)
        t.loads = p.sb("loads", [P, 2, TABLE], I32)
        t.ids = p.sb("ids", [P, TABLE], U32)
        t.rows = p.sb("rows", [P, TABLE], U32)
        t.x1 = p.sb("x1", [P, TB, D])
        t.row = {name: p.sb(name, [P, D]) for name in ROWS}
        with ExitStack() as inner:
            q = Names(nc, inner, "ex_")
            t.weights = q.sb("weights", [P, 2, EXPERT_WORDS])
            t.s_w = {n: [q.sem(f"{n}_loaded{i}") for i in range(2)] for n in ("w_gate", "w_up", "w_down")}
            merge(nc, a, t)
            route(nc, a, t)
            experts(nc, a, t)
        combine(nc, a, t, out)


_INS = ["x", "c", "w_ada", "b_ada", "g_pre_attn", "g_post_attn", "w_in", "b_forget", "lambda_q1", "lambda_k1",
        "lambda_q2", "lambda_k2", "g_diff_subln", "w_out", "g_pre_ffn", "g_post_ffn", "w_group", "b_group",
        "w_router", "b_router", "w_gate", "w_up", "w_down"]


def _constants():
    import numpy as np
    inv = (1.0 / (10000.0 ** (np.arange(0, HD, 2, dtype=np.float32) / np.float32(HD)))).astype(np.float32)
    ang = (np.arange(S, dtype=np.float32)[:, None] * inv[None, :]).astype(np.float32)
    reps = (P // (HD // 2), 1)
    cos = np.ascontiguousarray(np.tile(np.cos(ang).astype(np.float32).T, reps))
    sin = np.ascontiguousarray(np.tile(np.sin(ang).astype(np.float32).T, reps))
    k = np.zeros((P, C_END), np.float32)
    at = np.arange(P)
    k[:, C_IDENT:C_IDENT + P] = np.eye(P)
    for m in range(P):
        first = m % HD < HD // 2
        k[m + HD // 2 if first else m - HD // 2, C_ROT + m] = -1.0 if first else 1.0
    k[:, C_BEFORE:C_BEFORE + P] = at[:, None] < at[None, :]
    k[:, C_MASKD:C_MASKD + P] = -1e30 * (at[None, :] // 64 > at[:, None] // 64)
    k[:, C_MASKF:C_MASKF + P] = -1e30 * (at[None, :] > at[:, None])
    k[:, C_IOTA:C_IOTA + P] = at[None, :]
    k[:, C_GDESC:C_GDESC + GROUPS] = np.arange(GROUPS, 0, -1)
    k[:, C_EDESC:C_EDESC + PER_GROUP] = np.arange(PER_GROUP, 0, -1)
    k[:, C_TOKEN:C_TOKEN + TB] = np.arange(TB)[None, :] * P + at[:, None]
    k[:, C_TRASH] = 2 * S + 1 + at
    return {"consts": k, "zeros": np.zeros((P, P - FOX_HEADS), np.float32), "rope_cos": cos, "rope_sin": sin}


def kernel(**inputs):
    import numpy as np
    import concourse.bacc as bacc
    from concourse.bass_utils import run_bass_kernel_spmd

    nc = bacc.Bacc("TRN2", target_bir_lowering=False, num_devices=1)
    arrays, args = {}, {}
    for name, x in {**{n: inputs[n] for n in _INS}, **_constants()}.items():
        x = np.ascontiguousarray(x)
        arrays[f"in_{name}"] = x
        args[name] = nc.dram_tensor(f"in_{name}", x.shape, mybir.dt.from_np(x.dtype), kind="ExternalInput").ap()
    out = nc.dram_tensor("out_0", (1, S, D), F32, kind="ExternalOutput").ap()
    kernel_program(nc, args, out)
    r = run_bass_kernel_spmd(nc, [arrays], core_ids=[0])
    return r.results[0]["out_0"]
```

```python
from contextlib import ExitStack

import concourse.bass as bass
from concourse import mybir

P = 128
D = 1024
KT = D // P
S = 2048
TB = S // P
HD = 64
UNITS = 4
GROUPS = 4
PER_GROUP = 8
EXPERTS = GROUPS * PER_GROUP
LOGITS = GROUPS + EXPERTS
F = D // 2
FT = F // P
BANK = 512
CH = S // BANK
TPB = BANK // P
MAX_BLOCKS = 2 * S // P + EXPERTS
TABLE = MAX_BLOCKS + 2
EPS = 1e-6
LAMBDA_INIT = 0.2
QK_SCALE = HD ** -0.5
BIG = 3.0e38
COL = {"diff": (0, 512, 1024), "fox": (1536, 2048, 2560), "forget": 3072}
FOX_HEADS = 8
C_IDENT, C_ROT, C_BEFORE, C_MASKD, C_MASKF, C_IOTA, C_GDESC, C_EDESC, C_TOKEN, C_TRASH, C_END = (
    0, 128, 256, 384, 512, 640, 768, 772, 780, 796, 797)

ALU = mybir.AluOpType
ACT = mybir.ActivationFunctionType
F32 = mybir.dt.float32
F32R = mybir.dt.float32r
BF16 = mybir.dt.bfloat16
I32 = mybir.dt.int32
U32 = mybir.dt.uint32
X = mybir.AxisListType.X


W_GATE, W_UP, W_DOWN, EXPERT_WORDS = 0, KT * F, 2 * KT * F, 2 * KT * F + FT * D


UNIT_PIECES = 26
ROWS = ("gate_attn", "ffn_gain", "ffn_shift", "gate_ffn")


class Steps:

    def __init__(self, eng, sem):
        self.eng, self.sem, self.n, self.base = eng, sem, 0, 0

    def link(self, ins):
        ins.then_inc(self.sem, 1)
        self.n += 1
        self.eng.wait_ge(self.sem, self.base + self.n)


class Names:

    def __init__(self, nc, ctx, prefix=""):
        self.nc, self.ctx, self.prefix = nc, ctx, prefix

    def sb(self, name, shape, dt=F32):
        return self.ctx.enter_context(self.nc.sbuf_tensor(self.prefix + name, shape, dt))

    def ps(self, name, shape, dt=F32):
        return self.ctx.enter_context(self.nc.psum_tensor(self.prefix + name, shape, dt))

    def sem(self, name):
        return self.ctx.enter_context(self.nc.semaphore(self.prefix + name))


def modulate(nc, a, t):
    with ExitStack() as ctx:
        p = Names(nc, ctx, "mod_")
        NP = 6 * D // BANK
        RING = 2
        w_ada = [p.sb(f"w_ada{i}", [P, KT, BANK]) for i in range(RING)]
        b_ada = [p.sb(f"b_ada{i}", [P, BANK]) for i in range(RING)]
        xs = p.sb("xs", [P, TB, D])
        ccol = p.sb("ccol", [P, KT])
        cact = p.sb("cact", [P, KT])
        cwide = p.sb("cwide", [P, KT, P])
        gcol = p.sb("gcol", [P, KT])
        tmprow = p.sb("tmprow", [P, D])
        summed = p.sb("summed", [P, 2, BANK])
        ssq = p.sb("ssq", [P, TB])
        std = p.sb("std", [P, TB])
        rstd = p.sb("rstd", [P, TB])
        lamrow = p.sb("lamrow", [1, 4, HD])
        lamprod = p.sb("lamprod", [1, 2, HD])
        lamsum = p.sb("lamsum", [1, 2])
        lamexp = p.sb("lamexp", [1, 2])
        lamone = p.sb("lamone", [1, 1])
        onerow = p.sb("onerow", [1, P])
        squares = p.sb("squares", [P, D])
        modp = [p.ps(f"modp{i}", [P, BANK]) for i in range(2)]
        colp = p.ps("colp", [P, 2, P])
        lamp = p.ps("lamp", [P, 1])
        xtp = [p.ps(f"xtp{i}", [P, BANK]) for i in range(4)]
        s_small = p.sem("small_loaded")
        s_w = [p.sem(f"w_ada_loaded{i}") for i in range(RING)]
        s_x = [p.sem(f"x_loaded{i}") for i in range(4)]
        s_cact = p.sem("c_activated")
        s_cwide = p.sem("c_widened")
        s_mod = p.sem("mod_product")
        s_sum = p.sem("mod_summed")
        s_modrow = p.sem("mod_row_done")
        s_tr = p.sem("mod_transposed")
        s_col = p.sem("mod_column_done")
        s_sq = p.sem("x_squared")
        s_std = p.sem("std_done")
        s_xn = p.sem("x_normalised")
        s_xt = p.sem("x_transposed")
        s_hta = p.sem("hT_by_act")
        s_htv = p.sem("hT_by_dve")
        s_lam = p.sem("lambda_steps")
        s_lamexp = p.sem("lambda_exponentials")
        s_lamb = p.sem("lambda_broadcast")
        s_const = p.sem("constants_made")
        s_dve = p.sem("dve_steps")
        mod_of = {0: "sh_a", 1: "sc_a", 2: "gt_a", 3: "sh_f", 4: "sc_f", 5: "gt_f"}
        row = {name: p.sb(name, [P, D]) for name in ROWS}
        rows = {"sh_a": tmprow, "sc_a": tmprow, "gt_a": row["gate_attn"], "sh_f": row["ffn_shift"],
                "sc_f": row["ffn_gain"], "gt_f": row["gate_ffn"]}
        s_rows = p.sem("rows_stored")
        NSMALL = 12

        def turned_with(n):
            each = 4 * KT // (NP - 4)
            return range((n - 4) * each, (n - 3) * each)

        with nc.Block() as block:

            @block.sync
            def _(sp):
                sp.dma_start(t.consts[:, :], a["consts"]).then_inc(s_small, 16)
                sp.dma_start(ccol[:, :], a["c"].rearrange("a (k p) -> p (a k)", p=P),
                             allow_slow_non_contiguous=True).then_inc(s_small, 16)
                sp.dma_start(gcol[:, :], a["g_pre_attn"].rearrange("a (k p) -> p (a k)", p=P),
                             allow_slow_non_contiguous=True).then_inc(s_small, 16)
                sp.dma_start(t.subln[:, :], a["g_diff_subln"].rearrange("a p -> p a"),
                             allow_slow_non_contiguous=True).then_inc(s_small, 16)
                for dst, name in ((row["gate_attn"], "g_post_attn"), (row["ffn_gain"], "g_pre_ffn"),
                                  (row["gate_ffn"], "g_post_ffn")):
                    sp.dma_start(dst[:, :], a[name].to_broadcast([P, D])).then_inc(s_small, 16)
                for i, name in enumerate(("lambda_q1", "lambda_q2", "lambda_k1", "lambda_k2")):
                    sp.dma_start(lamrow[:, i, :], a[name]).then_inc(s_small, 16)
                sp.dma_start(t.bforget[:, :], a["b_forget"].rearrange("a h -> h a"),
                             allow_slow_non_contiguous=True).then_inc(s_small, 16)
                for n in range(NP):
                    if n >= RING:
                        sp.wait_ge(s_mod, n - RING + 1)
                        sp.wait_ge(s_sum, n - RING + 1)
                    cols = slice(n * BANK, (n + 1) * BANK)
                    sp.dma_start(w_ada[n % RING][:, :, :],
                                 a["w_ada"][0, :, cols].rearrange("(k p) n -> p k n", p=P)).then_inc(s_w[n % RING], 16)
                    sp.dma_start(b_ada[n % RING][:, :],
                                 a["b_ada"][:, cols].to_broadcast([P, BANK])).then_inc(s_w[n % RING], 16)
                sp.wait_ge(s_modrow, NP)
                for i, name in enumerate(ROWS):
                    sp.dma_start(t.row_dram[i:i + 1, :], row[name][0:1, :]).then_inc(s_rows, 16)
                sp.wait_ge(s_rows, 16 * len(ROWS))

            @block.scalar
            def _(act):
                for i in range(4):
                    if i < 2:
                        act.wait_ge(s_w[i], 32)
                    act.dma_start(xs[:, 4 * i:4 * i + 4, :],
                                  a["x"][0].rearrange("(t p) d -> p t d", p=P)[:, 4 * i:4 * i + 4, :]).then_inc(s_x[i], 16)
                act.wait_ge(s_small, 16 * NSMALL)
                act.activation(cact[:, :], ccol[:, :], ACT.Silu).then_inc(s_cact, 1)
                act.wait_ge(s_lam, 2)
                act.activation(lamexp[:, :], lamsum[:, :], ACT.Exp).then_inc(s_lamexp, 1)
                for i in range(TB):
                    if i % 4 == 0:
                        act.wait_ge(s_x[i // 4], 16)
                    if i:
                        act.wait_ge(s_sq, i)
                    act.activation(squares[:, :], xs[:, i, :], ACT.Square, accum_out=ssq[:, i:i + 1]).then_inc(s_sq, 1)
                act.wait_ge(s_sq, TB)
                act.wait_ge(s_const, 1)
                act.activation(std[:, :], ssq[:, :], ACT.Sqrt, scale=1.0 / D, bias=t.eps[:, :]).then_inc(s_std, 1)
                act.wait_ge(s_col, 16)
                for n in range(0, 4 * KT, 2):
                    tg, k = divmod(n, KT)
                    act.wait_ge(s_xt, n + 1)
                    act.activation(t.hT[:, k, tg * BANK:(tg + 1) * BANK], xtp[n % 4][:, :], ACT.Identity,
                                   scale=t.attn_gain[:, k:k + 1], bias=t.attn_shift[:, k:k + 1]).then_inc(s_hta, 1)

            @block.tensor
            def _(pe):
                def turn_x(g):
                    tg, k = divmod(g, KT)
                    if k == 0:
                        pe.wait_ge(s_xn, 4 * tg + 4)
                    if g >= 4:
                        pe.wait_ge(s_hta if g % 2 == 0 else s_htv, (g - 4) // 2 + 1)
                    for j in range(4):
                        mm = pe.transpose(xtp[g % 4][:, j * P:(j + 1) * P], xs[:, 4 * tg + j, k * P:(k + 1) * P], t.ident)
                    mm.then_inc(s_xt, 1)

                pe.wait_ge(s_cwide, KT)
                for n in range(NP):
                    pe.wait_ge(s_w[n % RING], 32 * (n // RING + 1))
                    if n >= 2:
                        pe.wait_ge(s_sum, n - 1)
                    for k in range(KT):
                        mm = pe.matmul(modp[n % 2][:, :], cwide[:, k, :], w_ada[n % RING][:, k, :],
                                       start=(k == 0), stop=(k == KT - 1))
                    mm.then_inc(s_mod, 1)
                    if n < 4:
                        pe.wait_ge(s_modrow, n + 1)
                        for j in range(TPB):
                            m = n * TPB + j
                            if m >= 1:
                                pe.wait_ge(s_col, m)
                            pe.transpose(colp[:, 0, :], tmprow[:, (n % 2) * BANK + j * P:(n % 2) * BANK + (j + 1) * P],
                                         t.ident).then_inc(s_tr, 1)
                        if n == 3:
                            pe.wait_ge(s_lam, 4)
                            pe.matmul(lamp[:, :], onerow[:, :], lamone[:, :], start=True, stop=True).then_inc(s_lamb, 1)
                    else:
                        for g in turned_with(n):
                            turn_x(g)

            @block.vector
            def _(dve):
                st = Steps(dve, s_dve)
                dve.memset(t.eps[:, :], EPS).then_inc(s_const, 1)
                st.link(dve.memset(cwide[:, :, :], 1.0))
                st.link(dve.memset(onerow[:, :], 1.0))
                dve.wait_ge(s_small, 16 * NSMALL)
                st.link(dve.tensor_copy(t.ident_bf[:, :], t.ident))
                st.link(dve.tensor_copy(t.mask["diff"][:, :], t.consts[:, C_MASKD:C_MASKD + P]))
                st.link(dve.tensor_copy(t.mask["fox"][:, :], t.consts[:, C_MASKF:C_MASKF + P]))
                st.link(dve.tensor_copy(t.before_bf[:, :], t.consts[:, C_BEFORE:C_BEFORE + P]))
                st.link(dve.memset(t.ones_bf[:, :], 1.0))
                st.link(dve.tensor_scalar(t.subln[:, :], t.subln[:, :], 1.0 - LAMBDA_INIT, None, ALU.mult))
                st.link(dve.tensor_tensor(lamprod[:, :, :], lamrow[:, 0:2, :], lamrow[:, 2:4, :], ALU.mult))
                dve.memset(lamsum[:, :], 0.0).then_inc(s_lam, 1)
                dve.wait_ge(s_lam, 1)
                dve.tensor_reduce(lamsum[:, :], lamprod[:, :, :], X, ALU.add).then_inc(s_lam, 1)
                dve.wait_ge(s_lamexp, 1)
                dve.tensor_tensor(lamone[:, :], lamexp[:, 1:2], lamexp[:, 0:1], ALU.subtract).then_inc(s_lam, 1)
                dve.wait_ge(s_lam, 3)
                dve.tensor_scalar(lamone[:, :], lamone[:, :], -LAMBDA_INIT, None, ALU.add).then_inc(s_lam, 1)
                dve.wait_ge(s_cact, 1)
                for k in range(KT):
                    dve.tensor_scalar(cwide[:, k, :], cwide[:, k, :], cact[:, k:k + 1], None, ALU.mult).then_inc(s_cwide, 1)
                for n in range(NP):
                    what = mod_of[n // 2]
                    half = slice((n % 2) * BANK, (n % 2 + 1) * BANK)
                    dve.wait_ge(s_mod, n + 1)
                    if n >= 2:
                        dve.wait_ge(s_modrow, n - 1)
                    dve.tensor_tensor(summed[:, n % 2, :], modp[n % 2][:, :], b_ada[n % RING][:, :], ALU.add).then_inc(s_sum, 1)
                    dve.wait_ge(s_sum, n + 1)
                    dst = rows[what][:, half]
                    if what in ("sh_a", "sh_f"):
                        ins = dve.tensor_copy(dst, summed[:, n % 2, :])
                    elif what == "sc_a":
                        ins = dve.tensor_scalar(dst, summed[:, n % 2, :], 1.0, None, ALU.add)
                    elif what == "sc_f":
                        ins = dve.scalar_tensor_tensor(out=dst, in0=summed[:, n % 2, :], scalar=1.0, in1=dst,
                                                       op0=ALU.add, op1=ALU.mult)
                    else:
                        ins = dve.tensor_tensor(dst, summed[:, n % 2, :], dst, ALU.mult)
                    ins.then_inc(s_modrow, 1)
                    if n < 4:
                        for j in range(TPB):
                            m = n * TPB + j
                            k = m % KT
                            dve.wait_ge(s_tr, m + 1)
                            if n < 2:
                                ins = dve.tensor_copy(t.attn_shift[:, k:k + 1], colp[:, 0, 0:1])
                            else:
                                ins = dve.tensor_tensor(t.attn_gain[:, k:k + 1], colp[:, 0, 0:1], gcol[:, k:k + 1], ALU.mult)
                            ins.then_inc(s_col, 1)
                    if n == 3:
                        dve.wait_ge(s_std, 1)
                        st.link(dve.reciprocal(rstd[:, :], std[:, :]))
                        for i in range(TB):
                            dve.tensor_scalar(xs[:, i, :], xs[:, i, :], rstd[:, i:i + 1], None, ALU.mult).then_inc(s_xn, 1)
                        dve.wait_ge(s_lamb, 1)
                        st.link(dve.tensor_copy(t.neg_lambda[:, :], lamp[:, :]))
                        dve.wait_ge(s_col, 4 * TPB)
                    if n >= 4:
                        for g in turned_with(n):
                            if g % 2:
                                tg, k = divmod(g, KT)
                                dve.wait_ge(s_xt, g + 1)
                                dve.tensor_scalar(t.hT[:, k, tg * BANK:(tg + 1) * BANK], xtp[g % 4][:, :],
                                                  t.attn_gain[:, k:k + 1], t.attn_shift[:, k:k + 1], ALU.mult, ALU.add
                                                  ).then_inc(s_htv, 1)


def split(nc, a, t):
    with ExitStack() as ctx:
        p = Names(nc, ctx, "spl_")
        s_hi, s_lo = p.sem("hT_hi"), p.sem("hT_lo")
        with nc.Block() as block:

            @block.scalar
            def _(act):
                for k in range(KT):
                    act.activation(t.h_hi[:, k, :], t.hT[:, k, :], ACT.Copy).then_inc(s_hi, 1)

            @block.vector
            def _(dve):
                for k in range(KT):
                    dve.wait_ge(s_hi, k + 1)
                    dve.tensor_tensor(t.h_lo[:, k, :], t.hT[:, k, :], t.h_hi[:, k, :].bitcast(F32), ALU.subtract).then_inc(s_lo, 1)


def project(nc, a, t):
    with ExitStack() as ctx:
        p = Names(nc, ctx, "prj_")
        H = FOX_HEADS
        h_hi, h_lo = t.h_hi, t.h_lo
        w_raw = p.sb("w_raw", [P, KT, P])
        w_lo = [p.sb(f"w_lo{i}", [P, KT, P], F32R) for i in range(3)]
        w_hi = [p.sb(f"w_hi{i}", [P, KT, P], F32R) for i in range(3)]
        cos = p.sb("cos", [P, S])
        sin = p.sb("sin", [P, S])
        raw = [p.sb(f"raw{i}", [P, BANK]) for i in range(2)]
        rsin = [p.sb(f"rsin{i}", [P, BANK]) for i in range(2)]
        hi = [p.sb(f"hi{i}", [P, BANK], F32R) for i in range(2)]
        lo = [p.sb(f"lo{i}", [P, BANK], F32R) for i in range(2)]
        full = [p.sb(f"full{i}", [P, BANK]) for i in range(2)]
        z = [p.sb(f"z{i}", [H, BANK]) for i in range(2)]
        ez = [p.sb(f"ez{i}", [H, BANK]) for i in range(2)]
        ones = p.sb("scan_ones", [H, 1])
        acc = [p.ps(f"acc{i}", [P, BANK]) for i in range(4)]
        tp_ = [p.ps(f"tposed{i}", [P, BANK]) for i in range(2)]
        names = ("rope_loaded weights_loaded weights_hi weights_lo projected copied rotated sin_part cos_part roped "
                 "chunk_hi chunk_lo v_turned v_copied forget_loaded forget_hi forget_lo "
                 "forget_product forget_dve forget_act").split()
        s = {n: p.sem(n) for n in names}
        s_store = [p.sem(f"chunk_stored{i}") for i in range(2)]
        s_vstore = [p.sem(f"v_stored{i}") for i in range(2)]
        s_fstore = [p.sem(f"neg_f_stored{i}") for i in range(2)]
        NPROJ, NQK = 3 * CH, 2 * CH
        ALL = 2 * UNITS
        FSTEPS = 6

        def units(eng, body):
            for kind, base in (("diff", 0), ("fox", UNITS)):
                with eng.Fori(0, UNITS - 1) as u:
                    body(kind, u, u + base, (kind, u + 1))
                body(kind, UNITS - 1, UNITS - 1 + base, ("fox", 0) if kind == "diff" else None)

        def load_weights(eng, part, kind, u, U):
            eng.wait_ge(s["forget_lo"], 1)
            eng.wait_ge(s["weights_lo"], 3 * U + part)
            eng.dma_start(w_raw[:, :, :], a["w_in"][0, :, bass.ds(u * P + COL[kind][part], P)].rearrange("(k p) n -> p k n", p=P)
                          ).then_inc(s["weights_loaded"], 16)

        def wait_weights_free(eng, part, U):
            if part == 2:
                eng.wait_ge(s["forget_product"], CH)
                eng.wait_ge(s["projected"], U * NPROJ)
            else:
                eng.wait_ge(s["projected"], (U - 1) * NPROJ + (part + 1) * CH)

        def hi_lo_products(pe, bank, w, rhs_cols):
            for k in range(KT):
                for a_, b_ in ((w_hi[w], h_hi), (w_hi[w], h_lo), (w_lo[w], h_hi)):
                    mm = pe.matmul(bank, a_[:, k, :], b_[:, k, rhs_cols],
                                   start=(k == 0 and a_ is w_hi[w] and b_ is h_hi), stop=(k == KT - 1 and a_ is w_lo[w]))
            return mm

        with nc.Block() as block:

            @block.gpsimd
            def _(pool):
                for part in range(2):
                    load_weights(pool, part, "diff", 0, 0)
                pool.dma_start(cos[:, :], a["rope_cos"]).then_inc(s["rope_loaded"], 16)
                pool.dma_start(sin[:, :], a["rope_sin"]).then_inc(s["rope_loaded"], 16)

                def body(kind, u, U, after):
                    for n in range(NPROJ):
                        if n == 0:
                            load_weights(pool, 2, kind, u, U)
                        if n in (CH, 2 * CH) and after:
                            load_weights(pool, n // CH - 1, *after, U + 1)
                        if kind == "diff" and n < NQK:
                            c = slice((n % CH) * BANK, (n % CH + 1) * BANK)
                            if n == 0:
                                pool.wait_ge(s["rope_loaded"], 32)
                            pool.wait_ge(s["copied"], U * NPROJ + n + 1)
                            if n >= 2:
                                pool.wait_ge(s["chunk_lo"], U * NQK + n - 1)
                            else:
                                pool.wait_ge(s_vstore[n % 2], 16 * U * (CH // 2))
                            pool.tensor_tensor(full[n % 2][:, :], raw[n % 2][:, :], cos[:, c], ALU.mult).then_inc(s["cos_part"], 1)

                units(pool, body)

            @block.sync
            def _(sp):
                c = COL["forget"]
                sp.dma_start(w_raw[:, :, H:], a["zeros"].unsqueeze(1).to_broadcast([P, KT, P - H])).then_inc(s["forget_loaded"], 16)
                sp.dma_start(w_raw[:, :, 0:H], a["w_in"][0, :, c:c + H].rearrange("(k p) n -> p k n", p=P)).then_inc(s["forget_loaded"], 16)
                for c in range(CH):
                    sp.wait_ge(s["forget_dve"], 1 + FSTEPS * (c + 1))
                    sp.dma_start(t.neg_f[:, c * BANK:(c + 1) * BANK], z[c % 2][:, :]).then_inc(s_fstore[c % 2], 16)

                def body(kind, u, U, after):
                    for n in range(NQK):
                        part, c = divmod(n, CH)
                        cols = slice(c * BANK, (c + 1) * BANK)
                        sp.wait_ge(s["chunk_lo"], U * NQK + n + 1)
                        for dst, src in ((t.hi[part], hi[n % 2][:, :].bitcast(F32)), (t.lo[part], lo[n % 2][:, :].bitcast(F32))):
                            sp.dma_start(dst[bass.ds(U * P, P), cols], src).then_inc(s_store[n % 2], 16)
                    for c in range(CH):
                        sp.wait_ge(s["v_copied"], U * CH + c + 1)
                        sp.dma_start(t.v[bass.ds(U * P, P), c * BANK:(c + 1) * BANK], full[c % 2][:, :]).then_inc(s_vstore[c % 2], 16)

                units(sp, body)
                for b in range(2):
                    sp.wait_ge(s_store[b], 32 * ALL * CH)
                    sp.wait_ge(s_vstore[b], 16 * ALL * CH // 2)
                    sp.wait_ge(s_fstore[b], 16 * CH // 2)

            @block.tensor
            def _(pe):
                pe.wait_ge(s["forget_lo"], 1)
                for c in range(CH):
                    hi_lo_products(pe, acc[c][:, :], 2, slice(c * BANK, (c + 1) * BANK)).then_inc(s["forget_product"], 1)

                def body(kind, u, U, after):
                    def rotate(n):
                        pe.wait_ge(s["copied"], U * NPROJ + n + 1)
                        if n < 2:
                            pe.wait_ge(s["v_copied"], U * CH)
                        else:
                            pe.wait_ge(s["sin_part"], U * NQK + n - 1)
                        pe.matmul(tp_[n % 2][:, :], t.rot, raw[n % 2][:, :], start=True, stop=True).then_inc(s["rotated"], 1)

                    def turn_v(c):
                        pe.wait_ge(s["copied"], U * NPROJ + NQK + c + 1)
                        if c >= 2:
                            pe.wait_ge(s["v_copied"], U * CH + c - 1)
                        else:
                            pe.wait_ge(s["sin_part"], (U + 1) * NQK if kind == "diff" else UNITS * NQK)
                            pe.wait_ge(s["v_copied"], U * CH)
                        for j in range(TPB):
                            mm = pe.transpose(tp_[c % 2][:, j * P:(j + 1) * P], raw[c % 2][:, j * P:(j + 1) * P], t.ident)
                        mm.then_inc(s["v_turned"], 1)

                    for n in range(NPROJ):
                        part, c = divmod(n, CH)
                        if c == 0:
                            pe.wait_ge(s["weights_lo"], 3 * U + part + 1)
                        if n == 0:
                            pe.wait_ge(s["forget_dve"], 2 + FSTEPS * (CH - 1))
                            pe.wait_ge(s["copied"], U * NPROJ)
                        if n >= 4:
                            pe.wait_ge(s["copied"], U * NPROJ + n - 3)
                        hi_lo_products(pe, acc[n % 4][:, :], part, slice(c * BANK, (c + 1) * BANK)).then_inc(s["projected"], 1)
                        if kind == "diff" and 1 <= n <= NQK:
                            rotate(n - 1)
                        if n > NQK:
                            turn_v(n - NQK - 1)
                    turn_v(CH - 1)

                units(pe, body)

            @block.scalar
            def _(act):
                def split_weights(part, U, free=True):
                    act.wait_ge(s["weights_loaded"], 16 * (3 * U + part + 1))
                    if free:
                        wait_weights_free(act, part, U)
                    act.activation(w_hi[part][:, :, :], w_raw[:, :, :], ACT.Copy).then_inc(s["weights_hi"], 1)

                act.wait_ge(s["forget_loaded"], 32)
                act.activation(w_hi[2][:, :, :], w_raw[:, :, :], ACT.Copy).then_inc(s["forget_hi"], 1)
                split_weights(0, 0, free=False)
                split_weights(1, 0, free=False)
                for c in range(CH):
                    act.wait_ge(s["forget_dve"], 1 + FSTEPS * c + 2)
                    act.activation(ez[c % 2][:, :], ez[c % 2][:, :], ACT.Exp).then_inc(s["forget_act"], 1)
                    act.wait_ge(s["forget_dve"], 1 + FSTEPS * c + 3)
                    act.activation(ez[c % 2][:, :], ez[c % 2][:, :], ACT.Ln).then_inc(s["forget_act"], 1)

                def body(kind, u, U, after):
                    for n in range(NPROJ):
                        act.wait_ge(s["projected"], U * NPROJ + n + 1)
                        scale = QK_SCALE if n < CH else 1.0
                        if kind == "diff" or n >= NQK:
                            if n < NQK:
                                if n < 2:
                                    act.wait_ge(s["v_turned"], U * CH)
                                else:
                                    act.wait_ge(s["rotated"], U * NQK + n - 1)
                                    act.wait_ge(s["cos_part"], U * NQK + n - 1)
                            elif n < NQK + 2:
                                done = (U + 1) * NQK if kind == "diff" else UNITS * NQK
                                act.wait_ge(s["rotated"], done)
                                act.wait_ge(s["cos_part"], done)
                                act.wait_ge(s["v_turned"], U * CH)
                            else:
                                act.wait_ge(s["v_turned"], U * CH + n - NQK - 1)
                            act.activation(raw[n % 2][:, :], acc[n % 4][:, :], ACT.Copy, scale=scale).then_inc(s["copied"], 1)
                        else:
                            act.wait_ge(s_store[n % 2], 32 * (U * CH + n // 2))
                            act.activation(hi[n % 2][:, :], acc[n % 4][:, :], ACT.Copy, scale=scale).then_inc(s["chunk_hi"], 1)
                            act.wait_ge(s["chunk_lo"], U * NQK + n + 1)
                            act.sem_inc(s["copied"], 1)
                        if kind == "diff" and 2 <= n < NQK + 2:
                            m = n - 2
                            act.wait_ge(s["roped"], U * NQK + m + 1)
                            act.wait_ge(s_store[m % 2], 32 * (U * CH + m // 2))
                            act.activation(hi[m % 2][:, :], full[m % 2][:, :], ACT.Copy).then_inc(s["chunk_hi"], 1)
                        if n == CH - 1:
                            split_weights(2, U)
                        elif n % CH == CH - 1 and after:
                            split_weights(n // CH - 1, U + 1)

                units(act, body)

            @block.vector
            def _(dve):
                f = s["forget_dve"]

                def split_weights(n_split, part):
                    dve.wait_ge(s["weights_hi"], n_split)
                    dve.tensor_tensor(w_lo[part][:, :, :], w_raw[:, :, :], w_hi[part][:, :, :].bitcast(F32), ALU.subtract
                                      ).then_inc(s["weights_lo"], 1)

                dve.memset(ones[:, :], 1.0).then_inc(f, 1)
                dve.wait_ge(s["forget_hi"], 1)
                dve.tensor_tensor(w_lo[2][:, :, :], w_raw[:, :, :], w_hi[2][:, :, :].bitcast(F32), ALU.subtract).then_inc(s["forget_lo"], 1)
                split_weights(1, 0)
                split_weights(2, 1)
                for c in range(CH):
                    zc, ec = z[c % 2][:, :], ez[c % 2][:, :]
                    base = 1 + FSTEPS * c
                    dve.wait_ge(s["forget_product"], c + 1)
                    if c >= 2:
                        dve.wait_ge(s_fstore[c % 2], 16)
                        dve.wait_ge(f, base)
                    dve.tensor_scalar(zc, acc[c][0:H, :], t.bforget[:, 0:1], None, ALU.add).then_inc(f, 1)
                    dve.wait_ge(f, base + 1)
                    dve.scalar_tensor_tensor(out=ec, in0=zc, scalar=-1.0, in1=zc, op0=ALU.mult, op1=ALU.min).then_inc(f, 1)
                    dve.wait_ge(s["forget_act"], 2 * c + 1)
                    dve.tensor_scalar(ec, ec, 1.0, None, ALU.add).then_inc(f, 1)
                    dve.tensor_scalar(zc, zc, 0.0, None, ALU.min).then_inc(f, 1)
                    dve.wait_ge(f, base + 4)
                    dve.wait_ge(s["forget_act"], 2 * c + 2)
                    dve.tensor_tensor(ec, ec, zc, ALU.subtract).then_inc(f, 1)
                    dve.wait_ge(f, base + 5)
                    start = z[(c - 1) % 2][:, BANK - 1:BANK] if c else 0.0
                    dve.tensor_tensor_scan(zc, ones[:, :].to_broadcast([H, BANK]), ec, start, ALU.mult, ALU.add).then_inc(f, 1)

                def body(kind, u, U, after):
                    def lo_part(n):
                        dve.wait_ge(s["chunk_hi"], U * NQK + n + 1)
                        dve.tensor_tensor(lo[n % 2][:, :], full[n % 2][:, :], hi[n % 2][:, :].bitcast(F32), ALU.subtract
                                          ).then_inc(s["chunk_lo"], 1)

                    for n in range(NPROJ):
                        c = n % CH
                        if kind == "diff" and n < NQK:
                            if n == 0:
                                dve.wait_ge(s["rope_loaded"], 32)
                            dve.wait_ge(s["rotated"], U * NQK + n + 1)
                            if n >= 2:
                                dve.wait_ge(s["roped"], U * NQK + n - 1)
                            else:
                                dve.wait_ge(s["roped"], U * NQK)
                            dve.tensor_tensor(rsin[n % 2][:, :], tp_[n % 2][:, :], sin[:, c * BANK:(c + 1) * BANK], ALU.mult
                                              ).then_inc(s["sin_part"], 1)
                            dve.wait_ge(s["sin_part"], U * NQK + n + 1)
                            dve.wait_ge(s["cos_part"], U * NQK + n + 1)
                            dve.tensor_tensor(full[n % 2][:, :], full[n % 2][:, :], rsin[n % 2][:, :], ALU.add).then_inc(s["roped"], 1)
                            if n:
                                lo_part(n - 1)
                            if n == NQK - 1:
                                lo_part(n)
                        elif n < NQK:
                            dve.wait_ge(s["chunk_hi"], U * NQK + n + 1)
                            dve.scalar_tensor_tensor(out=lo[n % 2][:, :], in0=acc[n % 4][:, :], scalar=QK_SCALE if n < CH else 1.0,
                                                     in1=hi[n % 2][:, :].bitcast(F32), op0=ALU.mult, op1=ALU.subtract
                                                     ).then_inc(s["chunk_lo"], 1)
                        else:
                            dve.wait_ge(s["v_turned"], U * CH + c + 1)
                            dve.wait_ge(s_vstore[c % 2], 16 * (U * (CH // 2) + c // 2))
                            if kind == "diff" and c < 2:
                                dve.wait_ge(s["chunk_lo"], (U + 1) * NQK)
                            dve.tensor_copy(full[c % 2][:, :], tp_[c % 2][:, :]).then_inc(s["v_copied"], 1)
                        if n == CH - 1:
                            split_weights(3 * U + 3, 2)
                        elif n % CH == CH - 1 and after:
                            split_weights(3 * U + 3 + n // CH, n // CH - 1)

                units(dve, body)


def load_unit_piece(eng, t, u, b, n):
    part, n = divmod(n, UNIT_PIECES // 2)
    cols = (slice(0, BANK), slice(BANK, S))[part]
    if n == 12:
        ins = eng.dma_start(t.v_in[b][:, cols], t.v[bass.ds(u * P, P), cols])
    else:
        m, n = divmod(n, 6)
        dst, at, src = ((t.q_hi, 0, t.hi[0]), (t.q_hi, HD, t.hi[0]), (t.q_lo, 0, t.lo[0]),
                        (t.q_lo, HD, t.lo[0]), (t.k_both, 0, t.hi[1]), (t.k_both, HD, t.lo[1]))[n]
        ins = eng.dma_start(dst[b][m][at:at + HD, cols].bitcast(F32), src[bass.ds(u * P + m * HD, HD), cols])
    ins.then_inc(t.s_in[b][part], 16)


def load_negf(eng, t, u):
    for m in range(2):
        eng.dma_start(t.negf[m][:, :], t.neg_f[bass.ds(u * 2 + m, 1), :].to_broadcast([P, S])).then_inc(t.s_negf, 16)


def attend(nc, a, t, kind):
    fox = kind == "fox"
    with ExitStack() as ctx:
        p = Names(nc, ctx, kind + "_")
        AHEAD = 2
        RING = AHEAD + 1
        q_hi, q_lo, k_both, v, negf, s_in = t.q_hi, t.q_lo, t.k_both, t.v_in, t.negf, t.s_in
        prob = [p.sb(f"prob{i}", [P, S]) for i in range(2 * RING)]
        probT = [p.sb(f"probT{i}", [P, TB, P]) for i in range(3)]
        if not fox:
            rden = p.sb("rden", [P, 2, 2])
            ratio = p.sb("ratio", [P, 2])
        low = p.sb("low", [P, 2 * RING, CH])
        den = p.sb("den", [P, 2 * RING])
        rec = p.sb("rec", [P, 4])
        outs = [p.sb(f"outs{i}", [P, P]) for i in range(2)]
        SCORE_BANKS, TURN_BANKS = 3, 3
        sp_ = [p.ps(f"score{i}", [P, BANK]) for i in range(SCORE_BANKS)]
        tp_ = [p.ps(f"tposed{i}", [P, BANK]) for i in range(TURN_BANKS)]
        op_ = [p.ps(f"value{i}", [P, P]) for i in range(2)]
        s_hold_sp = p.sem("hold_sp")
        if fox:
            s_rec, s_tcv, s_hold = (p.sem(n) for n in ("reciprocals", "transpose_copied_dve", "hold_dve"))
        else:
            s_comb = p.sem("combine_steps")
        s_negf = t.s_negf
        s_score = p.sem("scored")
        s_scopy = p.sem("score_copied")
        s_exp = p.sem("exponentials")
        s_tr = p.sem("transposed")
        s_tca = p.sem("transpose_copied_act")
        s_val = p.sem("values_done")
        s_ocopy = p.sem("output_copied")
        s_store = [p.sem(f"output_stored{i}") for i in range(2)]

        def chunks(i):
            return i // TPB + 1
        def width(i, c):
            return min(BANK, (i + 1) * P - c * BANK)
        def ring(i, m):
            return (i % RING) * 2 + m
        jobs = [(i, m) for i in range(TB) for m in range(2)]
        first_chunk = {}
        n = 0
        for j in jobs:
            first_chunk[j] = n
            n += chunks(j[0])
        NSC = n
        tjobs = jobs if fox else [(i, 0) for i in range(TB)]
        first_group = {}
        n = 0
        for j in tjobs:
            first_group[j] = n
            n += chunks(j[0])
        NTG = n
        NTJ = len(tjobs)
        def by_dve(g):
            return fox and g % 2 == 1
        A_T = sum(not by_dve(g) for g in range(NTG))
        V_T = NTG - A_T
        def copies_before(g, dve):
            return sum(by_dve(x) == dve for x in range(g))
        PER_COMB = 3
        BEFORE = UNITS // 2 if fox else 0

        def scores_of(i):
            return [("score", i, m, c) for m in range(2) for c in range(chunks(i))] if i < TB else []

        def order(i):
            groups = [(i, m, c) for m in range(2 if fox else 1) for c in range(chunks(i))]
            depth = TURN_BANKS - 1
            mine = [("turn", *group) for group in groups[:depth]]
            for g, group in enumerate(groups):
                if g + depth < len(groups):
                    mine.append(("turn", *groups[g + depth]))
                mine.append(("value", *group))
            ahead = scores_of(i + AHEAD)
            steps = []
            for x, step in enumerate(mine):
                steps.append(step)
                steps += ahead[len(ahead) * x // len(mine):len(ahead) * (x + 1) // len(mine)]
            return steps

        def units(eng, body):
            with eng.Fori(0, UNITS // 2) as pair:
                for b in range(2):
                    body(pair * 2 + b, b, pair)

        with nc.Block() as block:

            @block.gpsimd
            def _(pool):
                if not fox:
                    load_negf(pool, t, 0)
                else:
                    with pool.Fori(1, UNITS) as u:
                        pool.wait_ge(s_scopy, u * NSC)
                        load_negf(pool, t, u)

            @block.sync
            def _(sp):
                def store(u, following, slot):
                    for i in range(TB):
                        if i == 0:
                            sp.wait_ge(s_val, u * NTJ)
                        for n in range(2 * i, min(2 * i + 2, UNIT_PIECES)):
                            if following is not None:
                                load_unit_piece(sp, t, following, slot, n)
                        sp.wait_ge(s_ocopy, u * NTJ + (2 * i + 2 if fox else i + 1))
                        sp.sem_inc(s_hold_sp, 1)
                        c = 0 if not fox else UNITS * P
                        sp.dma_start(t.mixed[i * P:(i + 1) * P, bass.ds(u * P + c, P)], outs[i % 2][:, :]).then_inc(s_store[i % 2], 16)

                if not fox:
                    for n in range(UNIT_PIECES):
                        load_unit_piece(sp, t, 0, 0, n)
                with sp.Fori(0, UNITS // 2 - (1 if fox else 0)) as pair:
                    for b in range(2):
                        store(pair * 2 + b, pair * 2 + (b + 1 + 2 * BEFORE), 1 - b)
                if fox:
                    store(UNITS - 2, 2 * UNITS - 1, 1)
                    store(UNITS - 1, None, 0)
                for b in range(2):
                    sp.wait_ge(s_store[b], 16 * UNITS * TB // 2)

            @block.tensor
            def _(pe):
                def body(u, b, pair):
                    def score(i, m, c):
                        n = first_chunk[i, m] + c
                        if n == 0:
                            pe.wait_ge(s_in[b][0], (pair + (BEFORE + 1)) * (8 * UNIT_PIECES))
                            pe.wait_ge(s_scopy, u * NSC)
                        elif n >= SCORE_BANKS:
                            pe.wait_ge(s_scopy, u * NSC + n - SCORE_BANKS + 1)
                        if n == first_chunk[TPB, 0]:
                            pe.wait_ge(s_in[b][1], (pair + (BEFORE + 1)) * (8 * UNIT_PIECES))
                        wd = width(i, c)
                        wide = max(wd, 2 * P)
                        rows, cols = slice(i * P, (i + 1) * P), slice(c * BANK, c * BANK + wide)
                        last = c == chunks(i) - 1
                        pe.matmul(sp_[n % SCORE_BANKS][:, 0:wide], q_hi[b][m][:, rows], k_both[b][m][:, cols], start=True, stop=False)
                        mm = pe.matmul(sp_[n % SCORE_BANKS][:, 0:wide], q_lo[b][m][:, rows], k_both[b][m][:, cols], start=False, stop=not last)
                        if last:
                            mm = pe.matmul(sp_[n % SCORE_BANKS][:, wd - P:wd], t.ident_bf[:, :], t.mask[kind][:, :], start=False, stop=True)
                        mm.then_inc(s_score, 1)

                    def group_copied(g):
                        if by_dve(g):
                            pe.wait_ge(s_tcv, u * V_T + copies_before(g, True) + 1)
                        else:
                            pe.wait_ge(s_tca, u * A_T + copies_before(g, False) + 1)

                    def turn(i, m, c):
                        g = first_group[i, m] + c
                        if c == 0:
                            if fox:
                                pe.wait_ge(s_exp, u * 2 * TB + 2 * i + m + 1)
                            else:
                                pe.wait_ge(s_comb, u * TB * PER_COMB + (i + 1) * PER_COMB)
                        if g >= TURN_BANKS:
                            group_copied(g - TURN_BANKS)
                        for k in range(c * TPB, min((c + 1) * TPB, i + 1)):
                            mm = pe.transpose(tp_[g % TURN_BANKS][:, (k % TPB) * P:(k % TPB + 1) * P], prob[ring(i, m)][:, k * P:(k + 1) * P], t.ident)
                        mm.then_inc(s_tr, 1)

                    def value(i, m, c):
                        group_copied(first_group[i, m] + c)
                        n = tjobs.index((i, m))
                        if c == 0 and n >= 2:
                            pe.wait_ge(s_ocopy, u * NTJ + n - 1)
                        cols = slice(HD * m, HD * m + HD) if fox else slice(0, P)
                        o = op_[n % 2][:, 0:HD] if fox else op_[n % 2][:, :]
                        for k in range(c * TPB, min((c + 1) * TPB, i + 1)):
                            mm = pe.matmul(o, probT[n % 3][:, k, :], v[b][:, k * P + cols.start:k * P + cols.stop], start=(k == 0), stop=(k == i))
                        if c == chunks(i) - 1:
                            mm.then_inc(s_val, 1)

                    do = {"score": score, "turn": turn, "value": value}
                    for i in range(AHEAD):
                        for step in scores_of(i):
                            score(*step[1:])
                    for i in range(TB):
                        for step in order(i):
                            do[step[0]](*step[1:])

                units(pe, body)

            @block.scalar
            def _(act):
                def body(u, b, pair):
                    def exps(i, m):
                        r = ring(i, m)
                        act.wait_ge(s_scopy, u * NSC + first_chunk[i, m] + chunks(i))
                        act.activation(prob[r][:, 0:(i + 1) * P], prob[r][:, 0:(i + 1) * P], ACT.Exp, scale=-1.0,
                                       bias=low[:, r, chunks(i) - 1:chunks(i)],
                                       accum_out=den[:, r:r + 1]).then_inc(s_exp, 1)

                    def copy(i, m, c):
                        n = tjobs.index((i, m))
                        g = first_group[i, m] + c
                        if not by_dve(g):
                            act.wait_ge(s_tr, u * NTG + g + 1)
                            lo, hi = c * TPB, min((c + 1) * TPB, i + 1)
                            act.activation(probT[n % 3][:, lo:hi, :], tp_[g % TURN_BANKS][:, 0:(hi - lo) * P].rearrange("p (b n) -> p b n", n=P),
                                           ACT.Copy).then_inc(s_tca, 1)

                    for i in range(AHEAD):
                        exps(i, 0)
                        if i + 1 < AHEAD:
                            exps(i, 1)
                    for i in range(TB):
                        for x, (what, *step) in enumerate(order(i)):
                            if what == "turn":
                                copy(*step)
                            if x == 0 and i + AHEAD - 1 < TB:
                                exps(i + AHEAD - 1, 1)
                            if what == "score" and step[1:] == [0, chunks(step[0]) - 1]:
                                exps(step[0], 0)

                units(act, body)

            @block.vector
            def _(dve):
                def body(u, b, pair):
                    def copy_score(i, m, c):
                        r = ring(i, m)
                        n = first_chunk[i, m] + c
                        wd = width(i, c)
                        dve.wait_ge(s_score, u * NSC + n + 1)
                        if c:
                            dve.wait_ge(s_scopy, u * NSC + n)
                        init = low[:, r, c - 1:c] if c else BIG
                        if fox:
                            if n == 0:
                                dve.wait_ge(s_negf, (u + 1) * 32)
                            dve.sem_inc(s_hold, 1)
                            ins = dve.tensor_tensor_reduce(out=prob[r][:, c * BANK:c * BANK + wd], in0=sp_[n % SCORE_BANKS][:, 0:wd],
                                                           in1=negf[m][:, c * BANK:c * BANK + wd], scale=-1.0, scalar=init,
                                                           op0=ALU.add, op1=ALU.min, accum_out=low[:, r, c:c + 1])
                        else:
                            ins = dve.tensor_scalar(prob[r][:, c * BANK:c * BANK + wd], sp_[n % SCORE_BANKS][:, 0:wd], -1.0, init,
                                                    ALU.mult, ALU.min, accum_out=low[:, r, c:c + 1])
                        ins.then_inc(s_scopy, 1)

                    def combine(i):
                        q = ring(i, 0)
                        r = i % 2
                        base = u * TB * PER_COMB + i * PER_COMB
                        dve.wait_ge(s_exp, u * 2 * TB + 2 * i + 2)
                        dve.reciprocal(rden[:, r, :], den[:, q:q + 2]).then_inc(s_comb, 1)
                        dve.wait_ge(s_comb, base + 1)
                        dve.scalar_tensor_tensor(out=ratio[:, r:r + 1], in0=rden[:, r, 1:2], scalar=den[:, q:q + 1],
                                                 in1=t.neg_lambda[:, :], op0=ALU.mult, op1=ALU.mult).then_inc(s_comb, 1)
                        dve.wait_ge(s_comb, base + 2)
                        dve.scalar_tensor_tensor(out=prob[q][:, 0:(i + 1) * P], in0=prob[q + 1][:, 0:(i + 1) * P],
                                                 scalar=ratio[:, r:r + 1], in1=prob[q][:, 0:(i + 1) * P],
                                                 op0=ALU.mult, op1=ALU.add).then_inc(s_comb, 1)

                    def copy(i, m, c):
                        n = tjobs.index((i, m))
                        g = first_group[i, m] + c
                        if by_dve(g):
                            dve.wait_ge(s_tr, u * NTG + g + 1)
                            lo, hi = c * TPB, min((c + 1) * TPB, i + 1)
                            dve.tensor_copy(probT[n % 3][:, lo:hi, :],
                                            tp_[g % TURN_BANKS][:, 0:(hi - lo) * P].rearrange("p (b n) -> p b n", n=P)).then_inc(s_tcv, 1)

                    def output(i, m):
                        n = tjobs.index((i, m))
                        if m == 0:
                            dve.wait_ge(s_store[i % 2], u * (16 * TB // 2) + 16 * (i // 2))
                        if fox:
                            q = n % 4
                            r = ring(i, m)
                            dve.wait_ge(s_exp, u * 2 * TB + 2 * i + m + 1)
                            dve.reciprocal(rec[:, q:q + 1], den[:, r:r + 1]).then_inc(s_rec, 1)
                            dve.wait_ge(s_rec, u * 2 * TB + 2 * i + m + 1)
                            dve.wait_ge(s_val, u * NTJ + n + 1)
                            dve.tensor_scalar(outs[i % 2][:, HD * m:HD * m + HD], op_[n % 2][:, 0:HD], rec[:, q:q + 1], None,
                                              ALU.mult).then_inc(s_ocopy, 1)
                        else:
                            dve.wait_ge(s_val, u * NTJ + n + 1)
                            dve.tensor_scalar(outs[i % 2][:, :], op_[n % 2][:, :], rden[:, i % 2, 0:1], None,
                                              ALU.mult).then_inc(s_ocopy, 1)

                    for i in range(AHEAD):
                        for step in scores_of(i):
                            copy_score(*step[1:])
                    if not fox:
                        combine(0)
                    for i in range(TB):
                        steps = order(i)
                        for x, (what, *step) in enumerate(steps):
                            if x == len(steps) // 2 and not fox and i + 1 < TB:
                                combine(i + 1)
                            if what == "score":
                                copy_score(*step)
                            elif what == "turn":
                                copy(*step)
                            elif step[2] == chunks(i) - 1:
                                output(i, step[1])

                units(dve, body)


def load_expert(eng, a, t, e, slot, free=lambda name: None):
    for name, at, rows, cols in (("w_gate", W_GATE, KT, F), ("w_up", W_UP, KT, F), ("w_down", W_DOWN, FT, D)):
        free(name)
        eng.dma_start(t.weights[:, slot, at:at + rows * cols].rearrange("p (k n) -> p k n", n=cols),
                      a[name][0, bass.ds(e, 1)].rearrange("a (p k) n -> p (a k) n", p=P)).then_inc(t.s_w[name][slot], 16)


def merge(nc, a, t):
    with ExitStack() as ctx:
        p = Names(nc, ctx, "mrg_")
        w_hi = p.sb("w_hi", [P, KT, D], F32R)
        w_lo = p.sb("w_lo", [P, KT, D], F32R)
        RAW = 3
        w_raw = [p.sb(f"w_raw{i}", [P, D]) for i in range(RAW)]
        w_rt = p.sb("w_router_sb", [P, KT, LOGITS])
        b_rt = p.sb("b_router_sb", [P, LOGITS])
        mx = p.sb("mx", [P, D])
        xx = p.sb("xx", [P, D])
        ssh = p.sb("ssh", [P, 4])
        stdh = p.sb("stdh", [P, 4])
        rh = p.sb("rh", [P, 4])
        mT_hi = [p.sb(f"mT_hi{i}", [P, KT, P], F32R) for i in range(2)]
        mT_lo = [p.sb(f"mT_lo{i}", [P, KT, P], F32R) for i in range(2)]
        o = p.sb("o", [P, D])
        h2 = p.sb("h2", [P, D])
        h2T = p.sb("h2T", [P, KT, P])
        squares = p.sb("squares", [P, D])
        sq = squares[:, 0:F]
        ss = p.sb("ss", [P, 2])
        sd = p.sb("sd", [P, 2])
        rr = p.sb("rr", [P, 2])
        mtp = [p.ps(f"mtp{i}", [P, BANK]) for i in range(2)]
        outp = [p.ps(f"outp{i}", [P, BANK]) for i in range(2)]
        htp = [p.ps(f"htp{i}", [P, BANK]) for i in range(2)]
        rtp = [p.ps(f"rtp{i}", [P, LOGITS]) for i in range(2)]
        names = ("hold rows_loaded router_loaded mixed_loaded x_loaded w_hi w_lo head_squares head_std head_reciprocal "
                 "heads_scaled mixed_turned mT_hi mT_lo projected_out out_copied out_squares out_std reciprocals x1_steps "
                 "x1_squares x1_std h2_steps h2_stored h2_turned h2T_copied router_product logits_done").split()
        s = {n: p.sem("m_" + n) for n in names}
        s_raw = [p.sem(f"m_w_out_loaded{i}") for i in range(RAW)]
        AHEAD = 2
        PEELED = 4
        LOOPED = (TB - PEELED - (AHEAD + 1)) // 2 * 2

        def blocks(eng, step):
            def peeled(i):
                step(i, i % 2, turn_next=i + AHEAD < TB, head_next=i + AHEAD + 1 < TB, router=min(i, 2))

            for i in range(PEELED):
                peeled(i)
            with eng.Fori(0, LOOPED // 2) as pair:
                for d in range(2):
                    step(pair * 2 + (PEELED + d), d, turn_next=True, head_next=True, router=2)
            for i in range(PEELED + LOOPED, TB):
                peeled(i)

        with nc.Block() as block:

            @block.gpsimd
            def _(pool):
                pool.dma_start(w_rt[:, :, 0:GROUPS], a["w_group"][0].rearrange("(k p) n -> p k n", p=P)).then_inc(s["router_loaded"], 16)
                pool.dma_start(w_rt[:, :, GROUPS:], a["w_router"][0].rearrange("(k p) n -> p k n", p=P)).then_inc(s["router_loaded"], 16)
                pool.dma_start(b_rt[:, 0:GROUPS], a["b_group"].to_broadcast([P, GROUPS])).then_inc(s["router_loaded"], 16)
                pool.dma_start(b_rt[:, GROUPS:], a["b_router"].to_broadcast([P, EXPERTS])).then_inc(s["router_loaded"], 16)
                heads = mx[:, 0:F].rearrange("p (h e) -> p h e", e=P)
                with pool.Fori(0, TB) as i:
                    pool.wait_ge(s["mixed_loaded"], 16 * (i + 1))
                    pool.wait_ge(s["head_reciprocal"], i + 1)
                    pool.sem_inc(s["hold"], 1)
                    pool.tensor_tensor(heads, heads, rh[:, :].unsqueeze(2).to_broadcast([P, 4, P]), ALU.mult).then_inc(s["heads_scaled"], 1)

            @block.sync
            def _(sp):
                def load_x(i):
                    sp.wait_ge(s["x1_steps"], 2 * i)
                    sp.dma_start(xx[:, :], a["x"][0, bass.ds(i * P, P), :]).then_inc(s["x_loaded"], 16)

                def load_mixed(i):
                    sp.wait_ge(s["mixed_turned"], 2 * i)
                    sp.dma_start(mx[:, :], t.mixed[bass.ds(i * P, P), :]).then_inc(s["mixed_loaded"], 16)

                sp.dma_start(mx[:, :], t.mixed[0:P, :]).then_inc(s["mixed_loaded"], 16)
                for k in range(KT):
                    if k >= RAW:
                        sp.wait_ge(s["w_lo"], k - RAW + 1)
                    sp.dma_start(w_raw[k % RAW][:, :], a["w_out"][0, k * P:(k + 1) * P, :]).then_inc(s_raw[k % RAW], 16)
                for i, name in enumerate(ROWS):
                    sp.dma_start(t.row[name][:, :], t.row_dram[i:i + 1, :].to_broadcast([P, D])).then_inc(s["rows_loaded"], 16)
                load_x(0)
                for i in range(1, AHEAD + 1):
                    load_mixed(i)
                with sp.Fori(0, TB - 1 - AHEAD) as i:
                    load_mixed(i + (AHEAD + 1))
                    load_x(i + 1)
                    sp.wait_ge(s["h2_steps"], 2 * i + 2)
                    sp.dma_start(t.h2[bass.ds(i * P, P), :], h2[:, :]).then_inc(s["h2_stored"], 16)
                for i in range(TB - 1 - AHEAD, TB):
                    if i + 1 < TB:
                        load_x(i + 1)
                    sp.wait_ge(s["h2_steps"], 2 * i + 2)
                    sp.dma_start(t.h2[i * P:(i + 1) * P, :], h2[:, :]).then_inc(s["h2_stored"], 16)
                sp.wait_ge(s["h2_stored"], 16 * TB)

            @block.tensor
            def _(pe):
                def turn(i):
                    pe.wait_ge(s["heads_scaled"], i + 1)
                    pe.wait_ge(s["mT_lo"], i * 2)
                    for h in range(2):
                        for j in range(TPB):
                            mm = pe.transpose(mtp[h][:, j * P:(j + 1) * P], mx[:, (h * TPB + j) * P:(h * TPB + j + 1) * P], t.ident)
                        mm.then_inc(s["mixed_turned"], 1)

                def project_out(i, b, halves):
                    pe.wait_ge(s["mT_lo"], i * 2 + 2)
                    for h in halves:
                        cols = slice(h * BANK, (h + 1) * BANK)
                        pe.wait_ge(s["out_copied"], 2 * i + h - (1 if h else 0))
                        for k in range(KT):
                            pe.wait_ge(s["w_lo"], k + 1)
                            pe.matmul(outp[h][:, :], mT_hi[b][:, k, :], w_hi[:, k, cols], start=(k == 0), stop=False)
                            pe.matmul(outp[h][:, :], mT_hi[b][:, k, :], w_lo[:, k, cols], start=False, stop=False)
                            mm = pe.matmul(outp[h][:, :], mT_lo[b][:, k, :], w_hi[:, k, cols], start=False, stop=(k == KT - 1))
                        mm.then_inc(s["projected_out"], 1)

                def turn_h2(i):
                    pe.wait_ge(s["h2_steps"], i * 2 + 2)
                    pe.wait_ge(s["h2T_copied"], i * 2)
                    for h in range(2):
                        for j in range(TPB):
                            mm = pe.transpose(htp[h][:, j * P:(j + 1) * P], h2[:, (h * TPB + j) * P:(h * TPB + j + 1) * P], t.ident)
                        mm.then_inc(s["h2_turned"], 1)

                def router_product(i, b, early=False):
                    pe.wait_ge(s["h2T_copied"], i * 2 + 2)
                    if not early:
                        pe.wait_ge(s["logits_done"], i - 1)
                    pe.wait_ge(s["router_loaded"], 64)
                    for k in range(KT):
                        mm = pe.matmul(rtp[b][:, :], h2T[:, k, :], w_rt[:, k, :], start=(k == 0), stop=(k == KT - 1))
                    mm.then_inc(s["router_product"], 1)

                def step(i, b, turn_next, head_next, router):
                    project_out(i, b, [0])
                    if router == 2:
                        router_product(i - 2, b, early=isinstance(i, int) and i < 4)
                    project_out(i, b, [1])
                    if turn_next:
                        turn(i + AHEAD)
                    if router:
                        turn_h2(i - 1)

                for i in range(AHEAD):
                    turn(i)
                blocks(pe, step)
                router_product(TB - 2, TB % 2)
                turn_h2(TB - 1)
                router_product(TB - 1, (TB - 1) % 2)

            @block.scalar
            def _(act):
                def head_std(i):
                    act.wait_ge(s["mixed_loaded"], 16 * (i + 1))
                    act.wait_ge(s["head_std"], i)
                    for h in range(4):
                        act.activation(sq[:, h * P:(h + 1) * P], mx[:, h * P:(h + 1) * P], ACT.Square,
                                       accum_out=ssh[:, h:h + 1]).then_inc(s["head_squares"], 1)
                    act.wait_ge(s["head_squares"], 4 * i + 4)
                    act.wait_ge(s["head_reciprocal"], i)
                    act.activation(stdh[:, :], ssh[:, :], ACT.Sqrt, scale=1.0 / P, bias=t.eps[:, :]).then_inc(s["head_std"], 1)

                def hi_parts(i, b):
                    act.wait_ge(s["mixed_turned"], 2 * i + 1)
                    act.activation(mT_hi[b][:, 0:TPB, :], mtp[0][:, :].rearrange("p (b n) -> p b n", n=P), ACT.Identity,
                                   scale=t.subln[:, :]).then_inc(s["mT_hi"], 1)
                    act.wait_ge(s["mixed_turned"], 2 * i + 2)
                    act.activation(mT_hi[b][:, TPB:, :], mtp[1][:, :].rearrange("p (b n) -> p b n", n=P), ACT.Copy).then_inc(s["mT_hi"], 1)

                def copy_h2(i):
                    for h in range(2):
                        act.wait_ge(s["h2_turned"], 2 * i + h + 1)
                        act.activation(h2T[:, h * TPB:(h + 1) * TPB, :], htp[h][:, :].rearrange("p (b n) -> p b n", n=P),
                                       ACT.Copy).then_inc(s["h2T_copied"], 1)

                def step(i, b, turn_next, head_next, router):
                    act.wait_ge(s["out_copied"], 2 * i + 2)
                    act.wait_ge(s["x1_squares"], i)
                    act.activation(squares[:, :], o[:, :], ACT.Square, accum_out=ss[:, 0:1]).then_inc(s["out_squares"], 1)
                    act.wait_ge(s["out_squares"], i + 1)
                    act.activation(sd[:, 0:1], ss[:, 0:1], ACT.Sqrt, scale=1.0 / D, bias=t.eps[:, :]).then_inc(s["out_std"], 1)
                    if turn_next:
                        hi_parts(i + AHEAD, b)
                    if router:
                        copy_h2(i - 1)
                    act.wait_ge(s["x1_steps"], 2 * i + 2)
                    act.activation(squares[:, :], t.x1[:, bass.ds(i, 1), :].rearrange("p a d -> p (a d)"), ACT.Square,
                                   accum_out=ss[:, 1:2]).then_inc(s["x1_squares"], 1)
                    act.wait_ge(s["x1_squares"], i + 1)
                    act.activation(sd[:, 1:2], ss[:, 1:2], ACT.Sqrt, scale=1.0 / D, bias=t.eps[:, :]).then_inc(s["x1_std"], 1)
                    if head_next:
                        head_std(i + AHEAD + 1)

                head_std(0)
                for k in range(KT):
                    act.wait_ge(s_raw[k % RAW], 16 * (k // RAW + 1))
                    act.activation(w_hi[:, k, :], w_raw[k % RAW][:, :], ACT.Copy).then_inc(s["w_hi"], 1)
                for i in range(AHEAD):
                    hi_parts(i, i)
                    head_std(i + 1)
                blocks(act, step)
                copy_h2(TB - 1)

            @block.vector
            def _(dve):
                def head_part(i):
                    dve.wait_ge(s["head_std"], i + 1)
                    dve.wait_ge(s["heads_scaled"], i)
                    dve.reciprocal(rh[:, :], stdh[:, :]).then_inc(s["head_reciprocal"], 1)

                def lo_parts(i, b):
                    dve.wait_ge(s["mT_hi"], 2 * i + 1)
                    dve.scalar_tensor_tensor(out=mT_lo[b][:, 0:TPB, :].rearrange("p b n -> p (b n)"), in0=mtp[0][:, :],
                                             scalar=t.subln[:, :], in1=mT_hi[b][:, 0:TPB, :].rearrange("p b n -> p (b n)").bitcast(F32),
                                             op0=ALU.mult, op1=ALU.subtract).then_inc(s["mT_lo"], 1)
                    dve.wait_ge(s["mT_hi"], 2 * i + 2)
                    dve.tensor_tensor(mT_lo[b][:, TPB:, :].rearrange("p b n -> p (b n)"), mtp[1][:, :],
                                      mT_hi[b][:, TPB:, :].rearrange("p b n -> p (b n)").bitcast(F32), ALU.subtract).then_inc(s["mT_lo"], 1)

                def step(i, b, turn_next, head_next, router):
                    x1 = t.x1[:, bass.ds(i, 1), :].rearrange("p a d -> p (a d)")
                    for h in range(2):
                        dve.wait_ge(s["x1_steps"], 2 * i)
                        dve.wait_ge(s["projected_out"], 2 * i + h + 1)
                        dve.tensor_copy(o[:, h * BANK:(h + 1) * BANK], outp[h][:, :]).then_inc(s["out_copied"], 1)
                    dve.wait_ge(s["out_std"], i + 1)
                    dve.reciprocal(rr[:, 0:1], sd[:, 0:1]).then_inc(s["reciprocals"], 1)
                    dve.wait_ge(s["reciprocals"], 2 * i + 1)
                    dve.scalar_tensor_tensor(out=x1, in0=o[:, :], scalar=rr[:, 0:1], in1=t.row["gate_attn"][:, :],
                                             op0=ALU.mult, op1=ALU.mult).then_inc(s["x1_steps"], 1)
                    dve.wait_ge(s["x1_steps"], 2 * i + 1)
                    dve.wait_ge(s["x_loaded"], 16 * (i + 1))
                    dve.tensor_tensor(x1, x1, xx[:, :], ALU.add).then_inc(s["x1_steps"], 1)
                    if turn_next:
                        lo_parts(i + AHEAD, b)
                    dve.wait_ge(s["x1_std"], i + 1)
                    dve.reciprocal(rr[:, 1:2], sd[:, 1:2]).then_inc(s["reciprocals"], 1)
                    dve.wait_ge(s["reciprocals"], 2 * i + 2)
                    dve.wait_ge(s["h2_stored"], 16 * i)
                    dve.wait_ge(s["h2_turned"], 2 * i)
                    dve.scalar_tensor_tensor(out=h2[:, :], in0=x1, scalar=rr[:, 1:2], in1=t.row["ffn_gain"][:, :],
                                             op0=ALU.mult, op1=ALU.mult).then_inc(s["h2_steps"], 1)
                    dve.wait_ge(s["h2_steps"], 2 * i + 1)
                    dve.tensor_tensor(h2[:, :], h2[:, :], t.row["ffn_shift"][:, :], ALU.add).then_inc(s["h2_steps"], 1)
                    if head_next:
                        head_part(i + AHEAD + 1)
                    if router == 2:
                        logits(i - 2, b)

                def logits(i, b):
                    dve.wait_ge(s["router_product"], i + 1)
                    dve.tensor_tensor(t.logits[:, bass.ds(i, 1), :].rearrange("p a n -> p (a n)"), rtp[b][:, :], b_rt[:, :],
                                      ALU.add).then_inc(s["logits_done"], 1)

                head_part(0)
                for k in range(KT):
                    dve.wait_ge(s["w_hi"], k + 1)
                    dve.tensor_tensor(w_lo[:, k, :], w_raw[k % RAW][:, :], w_hi[:, k, :].bitcast(F32), ALU.subtract).then_inc(s["w_lo"], 1)
                for i in range(AHEAD):
                    lo_parts(i, i)
                    head_part(i + 1)
                dve.wait_ge(s["rows_loaded"], 16 * len(ROWS))
                blocks(dve, step)
                logits(TB - 2, TB % 2)
                logits(TB - 1, (TB - 1) % 2)


def route(nc, a, t):
    with ExitStack() as ctx:
        p = Names(nc, ctx, "rt_")
        G, E8, E = GROUPS, PER_GROUP, EXPERTS
        def tile(name, *shape, dt=F32):
            return p.sb(name, [P, *shape], dt)
        gmax, gpick, gw, m1, m2, pick = (tile(n, TB) for n in ("gmax", "gpick", "gw", "m1", "m2", "pick"))
        geq, goh, gexp = (tile(n, TB, G) for n in ("geq", "goh", "gexp"))
        emask = tile("emask", TB, G, E8)
        esel, eeq, oh1, oh2, esel2 = (tile(n, TB, E8) for n in ("esel", "eeq", "oh1", "oh2", "esel2"))
        gap, egap, dsum = (tile(n, TB) for n in ("gap", "egap", "dsum"))
        E1, E2, off, rank = (row[:, h * TB * E:(h + 1) * TB * E].rearrange("p (t e) -> p t e", e=E)
                             for row in (t.row["gate_attn"], t.row["ffn_gain"]) for h in range(2))
        both = tile("both", TB, E, dt=BF16)
        prod = tile("prod", TB, E)
        cnt = tile("cnt", E)
        cnti, nbi = tile("cnti", E, dt=I32), tile("nbi", E, dt=I32)
        nb, ones = tile("nb", E), tile("ones_e", E)
        ended = tile("ended", TABLE, E, dt=BF16)
        owner = tile("owner", TABLE)
        owneri, half = tile("owneri", TABLE, dt=I32), tile("half", TABLE, dt=I32)
        cum = tile("cum", E + 1)
        dest = tile("dest", 2, TB)
        desti, pi, bi = (tile(n, 2, TB, dt=I32) for n in ("desti", "pi", "bi"))
        pf, bf = tile("pf", 2, TB), tile("bf", 2, TB)
        vals = tile("vals", 2, TB)
        tab, second, unused = (tile(n, TABLE) for n in ("tab", "second", "unused"))
        at_p = [tile(f"at_p{i}", P) for i in range(2)]
        at_b = [tile(f"at_b{i}", TABLE) for i in range(2)]
        prefix = p.ps("prefix", [P, TB * E])
        totals = p.ps("totals", [P, TB * E])
        table = p.ps("table", [P, TABLE])
        s_v, s_a, s_cnt, s_at, s_tab = (p.sem(n) for n in
                                        ("r_dve", "r_exp", "r_counted", "r_onehots", "r_table"))
        READY_G, READY_E, READY_B = [0], [0], [0]

        with nc.Block() as block:

            @block.sync
            def _(sp):
                for e in range(2):
                    load_expert(sp, a, t, e, e)

            @block.vector
            def _(dve):
                st = Steps(dve, s_v)
                L = st.link
                gl = t.logits[:, :, 0:G]
                el = t.logits[:, :, G:].rearrange("p t (g e) -> p t g e", g=G)
                gdesc = t.consts[:, C_GDESC:C_GDESC + G].unsqueeze(1).to_broadcast([P, TB, G])
                edesc = t.consts[:, C_EDESC:C_EDESC + E8].unsqueeze(1).to_broadcast([P, TB, E8])

                def wide(x, n):
                    return x[:, :].unsqueeze(2).to_broadcast([P, TB, n])

                def first_max(src, value, equal, chosen, desc, n):
                    L(dve.tensor_reduce(value[:, :], src, X, ALU.max))
                    L(dve.tensor_tensor(equal[:, :, :], src, wide(value, n), ALU.is_equal))
                    L(dve.tensor_tensor(equal[:, :, :], equal[:, :, :], desc, ALU.mult))
                    L(dve.tensor_reduce(pick[:, :], equal[:, :, :], X, ALU.max))
                    L(dve.tensor_tensor(chosen[:, :, :], equal[:, :, :], wide(pick, n), ALU.is_equal))

                first_max(gl, gmax, geq, goh, gdesc, G)
                L(dve.tensor_tensor(gexp[:, :, :], gl, wide(gmax, G), ALU.subtract))
                READY_G[0] = st.n
                for g in range(G):
                    L(dve.tensor_tensor(emask[:, :, g, :], el[:, :, g, :], goh[:, :, g:g + 1].to_broadcast([P, TB, E8]), ALU.mult))
                L(dve.tensor_reduce(esel[:, :, :], emask[:, :, :, :].rearrange("p t g e -> p t e g"), X, ALU.add))
                first_max(esel[:, :, :], m1, eeq, oh1, edesc, E8)
                L(dve.scalar_tensor_tensor(out=esel2[:, :, :], in0=oh1[:, :, :], scalar=-BIG, in1=esel[:, :, :], op0=ALU.mult, op1=ALU.add))
                first_max(esel2[:, :, :], m2, eeq, oh2, edesc, E8)
                L(dve.tensor_tensor(gap[:, :], m2[:, :], m1[:, :], ALU.subtract))
                READY_E[0] = st.n
                for g in range(G):
                    gb = goh[:, :, g:g + 1].to_broadcast([P, TB, E8])
                    L(dve.tensor_tensor(E1[:, :, g * E8:(g + 1) * E8], oh1[:, :, :], gb, ALU.mult))
                    L(dve.tensor_tensor(E2[:, :, g * E8:(g + 1) * E8], oh2[:, :, :], gb, ALU.mult))
                L(dve.tensor_tensor(both[:, :, :], E1[:, :, :], E2[:, :, :], ALU.add))
                READY_B[0] = st.n
                dve.wait_ge(s_a, 1)
                L(dve.tensor_reduce(gw[:, :], gexp[:, :, :], X, ALU.add))
                L(dve.reciprocal(gw[:, :], gw[:, :]))
                dve.wait_ge(s_a, 2)
                L(dve.tensor_scalar(dsum[:, :], egap[:, :], 1.0, None, ALU.add))
                L(dve.reciprocal(dsum[:, :], dsum[:, :]))
                L(dve.tensor_tensor(t.weight[:, 0, :], gw[:, :], dsum[:, :], ALU.mult))
                L(dve.tensor_tensor(t.weight[:, 1, :], t.weight[:, 0, :], egap[:, :], ALU.mult))
                dve.wait_ge(s_cnt, 2)
                tot = totals[:, :].rearrange("p (t e) -> p t e", e=E)
                L(dve.memset(off[:, 0, :], 0.0))
                for i in range(1, TB):
                    L(dve.tensor_tensor(off[:, i, :], off[:, i - 1, :], tot[:, i - 1, :], ALU.add))
                L(dve.tensor_tensor(cnt[:, :], off[:, TB - 1, :], tot[:, TB - 1, :], ALU.add))
                L(dve.tensor_tensor(rank[:, :, :], off[:, :, :], prefix[:, :].rearrange("p (t e) -> p t e", e=E), ALU.add))
                L(dve.tensor_scalar(cnti[:, :], cnt[:, :], float(P - 1), None, ALU.add))
                L(dve.tensor_scalar(nbi[:, :], cnti[:, :], P.bit_length() - 1, None, ALU.logical_shift_right))
                L(dve.tensor_scalar(nb[:, :], nbi[:, :], 1.0, None, ALU.max))
                L(dve.memset(ones[:, :], 1.0))
                L(dve.memset(cum[:, 0:1], 0.0))
                L(dve.tensor_tensor_scan(cum[:, 1:E + 1], ones[:, :], nb[:, :], 0.0, ALU.mult, ALU.add))
                L(dve.tensor_copy(t.cum_blocks[:, 0:E + 1], cum[:, :]))
                L(dve.tensor_scalar(t.cum_blocks[:, E + 1:E + 2], cum[:, E:E + 1], -1.0, None, ALU.add))
                L(dve.memset(t.cum_prev[:, 0:1], 0))
                L(dve.tensor_copy(t.cum_prev[:, 1:E], cum[:, 0:E - 1]))
                L(dve.tensor_tensor(ended[:, :, :], cum[:, 1:E + 1].unsqueeze(1).to_broadcast([P, TABLE, E]),
                                    t.consts[:, C_IOTA:C_IOTA + TABLE].unsqueeze(2).to_broadcast([P, TABLE, E]), ALU.is_le))
                L(dve.tensor_reduce(owner[:, :], ended[:, :, :], X, ALU.add))
                L(dve.tensor_copy(owneri[:, :], owner[:, :]))
                L(dve.tensor_scalar(t.slot[:, :], owneri[:, :], 1, None, ALU.bitwise_and))
                L(dve.tensor_scalar(half[:, :], owneri[:, :], 1, None, ALU.logical_shift_right))
                L(dve.tensor_scalar(t.loads[:, 0, :], half[:, :], 1.0, 16.0, ALU.add, ALU.mult))
                L(dve.tensor_scalar(owneri[:, :], owneri[:, :], 1.0, None, ALU.add))
                L(dve.tensor_scalar(half[:, :], owneri[:, :], 1, None, ALU.logical_shift_right))
                L(dve.tensor_scalar(t.loads[:, 1, :], half[:, :], 16.0, None, ALU.mult))
                L(dve.tensor_scalar(cum[:, :], cum[:, :], float(P), None, ALU.mult))
                L(dve.tensor_tensor(rank[:, :, :], rank[:, :, :], cum[:, 0:E].unsqueeze(1).to_broadcast([P, TB, E]), ALU.add))
                for n, oh in enumerate((E1, E2)):
                    L(dve.tensor_tensor(prod[:, :, :], oh[:, :, :], rank[:, :, :], ALU.mult))
                    L(dve.tensor_reduce(dest[:, n, :], prod[:, :, :], X, ALU.add))
                L(dve.tensor_copy(desti[:, :, :], dest[:, :, :]))
                L(dve.tensor_scalar(pi[:, :, :], desti[:, :, :], P - 1, None, ALU.bitwise_and))
                L(dve.tensor_scalar(bi[:, :, :], desti[:, :, :], P.bit_length() - 1, None, ALU.logical_shift_right))
                L(dve.tensor_copy(pf[:, :, :], pi[:, :, :]))
                L(dve.tensor_copy(bf[:, :, :], bi[:, :, :]))
                L(dve.tensor_scalar(vals[:, 0, :], t.consts[:, C_TOKEN:C_TOKEN + TB], 1.0, None, ALU.add))
                L(dve.tensor_scalar(vals[:, 1, :], t.consts[:, C_TOKEN:C_TOKEN + TB], 1.0 + S, None, ALU.add))
                for q in range(2 * TB):
                    n, i = divmod(q, TB)
                    if q >= 2:
                        dve.wait_ge(s_tab, q - 1)
                    dve.tensor_scalar(at_p[q % 2][:, :], t.consts[:, C_IOTA:C_IOTA + P], pf[:, n, i:i + 1], None,
                                      ALU.is_equal).then_inc(s_at, 1)
                    dve.tensor_scalar(at_b[q % 2][:, :], t.consts[:, C_IOTA:C_IOTA + TABLE], bf[:, n, i:i + 1],
                                      vals[:, n, i:i + 1], ALU.is_equal, ALU.mult).then_inc(s_at, 1)
                dve.wait_ge(s_tab, 2 * TB)
                L(dve.tensor_copy(tab[:, :], table[:, :]))
                L(dve.tensor_scalar(second[:, :], tab[:, :], S + 0.5, float(-S), ALU.is_gt, ALU.mult))
                L(dve.scalar_tensor_tensor(out=second[:, :], in0=tab[:, :], scalar=-1.0, in1=second[:, :], op0=ALU.add, op1=ALU.add))
                L(dve.tensor_scalar(t.ids[:, :], second[:, :], 0.0, None, ALU.max))
                L(dve.tensor_scalar(unused[:, :], tab[:, :], 0.5, None, ALU.is_lt))
                L(dve.tensor_scalar(unused[:, :], unused[:, :], t.consts[:, C_TRASH:C_TRASH + 1], None, ALU.mult))
                L(dve.scalar_tensor_tensor(out=t.rows[:, :], in0=tab[:, :], scalar=-1.0, in1=unused[:, :], op0=ALU.add, op1=ALU.add))

            @block.scalar
            def _(act):
                act.wait_ge(s_v, READY_G[0])
                act.activation(gexp[:, :, :], gexp[:, :, :], ACT.Exp).then_inc(s_a, 1)
                act.wait_ge(s_v, READY_E[0])
                act.activation(egap[:, :], gap[:, :], ACT.Exp).then_inc(s_a, 1)

            @block.tensor
            def _(pe):
                pe.wait_ge(s_v, READY_B[0])
                flat = both[:, :, :].rearrange("p t e -> p (t e)")
                pe.matmul(prefix[:, :], t.before_bf[:, :], flat, start=True, stop=True).then_inc(s_cnt, 1)
                pe.matmul(totals[:, :], t.ones_bf[:, :], flat, start=True, stop=True).then_inc(s_cnt, 1)
                for q in range(2 * TB):
                    pe.wait_ge(s_at, 2 * q + 2)
                    pe.matmul(table[:, :], at_p[q % 2][:, :], at_b[q % 2][:, :], start=(q == 0), stop=(q == 2 * TB - 1)).then_inc(s_tab, 1)


def experts(nc, a, t):
    with ExitStack() as ctx:
        p = Names(nc, ctx, "ex_")
        ids = p.sb("ids_now", [P, 1], U32)
        rows = p.sb("rows_now", [P, 1], U32)
        xg = p.sb("xg", [P, D])
        xT = p.sb("xT", [P, KT, P])
        gate = p.sb("gate", [P, F])
        hid = p.sb("hid", [P, F])
        hidT = p.sb("hidT", [P, FT, P])
        y = p.sb("y", [P, D])
        xtp = [p.ps(f"ext{i}", [P, BANK]) for i in range(2)]
        gp = p.ps("gp", [P, F])
        up = p.ps("up", [P, F])
        hp = p.ps("hp", [P, F])
        yp = [p.ps(f"yp{i}", [P, BANK]) for i in range(2)]
        names = ("hold ids_ready rows_ready gathered x_turned x_copied gate_product up_product gate_activated hidden hidden_turned "
                 "hidden_copied down_product y_copied_a y_copied_v y_stored").split()
        s = {n: p.sem("e_" + n) for n in names}
        reader = {"w_gate": "gate_product", "w_up": "up_product", "w_down": "down_product"}

        def total_blocks(eng):
            return eng.value_load(t.cum_blocks[0:1, EXPERTS:EXPERTS + 1], min_val=EXPERTS, max_val=MAX_BLOCKS)

        def last_block(eng):
            return eng.value_load(t.cum_blocks[0:1, EXPERTS + 1:EXPERTS + 2], min_val=0, max_val=MAX_BLOCKS)

        with nc.Block() as block:

            @block.sync
            def _(sp):
                with sp.Fori(1, EXPERTS // 2) as pair:
                    for b in range(2):
                        e = pair * 2 + b
                        prev = sp.value_load(t.cum_prev[0:1, bass.ds(e, 1)], min_val=0, max_val=MAX_BLOCKS)
                        load_expert(sp, a, t, e, b, lambda name: sp.wait_ge(s[reader[name]], prev))

            @block.gpsimd
            def _(pool):
                def fetch(g):
                    pool.wait_ge(s["x_turned"], 2 * g)
                    pool.tensor_copy(ids[:, :], t.ids[:, bass.ds(g, 1)]).then_inc(s["ids_ready"], 1)
                    pool.wait_ge(s["ids_ready"], g + 1)
                    pool.sem_inc(s["hold"], 1)
                    pool.indirect_dma_start(out=xg[:, :], out_offset=None, in_=t.h2,
                                            in_offset=bass.IndirectOffsetOnAxis(ap=ids[:, 0:1], axis=0)).then_inc(s["gathered"], 16)

                fetch(0)
                fetch(1)
                total = total_blocks(pool)
                with pool.Fori(0, total) as g:
                    fetch(g + 2)
                    pool.wait_ge(s["y_stored"], 16 * g)
                    pool.tensor_copy(rows[:, :], t.rows[:, bass.ds(g, 1)]).then_inc(s["rows_ready"], 1)
                    pool.wait_ge(s["rows_ready"], g + 1)
                    pool.wait_ge(s["y_copied_a"], g + 1)
                    pool.wait_ge(s["y_copied_v"], g + 1)
                    pool.sem_inc(s["hold"], 1)
                    pool.indirect_dma_start(out=t.y, out_offset=bass.IndirectOffsetOnAxis(ap=rows[:, 0:1], axis=0),
                                            in_=y[:, :], in_offset=None).then_inc(s["y_stored"], 16)
                pool.wait_ge(s["gathered"], total * 16 + 32)
                pool.wait_ge(s["y_stored"], total * 16)
                pool.sem_inc(s["hold"], 1)
                pool.tensor_copy(ids[:, :], t.ids[:, 0:1]).then_inc(s["ids_ready"], 1)

            @block.tensor
            def _(pe):
                def slot_of(g):
                    return pe.value_load(t.slot[0:1, bass.ds(g, 1)], min_val=0, max_val=1)

                def weight(slot, at, cols, k, lo, n):
                    return t.weights[:, bass.ds(slot, 1), at + k * cols + lo:at + k * cols + lo + n].rearrange("p a n -> p (a n)")

                def turn(g):
                    pe.wait_ge(s["gathered"], 16 * g + 16)
                    pe.wait_ge(s["x_copied"], 2 * g)
                    for h in range(2):
                        for j in range(TPB):
                            mm = pe.transpose(xtp[h][:, j * P:(j + 1) * P], xg[:, h * TPB + j::KT], t.ident)
                        mm.then_inc(s["x_turned"], 1)

                def loads_for(g):
                    return [pe.value_load(t.loads[0:1, b, bass.ds(g, 1)], min_val=0, max_val=16 * (EXPERTS // 2 + 1))
                            for b in range(2)]

                def loaded(name, loads):
                    for b in range(2):
                        pe.wait_ge(t.s_w[name][b], loads[b])

                def gate_product(g, slot, loads):
                    loaded("w_gate", loads)
                    pe.wait_ge(s["x_copied"], 2 * g + 2)
                    pe.wait_ge(s["gate_activated"], g)
                    for k in range(KT):
                        mm = pe.matmul(gp[:, :], xT[:, k, :], weight(slot, W_GATE, F, k, 0, F), start=(k == 0), stop=(k == KT - 1))
                    mm.then_inc(s["gate_product"], 1)

                def up_product(g, slot, loads):
                    loaded("w_up", loads)
                    pe.wait_ge(s["hidden"], g)
                    for k in range(KT):
                        mm = pe.matmul(up[:, :], xT[:, k, :], weight(slot, W_UP, F, k, 0, F), start=(k == 0), stop=(k == KT - 1))
                    mm.then_inc(s["up_product"], 1)

                def turn_hidden(g):
                    pe.wait_ge(s["hidden"], g + 1)
                    pe.wait_ge(s["hidden_copied"], g)
                    for k in range(FT):
                        mm = pe.transpose(hp[:, k * P:(k + 1) * P], hid[:, k::FT], t.ident)
                    mm.then_inc(s["hidden_turned"], 1)

                def down_product(g, slot, loads):
                    loaded("w_down", loads)
                    pe.wait_ge(s["hidden_copied"], g + 1)
                    pe.wait_ge(s["y_copied_a"], g)
                    pe.wait_ge(s["y_copied_v"], g)
                    for h in range(2):
                        for k in range(FT):
                            mm = pe.matmul(yp[h][:, :], hidT[:, k, :], weight(slot, W_DOWN, D, k, h * BANK, BANK),
                                           start=(k == 0), stop=(k == FT - 1))
                    mm.then_inc(s["down_product"], 1)

                turn(0)
                first = slot_of(0)
                loads = loads_for(0)
                gate_product(0, first, loads)
                up_product(0, first, loads)
                turn(1)
                total = total_blocks(pe)
                with pe.Fori(1, total) as g:
                    slot = slot_of(g)
                    last = slot_of(g - 1)
                    loads = loads_for(g)
                    last_loads = loads_for(g - 1)
                    gate_product(g, slot, loads)
                    turn_hidden(g - 1)
                    up_product(g, slot, loads)
                    turn(g + 1)
                    down_product(g - 1, last, last_loads)
                end = last_block(pe)
                last = slot_of(end)
                last_loads = loads_for(end)
                turn_hidden(end)
                down_product(end, last, last_loads)

            @block.scalar
            def _(act):
                def copy_x(g):
                    for h in range(2):
                        act.wait_ge(s["x_turned"], 2 * g + h + 1)
                        act.wait_ge(s["up_product"], g)
                        act.activation(xT[:, h * TPB:(h + 1) * TPB, :], xtp[h][:, :].rearrange("p (b n) -> p b n", n=P),
                                       ACT.Copy).then_inc(s["x_copied"], 1)

                def activate(g):
                    act.wait_ge(s["gate_product"], g + 1)
                    act.wait_ge(s["hidden"], g)
                    act.activation(gate[:, :], gp[:, :], ACT.Silu).then_inc(s["gate_activated"], 1)

                def copy_y(g):
                    act.wait_ge(s["down_product"], g + 1)
                    act.wait_ge(s["y_stored"], 16 * g)
                    act.activation(y[:, 0:BANK], yp[0][:, :], ACT.Copy).then_inc(s["y_copied_a"], 1)

                copy_x(0)
                activate(0)
                copy_x(1)
                total = total_blocks(act)
                with act.Fori(1, total) as g:
                    activate(g)
                    copy_x(g + 1)
                    copy_y(g - 1)
                copy_y(last_block(act))

            @block.vector
            def _(dve):
                def multiply(g):
                    dve.wait_ge(s["gate_activated"], g + 1)
                    dve.wait_ge(s["up_product"], g + 1)
                    dve.wait_ge(s["hidden_turned"], g)
                    dve.tensor_tensor(hid[:, :], gate[:, :], up[:, :], ALU.mult).then_inc(s["hidden"], 1)

                def copy_hidden(g):
                    dve.wait_ge(s["hidden_turned"], g + 1)
                    dve.wait_ge(s["down_product"], g)
                    dve.tensor_copy(hidT[:, :, :], hp[:, :].rearrange("p (b n) -> p b n", n=P)).then_inc(s["hidden_copied"], 1)

                def copy_y(g):
                    dve.wait_ge(s["down_product"], g + 1)
                    dve.wait_ge(s["y_stored"], 16 * g)
                    dve.tensor_copy(y[:, BANK:], yp[1][:, :]).then_inc(s["y_copied_v"], 1)

                multiply(0)
                total = total_blocks(dve)
                with dve.Fori(1, total) as g:
                    copy_hidden(g - 1)
                    multiply(g)
                    copy_y(g - 1)
                end = last_block(dve)
                copy_hidden(end)
                copy_y(end)


def combine(nc, a, t, out):
    with ExitStack() as ctx:
        p = Names(nc, ctx, "cb_")
        NB = 4
        y1 = [p.sb(f"y1_{i}", [P, D]) for i in range(NB)]
        y2 = [p.sb(f"y2_{i}", [P, D]) for i in range(NB)]
        res = [p.sb(f"res{i}", [P, D]) for i in range(NB)]
        squares = p.sb("squares", [P, D])
        ss, sd, rr = (p.sb(n, [P, TB]) for n in ("ss3", "sd3", "rr3"))
        s_rows = [p.sem(f"c_rows{i}") for i in range(NB)]
        s_first, s_sum, s_sq, s_std, s_rec, s_scaled, s_out = (p.sem(n) for n in (
            "c_first_weighted", "c_summed", "c_squared", "c_std", "c_reciprocal", "c_scaled", "c_result"))
        s_store = [p.sem(f"c_stored{i}") for i in range(NB)]
        with nc.Block() as block:

            @block.gpsimd
            def _(pool):
                for i in range(TB):
                    b = i % NB
                    if i >= NB:
                        pool.wait_ge(s_sum, i - NB + 1)
                    pool.dma_start(y1[b][:, :], t.y[i * P:(i + 1) * P, :]).then_inc(s_rows[b], 16)
                    pool.dma_start(y2[b][:, :], t.y[S + i * P:S + (i + 1) * P, :]).then_inc(s_rows[b], 16)

            @block.scalar
            def _(act):
                for i in range(TB):
                    b = i % NB
                    act.wait_ge(s_rows[b], 32 * (i // NB + 1))
                    act.activation(y1[b][:, :], y1[b][:, :], ACT.Copy, scale=t.weight[:, 0, i:i + 1]).then_inc(s_first, 1)
                    act.wait_ge(s_sum, i + 1)
                    if i:
                        act.wait_ge(s_sq, i)
                    act.activation(squares[:, :], res[b][:, :], ACT.Square, accum_out=ss[:, i:i + 1]).then_inc(s_sq, 1)
                    act.wait_ge(s_sq, i + 1)
                    act.activation(sd[:, i:i + 1], ss[:, i:i + 1], ACT.Sqrt, scale=1.0 / D, bias=t.eps[:, :]).then_inc(s_std, 1)

            @block.vector
            def _(dve):
                for i in range(TB):
                    b = i % NB
                    dve.wait_ge(s_first, i + 1)
                    dve.wait_ge(s_rows[b], 32 * (i // NB + 1))
                    if i >= NB:
                        dve.wait_ge(s_store[b], 16 * (i // NB))
                    dve.scalar_tensor_tensor(out=res[b][:, :], in0=y2[b][:, :], scalar=t.weight[:, 1, i:i + 1], in1=y1[b][:, :],
                                             op0=ALU.mult, op1=ALU.add).then_inc(s_sum, 1)
                    dve.wait_ge(s_std, i + 1)
                    dve.reciprocal(rr[:, i:i + 1], sd[:, i:i + 1]).then_inc(s_rec, 1)
                    dve.wait_ge(s_rec, i + 1)
                    dve.scalar_tensor_tensor(out=res[b][:, :], in0=res[b][:, :], scalar=rr[:, i:i + 1], in1=t.row["gate_ffn"][:, :],
                                             op0=ALU.mult, op1=ALU.mult).then_inc(s_scaled, 1)
                    dve.wait_ge(s_scaled, i + 1)
                    dve.tensor_tensor(res[b][:, :], res[b][:, :], t.x1[:, i, :], ALU.add).then_inc(s_out, 1)

            @block.sync
            def _(sp):
                for i in range(TB):
                    sp.wait_ge(s_out, i + 1)
                    sp.dma_start(out[0, i * P:(i + 1) * P, :], res[i % NB][:, :]).then_inc(s_store[i % NB], 16)
                for b in range(NB):
                    sp.wait_ge(s_store[b], 16 * (TB // NB))


def kernel_program(nc, a, out):
    with ExitStack() as ctx:
        p = Names(nc, ctx)

        class T:
            pass
        t = T()
        t.consts = p.sb("consts_sb", [P, C_END])
        t.ident = t.consts[:, C_IDENT:C_IDENT + P]
        t.rot = t.consts[:, C_ROT:C_ROT + P]
        t.ident_bf = p.sb("ident_bf", [P, P], BF16)
        t.before_bf = p.sb("before_bf", [P, P], BF16)
        t.ones_bf = p.sb("ones_bf", [P, P], BF16)
        t.mask = {k: p.sb(f"mask_{k}", [P, P], BF16) for k in ("diff", "fox")}
        t.eps = p.sb("eps", [P, 1])
        t.subln = p.sb("subln", [P, 1])
        t.bforget = p.sb("bforget", [FOX_HEADS, 1])
        t.neg_lambda = p.sb("neg_lambda", [P, 1])
        t.attn_gain = p.sb("attn_gain", [P, KT])
        t.attn_shift = p.sb("attn_shift", [P, KT])
        t.mixed = nc.dram_tensor("mixed_d", (S, D), F32, kind="Internal").ap()
        t.neg_f = nc.dram_tensor("neg_f_d", (FOX_HEADS, S), F32, kind="Internal").ap()
        t.row_dram = nc.dram_tensor("mod_rows_d", (len(ROWS), D), F32, kind="Internal").ap()
        t.h2 = nc.dram_tensor("h2_d", (S, D), F32, kind="Internal").ap()
        t.y = nc.dram_tensor("y_d", (2 * S + P, D), F32, kind="Internal").ap()
        t.hi, t.lo = ([nc.dram_tensor(f"{'qk'[part]}_{n}_d", (2 * UNITS * P, S), F32, kind="Internal").ap()
                       for part in range(2)] for n in ("hi", "lo"))
        t.v = nc.dram_tensor("v_d", (2 * UNITS * P, TB * P), F32, kind="Internal").ap()
        with ExitStack() as inner:
            with ExitStack() as first:
                t.hT = first.enter_context(nc.sbuf_tensor("hT", [P, KT, S], F32, side="right"))
                modulate(nc, a, t)
                h = Names(nc, inner)
                t.h_hi, t.h_lo = (h.sb(n, [P, KT, S], F32R) for n in ("h_hi", "h_lo"))
                split(nc, a, t)
            project(nc, a, t)
        with ExitStack() as inner:
            h = Names(nc, inner, "unit_")
            t.q_hi, t.q_lo, t.k_both = ([[h.sb(f"{n}{b}{m}", [P, S], F32R) for m in range(2)] for b in range(2)]
                                        for n in ("q_hi", "q_lo", "k_both"))
            t.v_in = [h.sb(f"v{b}", [P, S]) for b in range(2)]
            t.negf = [h.sb(f"negf{m}", [P, S]) for m in range(2)]
            t.s_in = [[h.sem(f"slot{b}_part{part}_loaded") for part in range(2)] for b in range(2)]
            t.s_negf = h.sem("neg_f_loaded")
            attend(nc, a, t, "diff")
            attend(nc, a, t, "fox")
        t.logits = p.sb("logits", [P, TB, LOGITS])
        t.weight = p.sb("weight", [P, 2, TB])
        t.cum_blocks = p.sb("cum_blocks", [P, EXPERTS + 2], I32)
        t.cum_prev = p.sb("cum_prev", [P, EXPERTS], I32)
        t.slot = p.sb("slot", [P, TABLE], I32)
        t.loads = p.sb("loads", [P, 2, TABLE], I32)
        t.ids = p.sb("ids", [P, TABLE], U32)
        t.rows = p.sb("rows", [P, TABLE], U32)
        t.x1 = p.sb("x1", [P, TB, D])
        t.row = {name: p.sb(name, [P, D]) for name in ROWS}
        merge(nc, a, t)
        with ExitStack() as inner:
            q = Names(nc, inner, "ex_")
            t.weights = q.sb("weights", [P, 2, EXPERT_WORDS])
            t.s_w = {n: [q.sem(f"{n}_loaded{i}") for i in range(2)] for n in ("w_gate", "w_up", "w_down")}
            route(nc, a, t)
            experts(nc, a, t)
        combine(nc, a, t, out)


_INS = ["x", "c", "w_ada", "b_ada", "g_pre_attn", "g_post_attn", "w_in", "b_forget", "lambda_q1", "lambda_k1",
        "lambda_q2", "lambda_k2", "g_diff_subln", "w_out", "g_pre_ffn", "g_post_ffn", "w_group", "b_group",
        "w_router", "b_router", "w_gate", "w_up", "w_down"]


def _constants():
    import numpy as np
    inv = (1.0 / (10000.0 ** (np.arange(0, HD, 2, dtype=np.float32) / np.float32(HD)))).astype(np.float32)
    ang = (np.arange(S, dtype=np.float32)[:, None] * inv[None, :]).astype(np.float32)
    reps = (P // (HD // 2), 1)
    cos = np.ascontiguousarray(np.tile(np.cos(ang).astype(np.float32).T, reps))
    sin = np.ascontiguousarray(np.tile(np.sin(ang).astype(np.float32).T, reps))
    k = np.zeros((P, C_END), np.float32)
    at = np.arange(P)
    k[:, C_IDENT:C_IDENT + P] = np.eye(P)
    for m in range(P):
        first = m % HD < HD // 2
        k[m + HD // 2 if first else m - HD // 2, C_ROT + m] = -1.0 if first else 1.0
    k[:, C_BEFORE:C_BEFORE + P] = at[:, None] < at[None, :]
    k[:, C_MASKD:C_MASKD + P] = -1e30 * (at[None, :] // 64 > at[:, None] // 64)
    k[:, C_MASKF:C_MASKF + P] = -1e30 * (at[None, :] > at[:, None])
    k[:, C_IOTA:C_IOTA + P] = at[None, :]
    k[:, C_GDESC:C_GDESC + GROUPS] = np.arange(GROUPS, 0, -1)
    k[:, C_EDESC:C_EDESC + PER_GROUP] = np.arange(PER_GROUP, 0, -1)
    k[:, C_TOKEN:C_TOKEN + TB] = np.arange(TB)[None, :] * P + at[:, None]
    k[:, C_TRASH] = 2 * S + 1 + at
    return {"consts": k, "zeros": np.zeros((P, P - FOX_HEADS), np.float32), "rope_cos": cos, "rope_sin": sin}


def kernel(**inputs):
    import numpy as np
    import concourse.bacc as bacc
    from concourse.bass_utils import run_bass_kernel_spmd

    nc = bacc.Bacc("TRN2", target_bir_lowering=False, num_devices=1)
    arrays, args = {}, {}
    for name, x in {**{n: inputs[n] for n in _INS}, **_constants()}.items():
        x = np.ascontiguousarray(x)
        arrays[f"in_{name}"] = x
        args[name] = nc.dram_tensor(f"in_{name}", x.shape, mybir.dt.from_np(x.dtype), kind="ExternalInput").ap()
    out = nc.dram_tensor("out_0", (1, S, D), F32, kind="ExternalOutput").ap()
    kernel_program(nc, args, out)
    r = run_bass_kernel_spmd(nc, [arrays], core_ids=[0])
    return r.results[0]["out_0"]
```
